# Optimizing a Trainium2 kernel written in Bass

```python
import math
import jax, jax.numpy as jnp
from jax import lax
import numpy as np

D_MODEL = 1024
BATCH = 1
SEQ = 1024
DEPTH = 2
DEC_BATCH = 1
DEC_SEQ = 32
PAST_LEN = 2048

CHUNK = 64
EPS = 1e-6
DH = 64
H_A = D_MODEL // (2 * DH)
A_W = H_A * DH
H_I = 8
D_I = 64
K_TOP = 256
QBLK = 64
N_BUCKETS = 32
T5_MAX_DIST = 1024
DK_B = 128
DV_B = 128
H_B = D_MODEL // (2 * DV_B)
B_KW = H_B * DK_B
B_VW = H_B * DV_B
H_C = D_MODEL // DH
C_W = H_C * DH
C_BACK = 8
C_WIN = C_BACK * CHUNK
REL_CLIP = 128
D_FF = ((-(-8 * D_MODEL // 3) + 255) // 256) * 256
N_EVEN = (DEPTH + 1) // 2
N_ODD = DEPTH // 2
EVEN_SIZES = (A_W, A_W, A_W, H_I * D_I, D_I, H_I, B_KW, B_KW, B_VW, B_VW)
EVEN_IN = sum(EVEN_SIZES)

kernel_name = "hybrid_streaming_dsa_hgrn2_chunkband"

F32 = jnp.float32

def _split(z, sizes):
    out, off = [], 0
    for s in sizes:
        out.append(z[..., off:off + s])
        off += s
    return out

def _rmsnorm(x, g):
    xf = x.astype(F32)
    y = xf * lax.rsqrt(jnp.mean(xf * xf, axis=-1, keepdims=True) + EPS)
    return (y * g.astype(F32)).astype(x.dtype)

def _adaln(c, w_ada, b_ada):
    mod = jnp.einsum('bd,de->be', jax.nn.silu(c), w_ada) + b_ada
    return jnp.split(mod, 6, axis=-1)

def _modulate(x, g, shift, scale):
    return _rmsnorm(x, g) * (1 + scale[:, None]) + shift[:, None]

def _swiglu(h, wg, wu, wd):
    a = jnp.einsum('btd,df->btf', h, wg)
    b = jnp.einsum('btd,df->btf', h, wu)
    return jnp.einsum('btf,fd->btd', jax.nn.silu(a) * b, wd)

def _t5_bucket(rel):
    nb = N_BUCKETS // 2
    max_exact = nb // 2
    base = jnp.where(rel > 0, nb, 0)
    n = jnp.abs(rel)
    large = max_exact + (jnp.log(jnp.maximum(n, 1).astype(F32) / max_exact)
                         / math.log(T5_MAX_DIST / max_exact) * (nb - max_exact)).astype(jnp.int32)
    large = jnp.minimum(large, nb - 1)
    return base + jnp.where(n < max_exact, n, large)

def _dsa_attend(q, qi, wi, k, v, ki, q_pos, k_pos, t5_table, k_sel):
    B, T = q.shape[:2]
    blk = min(QBLK, T)
    nb = T // blk

    def blocks(a):
        return jnp.moveaxis(a.reshape(B, nb, blk, *a.shape[2:]), 1, 0)

    k_chunk = k_pos // CHUNK

    def one_block(xs):
        qb, qib, wb, pb = xs
        s = jnp.einsum('bthd,bsd->bths', qib, ki).astype(F32) * (D_I ** -0.5)
        score = jnp.einsum('bth,bths->bts', wb.astype(F32) * (H_I ** -0.5), jax.nn.relu(s))
        q_chunk = pb // CHUNK
        adm = k_chunk[None, :] <= q_chunk[:, None]
        score = jnp.where(adm[None], score, -jnp.inf)
        _, idx = lax.top_k(score, k_sel)
        ks = jax.vmap(lambda kk, ii: kk[ii])(k, idx)
        vs = jax.vmap(lambda vv, ii: vv[ii])(v, idx)
        sel_pos = k_pos[idx]
        valid = (sel_pos // CHUNK) <= q_chunk[None, :, None]
        bias = t5_table[_t5_bucket(sel_pos - pb[None, :, None])]
        logits = (jnp.einsum('bthd,btkhd->bhtk', qb, ks).astype(F32) * (DH ** -0.5)
                  + jnp.moveaxis(bias, -1, 1).astype(F32))
        logits = jnp.where(valid[:, None], logits, -jnp.inf)
        p = jax.nn.softmax(logits, axis=-1)
        return jnp.einsum('bhtk,btkhd->bthd', p.astype(vs.dtype), vs)

    out = lax.map(one_block, (blocks(q), blocks(qi), blocks(wi), q_pos.reshape(nb, blk)))
    return jnp.moveaxis(out, 0, 1).reshape(B, T, H_A, DH)

def _hgrn2_chunk(S0, xs):
    q, k, v, g = xs
    T = q.shape[1]
    G = jnp.cumsum(g, axis=1)
    causal = jnp.tril(jnp.ones((T, T), dtype=bool))[None, :, :, None, None]
    decay = jnp.exp(jnp.where(causal, G[:, :, None] - G[:, None, :], -jnp.inf))
    att = jnp.einsum('bthk,btshk,bshk->bhts', q, decay, k)
    o = (jnp.einsum('bhts,bshv->bthv', att, v)
         + jnp.einsum('bthk,bhkv->bthv', q * jnp.exp(G), S0))
    G_end = G[:, -1]
    S = (jnp.exp(G_end)[..., None] * S0
         + jnp.einsum('bshk,bshv->bhkv', k * jnp.exp(G_end[:, None] - G), v))
    return S, o

def _hgrn2_scan(S0, q, k, v, g):
    B, T = q.shape[:2]
    blk = min(CHUNK, T)
    n = T // blk

    def to_chunks(a):
        return jnp.moveaxis(a.reshape(B, n, blk, *a.shape[2:]), 1, 0)

    S, o = lax.scan(_hgrn2_chunk, S0, (to_chunks(q), to_chunks(k), to_chunks(v), to_chunks(g)))
    return S, jnp.moveaxis(o, 0, 1).reshape(B, T, H_B, DV_B)

def _even_mixer(h, k_past, v_past, ki_past, S0, q_pos, k_pos, k_sel,
                w_in, w_out, t5_table, lb, g_norm):
    B, T = h.shape[:2]
    z = jnp.einsum('btd,de->bte', h, w_in)
    qa, ka, va, qi, ki, wi, qb, fb, ib, gb = _split(z, EVEN_SIZES)
    qa = qa.reshape(B, T, H_A, DH)
    ka = ka.reshape(B, T, H_A, DH)
    va = va.reshape(B, T, H_A, DH)
    qi = qi.reshape(B, T, H_I, D_I)
    if k_past is None:
        k_all, v_all, ki_all = ka, va, ki
    else:
        k_all = jnp.concatenate([k_past.astype(ka.dtype), ka], axis=1)
        v_all = jnp.concatenate([v_past.astype(va.dtype), va], axis=1)
        ki_all = jnp.concatenate([ki_past.astype(ki.dtype), ki], axis=1)
    oa = _dsa_attend(qa, qi, wi, k_all, v_all, ki_all, q_pos, k_pos, t5_table, k_sel)
    qh = jax.nn.silu(qb.astype(F32)).reshape(B, T, H_B, DK_B)
    f = lb + (1.0 - lb) * jax.nn.sigmoid(fb.astype(F32))
    kh = (1.0 - f).reshape(B, T, H_B, DK_B)
    gh = jnp.log(f).reshape(B, T, H_B, DK_B)
    vh = ib.astype(F32).reshape(B, T, H_B, DV_B)
    S, ob = _hgrn2_scan(S0.astype(F32), qh, kh, vh, gh)
    ob = ob * lax.rsqrt(jnp.mean(ob * ob, axis=-1, keepdims=True) + EPS)
    ob = ob.reshape(B, T, B_VW) * g_norm.astype(F32) * jax.nn.silu(gb.astype(F32))
    mix = jnp.concatenate([oa.reshape(B, T, A_W), ob.astype(oa.dtype)], axis=-1)
    return jnp.einsum('bte,ed->btd', mix, w_out), ka, va, ki, S

def _band_attend(q, k, v, q_pos, k_pos, rel_table):
    rel = jnp.clip(q_pos[:, None] - k_pos[None, :], -REL_CLIP, REL_CLIP) + REL_CLIP
    bias = jnp.moveaxis(rel_table[rel], -1, 0).astype(F32)
    logits = jnp.einsum('bthd,bshd->bhts', q, k).astype(F32) * (DH ** -0.5) + bias[None]
    logits = jnp.where((k_pos >= 0)[None, None, None, :], logits, -jnp.inf)
    p = jax.nn.softmax(logits, axis=-1)
    return jnp.einsum('bhts,bshd->bthd', p.astype(v.dtype), v)

def _chunk_band_prompt(q, k, v, rel_table):
    B, T = q.shape[:2]
    n = T // CHUNK
    pad = ((0, 0), (C_WIN, 0), (0, 0), (0, 0))
    kp = jnp.pad(k, pad)
    vp = jnp.pad(v, pad)
    qc = jnp.moveaxis(q.reshape(B, n, CHUNK, H_C, DH), 1, 0)

    def one_chunk(xs):
        qn, ci = xs
        start = ci * CHUNK
        kb = lax.dynamic_slice_in_dim(kp, start, C_WIN + CHUNK, axis=1)
        vb = lax.dynamic_slice_in_dim(vp, start, C_WIN + CHUNK, axis=1)
        q_pos = start + jnp.arange(CHUNK)
        k_pos = start - C_WIN + jnp.arange(C_WIN + CHUNK)
        return _band_attend(qn, kb, vb, q_pos, k_pos, rel_table)

    out = lax.map(one_chunk, (qc, jnp.arange(n)))
    return jnp.moveaxis(out, 0, 1).reshape(B, T, H_C, DH)

def _odd_project(h, w_in):
    B, T = h.shape[:2]
    z = jnp.einsum('btd,de->bte', h, w_in)
    q, k, v = _split(z, (C_W, C_W, C_W))
    return q.reshape(B, T, H_C, DH), k.reshape(B, T, H_C, DH), v.reshape(B, T, H_C, DH)

def setup_inputs(seed: int = 0) -> dict:
    key = jax.random.key(seed)
    ks = jax.random.split(key, 26)

    def nrm(k, shape, s):
        return jax.random.normal(k, shape, F32) * s

    c_buf = min(C_WIN, PAST_LEN)
    return {
        "x_prompt": nrm(ks[0], (BATCH, SEQ, D_MODEL), 1.0),
        "x_sample": nrm(ks[1], (DEC_BATCH, DEC_SEQ, D_MODEL), 1.0),
        "c_prompt": nrm(ks[2], (BATCH, D_MODEL), 1.0),
        "c_sample": nrm(ks[3], (DEC_BATCH, D_MODEL), 1.0),
        "cache_a_k": nrm(ks[4], (N_EVEN, DEC_BATCH, PAST_LEN, H_A, DH), 1.0),
        "cache_a_v": nrm(ks[5], (N_EVEN, DEC_BATCH, PAST_LEN, H_A, DH), 1.0),
        "cache_a_kidx": nrm(ks[6], (N_EVEN, DEC_BATCH, PAST_LEN, D_I), 1.0),
        "state_b": nrm(ks[7], (N_EVEN, DEC_BATCH, H_B, DK_B, DV_B), 0.5),
        "cache_c_k": nrm(ks[8], (N_ODD, DEC_BATCH, c_buf, H_C, DH), 1.0),
        "cache_c_v": nrm(ks[9], (N_ODD, DEC_BATCH, c_buf, H_C, DH), 1.0),
        "w_ada": nrm(ks[10], (DEPTH, D_MODEL, 6 * D_MODEL), 0.3 * D_MODEL ** -0.5),
        "b_ada": nrm(ks[11], (DEPTH, 6 * D_MODEL), 0.02),
        "norm_mix": 1.0 + nrm(ks[12], (DEPTH, D_MODEL), 0.05),
        "norm_ffn": 1.0 + nrm(ks[13], (DEPTH, D_MODEL), 0.05),
        "norm_final": 1.0 + nrm(ks[14], (D_MODEL,), 0.05),
        "w_in_even": nrm(ks[15], (N_EVEN, D_MODEL, EVEN_IN), D_MODEL ** -0.5),
        "w_out_even": nrm(ks[16], (N_EVEN, A_W + B_VW, D_MODEL), (A_W + B_VW) ** -0.5),
        "t5_table": nrm(ks[17], (N_BUCKETS, H_A), 0.5),
        "lb_logits": nrm(ks[18], (N_EVEN + 1, B_KW), 0.5),
        "norm_b_out": 1.0 + nrm(ks[19], (N_EVEN, B_VW), 0.05),
        "w_in_odd": nrm(ks[20], (N_ODD, D_MODEL, 3 * C_W), D_MODEL ** -0.5),
        "w_out_odd": nrm(ks[21], (N_ODD, C_W, D_MODEL), C_W ** -0.5),
        "rel_table_c": nrm(ks[22], (N_ODD, 2 * REL_CLIP + 1, H_C), 0.5),
        "w_ffn_gate": nrm(ks[23], (DEPTH, D_MODEL, D_FF), D_MODEL ** -0.5),
        "w_ffn_up": nrm(ks[24], (DEPTH, D_MODEL, D_FF), D_MODEL ** -0.5),
        "w_ffn_down": nrm(ks[25], (DEPTH, D_FF, D_MODEL), D_FF ** -0.5),
    }

def reference(x_prompt, x_sample, c_prompt, c_sample, cache_a_k, cache_a_v, cache_a_kidx, state_b,
              cache_c_k, cache_c_v, w_ada, b_ada, norm_mix, norm_ffn, norm_final, w_in_even, w_out_even,
              t5_table, lb_logits, norm_b_out, w_in_odd, w_out_odd, rel_table_c,
              w_ffn_gate, w_ffn_up, w_ffn_down):
    Bp, T = x_prompt.shape[:2]
    Bs, Ts = x_sample.shape[:2]
    P = cache_a_k.shape[2]
    c_buf = cache_c_k.shape[2]
    lb_all = jnp.cumsum(jax.nn.softmax(lb_logits.astype(F32), axis=0), axis=0)
    pos_p = jnp.arange(T)
    pos_s = P + jnp.arange(Ts)
    kpos_s = jnp.arange(P + Ts)
    cpos_s = jnp.concatenate([P - c_buf + jnp.arange(c_buf), pos_s])
    ksel_p = min(K_TOP, T // 4)
    ksel_s = min(K_TOP, (P + Ts) // 4)
    c_keep = min(C_WIN, T)

    xp, xs = x_prompt, x_sample
    akp, avp, aip, bsp, ckp, cvp = [], [], [], [], [], []
    aks, avs, ais, bss, cks, cvs = [], [], [], [], [], []
    for l in range(DEPTH):
        sh1p, sc1p, g1p, sh2p, sc2p, g2p = _adaln(c_prompt, w_ada[l], b_ada[l])
        sh1s, sc1s, g1s, sh2s, sc2s, g2s = _adaln(c_sample, w_ada[l], b_ada[l])
        hp = _modulate(xp, norm_mix[l], sh1p, sc1p)
        hs = _modulate(xs, norm_mix[l], sh1s, sc1s)
        if l % 2 == 0:
            e = l // 2
            lb = lb_all[e]
            mp, ka, va, ki, S = _even_mixer(hp, None, None, None, jnp.zeros((Bp, H_B, DK_B, DV_B), F32),
                                            pos_p, pos_p, ksel_p, w_in_even[e], w_out_even[e],
                                            t5_table, lb, norm_b_out[e])
            akp.append(ka); avp.append(va); aip.append(ki); bsp.append(S)
            ms, ka, va, ki, S = _even_mixer(hs, cache_a_k[e], cache_a_v[e], cache_a_kidx[e], state_b[e],
                                            pos_s, kpos_s, ksel_s, w_in_even[e], w_out_even[e],
                                            t5_table, lb, norm_b_out[e])
            aks.append(ka); avs.append(va); ais.append(ki); bss.append(S)
        else:
            o = l // 2
            q, k, v = _odd_project(hp, w_in_odd[o])
            op = _chunk_band_prompt(q, k, v, rel_table_c[o])
            mp = jnp.einsum('bte,ed->btd', op.reshape(Bp, T, C_W), w_out_odd[o])
            ckp.append(k[:, T - c_keep:]); cvp.append(v[:, T - c_keep:])
            q, k, v = _odd_project(hs, w_in_odd[o])
            k_all = jnp.concatenate([cache_c_k[o].astype(k.dtype), k], axis=1)
            v_all = jnp.concatenate([cache_c_v[o].astype(v.dtype), v], axis=1)
            osm = _band_attend(q, k_all, v_all, pos_s, cpos_s, rel_table_c[o])
            ms = jnp.einsum('bte,ed->btd', osm.reshape(Bs, Ts, C_W), w_out_odd[o])
            cks.append(k); cvs.append(v)
        xp = xp + g1p[:, None] * mp
        xs = xs + g1s[:, None] * ms
        hp = _modulate(xp, norm_ffn[l], sh2p, sc2p)
        hs = _modulate(xs, norm_ffn[l], sh2s, sc2s)
        xp = xp + g2p[:, None] * _swiglu(hp, w_ffn_gate[l], w_ffn_up[l], w_ffn_down[l])
        xs = xs + g2s[:, None] * _swiglu(hs, w_ffn_gate[l], w_ffn_up[l], w_ffn_down[l])

    y_prompt = _rmsnorm(xp, norm_final)
    y_sample = _rmsnorm(xs, norm_final)
    a_k_p = jnp.stack(akp); a_v_p = jnp.stack(avp); a_kidx_p = jnp.stack(aip); b_state_p = jnp.stack(bsp)
    c_k_p = jnp.stack(ckp); c_v_p = jnp.stack(cvp)
    a_k_s = jnp.stack(aks); a_v_s = jnp.stack(avs); a_kidx_s = jnp.stack(ais); b_state_s = jnp.stack(bss)
    c_k_s = jnp.stack(cks); c_v_s = jnp.stack(cvs)
    return (y_prompt, y_sample, a_k_p, a_v_p, a_kidx_p, b_state_p, c_k_p, c_v_p,
            a_k_s, a_v_s, a_kidx_s, b_state_s, c_k_s, c_v_s)


_drawn_inputs = setup_inputs


def setup_inputs(seed=0):
    import zlib

    import numpy as np

    out = dict(_drawn_inputs(seed))
    spreads = {}
    factors = {'cache_a_k': 5.438,
     'cache_a_v': 4.295,
     'cache_a_kidx': 4.522,
     'cache_c_k': 5.286,
     'cache_c_v': 4.239,
     'norm_ffn': 4.753,
     't5_table': 8.0,
     'norm_b_out': 8.0,
     'rel_table_c': 7.034}
    for name, (base, spread) in spreads.items():
        noise = np.random.default_rng([zlib.crc32(name.encode()), seed]).standard_normal(out[name].shape)
        drawn = base * np.exp(spread * noise) if base else spread * noise
        out[name] = __import__('jax').numpy.asarray(drawn.astype(out[name].dtype))
    for name, factor in factors.items():
        out[name] = (out[name] * factor).astype(out[name].dtype)
    return out
```

```python
from contextlib import ExitStack

import numpy as np

import concourse.bass as bass
from concourse import mybir

F32 = mybir.dt.float32
ACT = mybir.ActivationFunctionType
ALU = mybir.AluOpType
AX_X = mybir.AxisListType.X

P = 128
D = 1024
KD = D // P
T = 1024
S = 32
N = T + S
PAST = 2048
EPS = 1e-6
DH = 64
HA = 8
HC = 16
HB = 4
KTOP = 256
FF = 2816
KF = FF // P
CHUNK = 64
BACK = 8 * CHUNK
TILES = T // P
THIRD = N // 3
THIRDS = [(t * THIRD, (t + 1) * THIRD) for t in range(3)]
SPANS = [(0, THIRD, 0), (THIRD, 2 * THIRD, 0), (2 * THIRD, T, 0), (T, N, 1)]
MASKED = -1e30
OUT_OF_REACH = -3.0e38
TAKEN = -3.4e38
QA, KA, QI, KI, QB, FB, GB, Z0_CHUNKS = 0, 4, 8, 12, 13, 17, 21, 25
Z0_FIRST = 13
Z1_CHUNKS = 16
T5_LEN = PAST + S - 1 + P
BAND_KEYS = BACK + P
REL = 128
BAND_LEN = 768
SKEW_A, SKEW_C, SKEW_S = T + P - 1, BAND_KEYS + P - 1, PAST + S + S - 1


class Tools:

    def __init__(self, nc):
        self.nc, self.stack, self.sems = nc, ExitStack(), []

    def sb(self, name, shape, dt=F32):
        return self.stack.enter_context(self.nc.sbuf_tensor(name, shape, dt))

    def ps(self, name, shape, dt=F32):
        return self.stack.enter_context(self.nc.psum_tensor(name, shape, dt))

    def sem(self, name):
        self.sems.append(self.nc.alloc_semaphore(name))
        return self.sems[-1]

    def block(self):
        for sem in self.sems:
            self.nc.gpsimd.sem_inc(sem, START)
        self.nc.all_engine_barrier()
        return self.stack.enter_context(self.nc.Block())

    def __enter__(self):
        self.stack.__enter__()
        return self

    def __exit__(self, *a):
        self.stack.__exit__(*a)
        if self.sems:
            self.nc.clear_and_free_semaphores(self.sems)


START = 1


def after(count):
    return START + count


def wait_apart(eng, *waits):
    for _, count in waits:
        if not isinstance(count, int):
            eng.to_reg(after(count))
    eng.wait_ge(waits[0][0], after(0))
    for sem, count in waits:
        eng.wait_ge(sem, after(count))


def setup_phase(nc, io, x, mod, cols, gfin, ident, ones):
    GROUP = 4
    GROUPS = 2 * 48 // GROUP
    with Tools(nc) as m:
        cT = m.sb("cT", [P, KD, 2])
        sc = m.sb("silu_c", [P, KD, 2])
        bada = m.sb("b_ada", [P, 96])
        norms = m.sb("norms", [P, 5, KD])
        wada = [m.sb(f"w_ada{b}", [P, GROUP, KD, P]) for b in range(2)]
        acc = [m.ps(f"ada_acc{b}", [P, 512]) for b in range(2)]
        small_in, x_in = m.sem("small_in"), m.sem("x_in")
        silu_c = m.sem("silu_c_ready")
        w_in = [m.sem(f"w_ada_in{b}") for b in range(2)]
        acc_ready = [m.sem(f"ada_acc{b}") for b in range(2)]
        acc_read = [m.sem(f"ada_acc_read{b}") for b in range(2)]
        ident_zero, scale_one = m.sem("ident_zero"), m.sem("scale_plus_one")
        modf = mod[:].rearrange("p l j k s -> p (l j k) s")
        block = m.block()

        @block.sync
        def _(sp):
            sp.dma_start(cT[:], io["cT"]).then_inc(small_in, 16)
            sp.dma_start(bada[:], io["b_ada"]).then_inc(small_in, 16)
            sp.dma_start(norms[:], io["norms"]).then_inc(small_in, 16)
            with sp.Fori(0, GROUPS // 2) as i:
                for b in range(2):
                    sp.wait_ge(acc_ready[b], after(i))
                    sp.dma_start(wada[b][:], io["w_ada"][2 * i + b]).then_inc(w_in[b], 16)

        @block.gpsimd
        def _(pool):
            pool.memset(ones[:], 1.0)
            pool.memset(ident[:], 0.0).then_inc(ident_zero, 1)
            pool.wait_ge(ident_zero, after(1))
            pool.affine_select(out=ident[:], in_=ident[:], compare_op=ALU.not_equal, fill=1.0,
                               base=0, pattern=[[-1, P]], channel_multiplier=1)

        @block.scalar
        def _(act):
            act.dma_start(x[:], io["xT"]).then_inc(x_in, 16)
            act.wait_ge(small_in, after(48))
            act.activation(sc[:], cT[:], ACT.Silu).then_inc(silu_c, 1)
            act.wait_ge(x_in, after(16))

        @block.tensor
        def _(pe):
            pe.wait_ge(silu_c, after(1))
            with pe.Fori(0, GROUPS // 2) as i:
                for b in range(2):
                    pe.wait_ge(w_in[b], after(16 * i + 16))
                    pe.wait_ge(acc_read[b], after(i))
                    for g in range(GROUP):
                        for k in range(KD):
                            last = pe.matmul(acc[b][:, 2 * g:2 * g + 2], wada[b][:, g, k, :], sc[:, k, :],
                                             start=k == 0, stop=k == KD - 1)
                    last.then_inc(acc_ready[b], 1)

        @block.vector
        def _(dve):
            dve.wait_ge(small_in, after(48))
            dve.tensor_copy(gfin[:], norms[:, 4])
            with dve.Fori(0, GROUPS // 2) as i:
                for b in range(2):
                    dve.wait_ge(acc_ready[b], after(i + 1))
                    c = (2 * i + b) * GROUP
                    dve.tensor_tensor(modf[:, bass.ds(c, GROUP), :],
                                      acc[b][:, 0:2 * GROUP].rearrange("p (g s) -> p g s", s=2),
                                      bada[:, bass.ds(c, GROUP)].unsqueeze(2).to_broadcast([P, GROUP, 2]),
                                      ALU.add).then_inc(acc_read[b], 1)
            dve.wait_ge(acc_read[0], after(GROUPS // 2))
            dve.wait_ge(acc_read[1], after(GROUPS // 2))
            for l in range(2):
                for half in range(2):
                    n = 2 * l + half
                    dve.tensor_scalar(cols[:, n], mod[:, l, 3 * half + 1], 1.0, None, ALU.add).then_inc(scale_one, 1)
                    dve.wait_ge(scale_one, after(2 * n + 1))
                    dve.tensor_tensor(cols[:, n], cols[:, n],
                                      norms[:, n].unsqueeze(2).to_broadcast([P, KD, 2]), ALU.mult
                                      ).then_inc(scale_one, 1)


def norm_phase(nc, name, x, out, gain, shift, ones, store=None):
    with Tools(nc) as m:
        sq = [m.sb(f"{name}_sq{b}", [P, THIRD]) for b in range(2)]
        rstd = m.sb(f"{name}_rstd", [P, N])
        eps = m.sb(f"{name}_eps", [P, 1])
        ssq = [m.ps(f"{name}_ssq{t}", [P, 512]) for t in range(3)]
        eps_set, sq_ready, sq_used = m.sem(f"{name}_eps"), m.sem(f"{name}_sq"), m.sem(f"{name}_sq_used")
        root, rstd_ready = m.sem(f"{name}_root"), m.sem(f"{name}_rstd")
        scaled, done = m.sem(f"{name}_scaled"), m.sem(f"{name}_stored")
        block = m.block()

        @block.scalar
        def _(act):
            n = 0
            for lo, hi in THIRDS:
                for k in range(KD):
                    if n >= 2:
                        act.wait_ge(sq_used, after(n - 1))
                    act.activation(sq[n % 2][:], x[:, k, lo:hi], ACT.Square).then_inc(sq_ready, 1)
                    n += 1
            act.wait_ge(eps_set, after(1))
            for t, (lo, hi) in enumerate(THIRDS):
                act.wait_ge(sq_used, after(KD * (t + 1)))
                act.activation(rstd[:, lo:hi], ssq[t][:, 0:THIRD], ACT.Sqrt, bias=eps[:, 0:1],
                               scale=1.0 / D).then_inc(root, 1)
            if shift is not None:
                n = 0
                for a, b, s in SPANS:
                    for k in range(KD):
                        n += 1
                        act.wait_ge(scaled, after(n))
                        act.activation(out[:, k, a:b], out[:, k, a:b], ACT.Identity,
                                       bias=shift[:, k, s:s + 1])

        @block.tensor
        def _(pe):
            n = 0
            for t in range(3):
                for k in range(KD):
                    n += 1
                    pe.wait_ge(sq_ready, after(n))
                    last = pe.matmul(ssq[t][:, 0:THIRD], ones[:], sq[(n - 1) % 2][:], start=k == 0, stop=k == KD - 1)
                    last.then_inc(sq_used, 1)

        @block.vector
        def _(dve):
            dve.memset(eps[:], EPS).then_inc(eps_set, 1)
            for t, (lo, hi) in enumerate(THIRDS):
                dve.wait_ge(root, after(t + 1))
                dve.reciprocal(rstd[:, lo:hi], rstd[:, lo:hi]).then_inc(rstd_ready, 1)
            for n, (a, b, s) in enumerate(SPANS):
                dve.wait_ge(rstd_ready, after(min(n + 1, 3)))
                for k in range(KD):
                    dve.scalar_tensor_tensor(out=out[:, k, a:b], in0=x[:, k, a:b],
                                             scalar=gain[:, k, s:s + 1] if shift is not None else gain[:, k:k + 1],
                                             in1=rstd[:, a:b], op0=ALU.mult, op1=ALU.mult).then_inc(scaled, 1)

        @block.sync
        def _(sp):
            if store is not None:
                sp.wait_ge(scaled, after(KD * len(SPANS)))
                sp.dma_start(store, out[:]).then_inc(done, 16)
                sp.wait_ge(done, after(16))


def over_chunks(eng, count, body):
    if count >= 2:
        with eng.Fori(0, count // 2) as i:
            for b in range(2):
                body(i, b)
    if count % 2:
        body(count // 2, 0)


def projection(m, name, w_dram, first, count, src, z_dram):
    w = [m.sb(f"{name}_w{b}", [P, KD, P]) for b in range(2)]
    stage = [m.sb(f"{name}_stage{b}", [P, N]) for b in range(2)]
    acc = [[m.ps(f"{name}_acc{b}{t}", [P, 512]) for t in range(3)] for b in range(2)]
    w_in = [m.sem(f"{name}_w_in{b}") for b in range(2)]
    acc_ready = [m.sem(f"{name}_acc{b}") for b in range(2)]
    acc_read = [m.sem(f"{name}_acc_read{b}") for b in range(2)]
    stored = [m.sem(f"{name}_stored{b}") for b in range(2)]

    def loads(sp):
        def body(i, b):
            sp.wait_ge(acc_ready[b], after(3 * i))
            sp.dma_start(w[b][:], w_dram[first + 2 * i + b]).then_inc(w_in[b], 16)
        over_chunks(sp, count, body)

    def products(pe):
        def body(i, b):
            pe.wait_ge(w_in[b], after(16 * i + 16))
            for t, (lo, hi) in enumerate(THIRDS):
                pe.wait_ge(acc_read[b], after(3 * i))
                for k in range(KD):
                    last = pe.matmul(acc[b][t][:, 0:THIRD], w[b][:, k, :], src[:, k, lo:hi],
                                     start=k == 0, stop=k == KD - 1)
                last.then_inc(acc_ready[b], 1)
        over_chunks(pe, count, body)

    def copies(act):
        def body(i, b):
            act.wait_ge(stored[b], after(16 * i))
            for t, (lo, hi) in enumerate(THIRDS):
                act.wait_ge(acc_ready[b], after(3 * i + t + 1))
                act.activation(stage[b][:, lo:hi], acc[b][t][:, 0:THIRD], ACT.Copy).then_inc(acc_read[b], 1)
            act.wait_ge(acc_read[b], after(3 * i + 3))
            act.dma_start(z_dram[first + 2 * i + b], stage[b][:]).then_inc(stored[b], 16)
        over_chunks(act, count, body)
        act.wait_ge(stored[0], after(16 * ((count + 1) // 2)))
        if count >= 2:
            act.wait_ge(stored[1], after(16 * (count // 2)))

    return loads, products, copies


def token_major_phase(nc, name, w_dram, wide, src, out_dram):
    narrow = out_dram.shape[1] - 512 * wide
    blocks = [(c, 512) for c in range(wide)] + ([(wide, narrow)] if narrow else [])
    with Tools(nc) as m:
        w = [m.sb(f"{name}_w{c}", [P, KD, n]) for c, n in blocks]
        stage = [m.sb(f"{name}_stage{b}", [P, 512]) for b in range(4)]
        acc = [m.ps(f"{name}_acc{b}", [P, 512]) for b in range(4)]
        w_in = [m.sem(f"{name}_w_in{c}") for c, _ in blocks]
        acc_ready, acc_read = m.sem(f"{name}_acc"), m.sem(f"{name}_acc_read")
        stored = [m.sem(f"{name}_stored{b}") for b in range(4)]
        block = m.block()
        units = [(c, n, lo, min(lo + P, N)) for c, n in blocks for lo in range(0, N, P)]

        @block.sync
        def _(sp):
            for c, n in blocks:
                sp.dma_start(w[c][:], w_dram[c][:, :, 0:n]).then_inc(w_in[c], 16)
            for u, (c, n, lo, hi) in enumerate(units):
                sp.wait_ge(acc_read, after(u + 1))
                sp.dma_start(out_dram[lo:hi, 512 * c:512 * c + n], stage[u % 4][0:hi - lo, 0:n]
                             ).then_inc(stored[u % 4], 16)
            for b in range(4):
                sp.wait_ge(stored[b], after(16 * ((len(units) - b + 3) // 4)))

        @block.tensor
        def _(pe):
            for u, (c, n, lo, hi) in enumerate(units):
                if lo == 0:
                    pe.wait_ge(w_in[c], after(16))
                if u >= 4:
                    pe.wait_ge(acc_read, after(u - 3))
                for k in range(KD):
                    last = pe.matmul(acc[u % 4][0:hi - lo, 0:n], src[:, k, lo:hi], w[c][:, k, :],
                                     start=k == 0, stop=k == KD - 1)
                last.then_inc(acc_ready, 1)

        @block.vector
        def _(dve):
            for u, (c, n, lo, hi) in enumerate(units):
                dve.wait_ge(acc_ready, after(u + 1))
                if u >= 4:
                    dve.wait_ge(stored[u % 4], after(16 * (u // 4)))
                dve.tensor_copy(stage[u % 4][0:hi - lo, 0:n], acc[u % 4][0:hi - lo, 0:n]).then_inc(acc_read, 1)


def residual_phase(nc, name, w_dram, nk, src, x, gate, src_dram=None):
    with Tools(nc) as m:
        w = [m.sb(f"{name}_w{b}", [P, nk, P]) for b in range(2)]
        acc = [[m.ps(f"{name}_acc{b}{t}", [P, 512]) for t in range(3)] for b in range(2)]
        w_in = [m.sem(f"{name}_w_in{b}") for b in range(2)]
        src_in = m.sem(f"{name}_src_in")
        acc_ready = [m.sem(f"{name}_acc{b}") for b in range(2)]
        acc_read = [m.sem(f"{name}_acc_read{b}") for b in range(2)]
        block = m.block()

        @block.sync
        def _(sp):
            with sp.Fori(0, KD // 2) as i:
                for b in range(2):
                    sp.wait_ge(acc_ready[b], after(3 * i))
                    sp.dma_start(w[b][:], w_dram[2 * i + b]).then_inc(w_in[b], 16)

        @block.scalar
        def _(act):
            if src_dram is not None:
                act.dma_start(src[:], src_dram.rearrange("k p n -> p k n")).then_inc(src_in, 16)
                act.wait_ge(src_in, after(16))

        @block.tensor
        def _(pe):
            if src_dram is not None:
                pe.wait_ge(src_in, after(16))
            with pe.Fori(0, KD // 2) as i:
                for b in range(2):
                    pe.wait_ge(w_in[b], after(16 * i + 16))
                    pe.wait_ge(acc_read[b], after(4 * i))
                    for t, (lo, hi) in enumerate(THIRDS):
                        for k in range(nk):
                            last = pe.matmul(acc[b][t][:, 0:THIRD], w[b][:, k, :], src[:, k, lo:hi],
                                             start=k == 0, stop=k == nk - 1)
                        last.then_inc(acc_ready[b], 1)

        @block.vector
        def _(dve):
            with dve.Fori(0, KD // 2) as i:
                for b in range(2):
                    c = 2 * i + b
                    for n, (lo, hi, s) in enumerate(SPANS):
                        t = min(n, 2)
                        dve.wait_ge(acc_ready[b], after(3 * i + t + 1))
                        dve.scalar_tensor_tensor(out=x[:, bass.ds(c, 1), lo:hi],
                                                 in0=acc[b][t][:, lo - t * THIRD:hi - t * THIRD].unsqueeze(1),
                                                 scalar=gate[:, bass.ds(c, 1), s], in1=x[:, bass.ds(c, 1), lo:hi],
                                                 op0=ALU.mult, op1=ALU.add).then_inc(acc_read[b], 1)


def ffn_up_phase(nc, name, wg_dram, wu_dram, src, out):
    with Tools(nc) as m:
        wg = [m.sb(f"{name}_wg{b}", [P, KD, P]) for b in range(2)]
        wu = [m.sb(f"{name}_wu{b}", [P, KD, P]) for b in range(2)]
        gate = [m.ps(f"{name}_gate{t}", [P, 512]) for t in range(3)]
        up = [m.ps(f"{name}_up{t}", [P, 512]) for t in range(3)]
        silu = [m.sb(f"{name}_silu{t}", [P, THIRD]) for t in range(3)]
        w_in = [m.sem(f"{name}_w_in{b}") for b in range(2)]
        acc_ready = [[m.sem(f"{name}_acc{b}{t}") for t in range(3)] for b in range(2)]
        gated = [m.sem(f"{name}_gated{t}") for t in range(3)]
        acc_read = [[m.sem(f"{name}_acc_read{b}{t}") for t in range(3)] for b in range(2)]
        block = m.block()

        @block.sync
        def _(sp):
            with sp.Fori(0, KF // 2) as i:
                for b in range(2):
                    sp.wait_ge(acc_ready[b][2], after(i))
                    sp.dma_start(wg[b][:], wg_dram[2 * i + b]).then_inc(w_in[b], 16)
                    sp.dma_start(wu[b][:], wu_dram[2 * i + b]).then_inc(w_in[b], 16)

        @block.tensor
        def _(pe):
            with pe.Fori(0, KF // 2) as i:
                for b in range(2):
                    pe.wait_ge(w_in[b], after(32 * i + 32))
                    for t, (lo, hi) in enumerate(THIRDS):
                        pe.wait_ge(acc_read[1 - b][t], after(i + b))
                        for w, acc in ((wg, gate), (wu, up)):
                            for k in range(KD):
                                last = pe.matmul(acc[t][:, 0:THIRD], w[b][:, k, :], src[:, k, lo:hi],
                                                 start=k == 0, stop=k == KD - 1)
                        last.then_inc(acc_ready[b][t], 1)

        @block.scalar
        def _(act):
            with act.Fori(0, KF // 2) as i:
                for b in range(2):
                    for t in range(3):
                        act.wait_ge(acc_ready[b][t], after(i + 1))
                        act.wait_ge(acc_read[1 - b][t], after(i + b))
                        act.activation(silu[t][:], gate[t][:, 0:THIRD], ACT.Silu).then_inc(gated[t], 1)

        @block.vector
        def _(dve):
            with dve.Fori(0, KF // 2) as i:
                for b in range(2):
                    for t, (lo, hi) in enumerate(THIRDS):
                        dve.wait_ge(gated[t], after(2 * i + b + 1))
                        dve.tensor_tensor(out[:, bass.ds(2 * i + b, 1), lo:hi], silu[t][:].unsqueeze(1),
                                          up[t][:, 0:THIRD].unsqueeze(1), ALU.mult).then_inc(acc_read[b][t], 1)


def bias_phase(nc, io):
    with Tools(nc) as m:
        t5 = m.sb("t5", [32, HA])
        onehot = m.sb("onehot", [32, T5_LEN])
        fa = m.sb("t5_by_distance", [HA, T5_LEN])
        rel = m.sb("rel_reversed", [HC, 2 * REL + 1])
        fc = m.sb("rel_by_distance", [HC, BAND_LEN])
        acc = [m.ps(f"t5_acc{c}", [HA, 512]) for c in range(5)]
        loaded, acc_ready, fa_ready, fc_ready = m.sem("bias_in"), m.sem("t5_acc"), m.sem("t5_ready"), m.sem("rel_ready")
        lines_out = m.sem("bias_lines_out")
        pieces = [(lo, min(lo + 512, T5_LEN)) for lo in range(0, T5_LEN, 512)]
        block = m.block()

        @block.sync
        def _(sp):
            sp.dma_start(t5[:], io["t5"]).then_inc(loaded, 16)
            sp.dma_start(onehot[:], io["t5_onehot"]).then_inc(loaded, 16)
            sp.dma_start(rel[:], io["rel_rev"]).then_inc(loaded, 16)
            for name, line, ready, heads, rows, first, length in (
                    ("skew_a", fa, (fa_ready, len(pieces)), HA, P, T5_LEN - SKEW_A, SKEW_A),
                    ("skew_s", fa, (fa_ready, len(pieces)), HA, S, 0, SKEW_S),
                    ("skew_c", fc, (fc_ready, 2), HC, P, 0, SKEW_C)):
                sp.wait_ge(ready[0], after(ready[1]))
                sp.dma_start(io[name].rearrange("h (p n) -> h p n", p=rows),
                             line[:, first:first + length].unsqueeze(1).to_broadcast([heads, rows, length])
                             ).then_inc(lines_out, 16)
            sp.wait_ge(lines_out, after(48))

        @block.tensor
        def _(pe):
            pe.wait_ge(loaded, after(48))
            for c, (lo, hi) in enumerate(pieces):
                pe.matmul(acc[c][:, 0:hi - lo], t5[:], onehot[:, lo:hi], start=True, stop=True).then_inc(acc_ready, 1)

        @block.vector
        def _(dve):
            for c, (lo, hi) in enumerate(pieces):
                dve.wait_ge(acc_ready, after(c + 1))
                dve.tensor_scalar(fa[:, lo:hi], acc[c][:, 0:hi - lo], DH ** 0.5, None, ALU.mult).then_inc(fa_ready, 1)
            far = BAND_LEN - 1 - 2 * REL
            dve.tensor_scalar(fc[:, 0:far], rel[:, 0:1].to_broadcast([HC, far]), DH ** 0.5, None, ALU.mult).then_inc(fc_ready, 1)
            dve.tensor_scalar(fc[:, far:BAND_LEN], rel[:], DH ** 0.5, None, ALU.mult).then_inc(fc_ready, 1)


def shifted(skew, rows, length, shift, keys):
    return skew[:, shift:shift + rows * (length - 1)].rearrange(
        "h (p n) -> p h n", n=length - 1)[:, :, 0:keys]


def score_offset(i):
    return P * i * (i + 1) // 2


SAMPLE_KEYS = PAST + S
SAMPLE_AT = score_offset(TILES)


def index_phase(nc, io, score):
    with Tools(nc) as m:
        qi = m.sb("qi", [P, 4, N])
        ki = m.sb("ki", [P, N])
        ki_past = m.sb("ki_past", [P, PAST])
        w = m.sb("w_index", [P, TILES + 1, HA])
        relu = [m.sb(f"relu{b}", [P, 1024]) for b in range(2)]
        dots = [m.ps(f"dots{b}", [P, 1024]) for b in range(2)]
        loaded, w_scaled = m.sem("index_in"), m.sem("w_index_scaled")
        dots_ready, relu_ready, added = m.sem("dots"), m.sem("relu"), m.sem("score_added")
        units = [(i, P, hd, ki, 0, P * (i + 1), score_offset(i)) for i in range(2, TILES) for hd in range(HA)]
        for src, lo, n, at in ((ki_past, 0, 1024, 0), (ki_past, 1024, 1024, 1024), (ki, T, S, PAST)):
            units += [(TILES, S, hd, src, lo, n, SAMPLE_AT + at) for hd in range(HA)]
        block = m.block()

        @block.sync
        def _(sp):
            sp.dma_start(qi[:], io["z0"][QI:QI + 4].rearrange("c p n -> p c n")).then_inc(loaded, 16)
            sp.dma_start(ki[:], io["z0"][KI]).then_inc(loaded, 16)
            sp.dma_start(ki_past[:], io["ki_past"]).then_inc(loaded, 16)
            sp.dma_start(w[:, 0:TILES, :], io["zt0"][0:T, 1024:1024 + HA].rearrange("(i p) h -> p i h", p=P)
                         ).then_inc(loaded, 16)
            sp.dma_start(w[0:S, TILES, :], io["zt0"][T:N, 1024:1024 + HA]).then_inc(loaded, 16)

        @block.tensor
        def _(pe):
            pe.wait_ge(loaded, after(80))
            for u, (i, rows, hd, src, lo, n, at) in enumerate(units):
                half = slice(DH * (hd % 2), DH * (hd % 2) + DH)
                if u >= 2:
                    pe.wait_ge(relu_ready, after(u - 1))
                for c in range(0, n, 512):
                    e = min(c + 512, n)
                    last = pe.matmul(dots[u % 2][0:rows, c:e], qi[half, hd // 2, P * i:P * i + rows],
                                     src[half, lo + c:lo + e], start=True, stop=True)
                last.then_inc(dots_ready, 1)

        @block.scalar
        def _(act):
            for u, (i, rows, hd, src, lo, n, at) in enumerate(units):
                act.wait_ge(dots_ready, after(u + 1))
                if u >= 2:
                    act.wait_ge(added, after(u - 1))
                act.activation(relu[u % 2][0:rows, 0:n], dots[u % 2][0:rows, 0:n], ACT.Relu,
                               scale=DH ** -0.5).then_inc(relu_ready, 1)

        @block.vector
        def _(dve):
            dve.wait_ge(loaded, after(80))
            dve.tensor_scalar(w[:, 0:TILES, :], w[:, 0:TILES, :], HA ** -0.5, None, ALU.mult).then_inc(w_scaled, 1)
            dve.tensor_scalar(w[0:S, TILES, :], w[0:S, TILES, :], HA ** -0.5, None, ALU.mult).then_inc(w_scaled, 1)
            dve.wait_ge(w_scaled, after(2))
            for u, (i, rows, hd, src, lo, n, at) in enumerate(units):
                dve.wait_ge(relu_ready, after(u + 1))
                out = score[0:rows, at:at + n]
                if hd == 0:
                    dve.tensor_scalar(out, relu[u % 2][0:rows, 0:n], w[0:rows, i, 0:1], None, ALU.mult
                                      ).then_inc(added, 1)
                else:
                    dve.wait_ge(added, after(u))
                    dve.scalar_tensor_tensor(out=out, in0=relu[u % 2][0:rows, 0:n], scalar=w[0:rows, i, hd:hd + 1],
                                             in1=out, op0=ALU.mult, op1=ALU.add).then_inc(added, 1)
            dve.wait_ge(added, after(len(units)))
            for i in range(2, TILES):
                end = score_offset(i + 1)
                dve.memset(score[0:CHUNK, end - CHUNK:end], OUT_OF_REACH)


def choosing(m, score, mask_sample_dram):
    rounds = KTOP // 8
    lists = [[(P, score_offset(i), P * (i + 1)) for i in pair] for pair in ((2, 3), (4, 5), (6, 7))]
    lists.append([(S, SAMPLE_AT, SAMPLE_KEYS)])
    top = [m.sb(f"top{a}", [P, 8]) for a in range(2)]
    found = [[m.sem(f"top_found{n}{a}") for a in range(len(rows))] for n, rows in enumerate(lists)]
    taken = [[m.sem(f"top_taken{n}{a}") for a in range(len(rows))] for n, rows in enumerate(lists)]
    masked, stored = m.sem("mask_ready"), m.sem("mask_stored")

    def choose(dve):
        for n, rows in enumerate(lists):
            with dve.Fori(0, rounds) as r:
                for a, (p, at, width) in enumerate(rows):
                    wait_apart(dve, (taken[n][a], r))
                    dve.max(top[a][0:p, :], score[0:p, at:at + width]).then_inc(found[n][a], 1)
                for a, (p, at, width) in enumerate(rows):
                    wait_apart(dve, (found[n][a], r + 1))
                    dve.match_replace(score[0:p, at:at + width], top[a][0:p, :], score[0:p, at:at + width],
                                      TAKEN).then_inc(taken[n][a], 1)
            for a, (p, at, width) in enumerate(rows):
                dve.wait_ge(taken[n][a], after(rounds))
                dve.tensor_scalar(score[0:p, at:at + width], score[0:p, at:at + width], (TAKEN + OUT_OF_REACH) / 2,
                                  MASKED, ALU.is_gt, ALU.mult).then_inc(masked, 1)
        for i in range(2):
            end = score_offset(i + 1)
            dve.memset(score[:, score_offset(i):end], 0.0).then_inc(masked, 1)
            dve.wait_ge(masked, after(8 + i))
            dve.memset(score[0:CHUNK, end - CHUNK:end], MASKED)

    def store(sp):
        sp.wait_ge(masked, after(7))
        sp.dma_start(mask_sample_dram, score[0:S, SAMPLE_AT:SAMPLE_AT + SAMPLE_KEYS]).then_inc(stored, 16)
        sp.wait_ge(stored, after(16))

    return choose, store


def prompt_attention_phase(nc, name, io, z, q0, k0, vt, v0, skew, width, heads, back, mask, ident, mix):
    pairs = heads // 2
    units = 2 * TILES
    keys = [P * min(i + 1, (back or TILES) + 1) for i in range(TILES)]
    with Tools(nc) as m:
        q = [m.sb(f"{name}_q{b}", [P, T]) for b in range(2)]
        k = [m.sb(f"{name}_k{b}", [P, T]) for b in range(2)]
        v = [m.sb(f"{name}_v{b}", [P, TILES, P]) for b in range(2)]
        bias = [m.sb(f"{name}_bias{b}", [P, 2, width]) for b in range(2)]
        extra = [m.sb(f"{name}_extra{a}", [P, T]) for a in range(2)] if mask is not None else None
        prob = [m.sb(f"{name}_prob{a}", [P, max(keys)]) for a in range(2)]
        probT = [m.sb(f"{name}_probT{a}", [P, max(keys)]) for a in range(2)]
        top, ntop, total, inv = (m.sb(f"{name}_{x}", [P, 2 * units]) for x in ("max", "nmax", "sum", "inv"))
        o = [m.sb(f"{name}_o{a}", [P, P]) for a in range(2)]
        oT = [m.sb(f"{name}_oT{b}", [P, T]) for b in range(2)]
        dots = [m.ps(f"{name}_dots{a}", [P, 1024]) for a in range(2)]
        turn = [m.ps(f"{name}_turn{g}", [P, 512]) for g in range(2)]
        ops = m.ps(f"{name}_out", [P, 512])
        oTps = m.ps(f"{name}_outT", [P, 512])
        loaded = [m.sem(f"{name}_in{b}") for b in range(2)]
        band_masked = [m.sem(f"{name}_band{b}") for b in range(2)]
        dots_ready, extra_ready, logits, ntop_ready = (m.sem(f"{name}_{x}") for x in ("dots", "extra", "logits", "nmax"))
        prob_ready, inv_ready, o_ready, oT_ready = (m.sem(f"{name}_{x}") for x in ("prob", "inv", "o", "outT"))
        turned = [m.sem(f"{name}_turned{g}") for g in range(2)]
        probT_ready = [m.sem(f"{name}_probT{g}") for g in range(2)]
        out_ready = [m.sem(f"{name}_out{b}") for b in range(2)]
        oT_copied = [m.sem(f"{name}_oT{b}") for b in range(2)]
        stored = [m.sem(f"{name}_stored{b}") for b in range(2)]
        all_units = [(b, i, hd) for b in range(2) for i in range(TILES) for hd in range(2)]
        U = len(all_units)
        second = [keys[i] > 512 for _, i, _ in all_units]
        seconds = sum(second)
        block = m.block()

        @block.sync
        def _(sp):
            with sp.Fori(0, pairs // 2) as it:
                for b in range(2):
                    g = 2 * it + b
                    sp.wait_ge(out_ready[b], after(units * it))
                    sp.dma_start(q[b][:], z[q0 + g][:, 0:T]).then_inc(loaded[b], 16)
                    sp.dma_start(k[b][:], z[k0 + g][:, 0:T]).then_inc(loaded[b], 16)
                    sp.dma_start(bias[b][:], shifted(skew[bass.ds(2 * g, 2)], P, width + P - 1, P - 1, width)
                                 ).then_inc(loaded[b], 16)
                    sp.dma_start(v[b][:], vt[0:T, bass.ds(v0 + P * g, P)].rearrange("(i p) n -> p i n", p=P)
                                 ).then_inc(loaded[b], 16)

        @block.gpsimd
        def _(pool):
            with pool.Fori(0, pairs // 2) as it:
                for b in range(2):
                    if mask is None:
                        wait_apart(pool, (loaded[b], 64 * it + 64))
                        pool.memset(bias[b][0:CHUNK, :, width - CHUNK:width], MASKED).then_inc(band_masked[b], 1)
                        pool.memset(bias[b][CHUNK:P, :, 0:CHUNK], MASKED).then_inc(band_masked[b], 1)
                    else:
                        pool.wait_ge(loaded[b], after(64 * it + 64))
                        for i in range(TILES):
                            for hd in range(2):
                                u = units * b + 2 * i + hd
                                pool.wait_ge(logits, after(U * it + max(u - 1, 0)))
                                pool.tensor_tensor(extra[u % 2][:, 0:keys[i]], bias[b][:, hd, width - keys[i]:width],
                                                   mask[:, score_offset(i):score_offset(i + 1)], ALU.add
                                                   ).then_inc(extra_ready, 1)

        @block.tensor
        def _(pe):
            def scores(it, u):
                b, i, hd = all_units[u]
                half = slice(DH * hd, DH * hd + DH)
                if u % units == 0:
                    pe.wait_ge(loaded[b], after(64 * it + 64))
                pe.wait_ge(logits, after(U * it + max(u - 1, 0)))
                first = P * (i + 1) - keys[i]
                for c in range(0, keys[i], 512):
                    e = min(c + 512, keys[i])
                    last = pe.matmul(dots[u % 2][:, c:e], q[b][half, P * i:P * i + P],
                                     k[b][half, first + c:first + e], start=True, stop=True)
                last.then_inc(dots_ready, 1)

            def turns(it, u):
                b, i, hd = all_units[u]
                pe.wait_ge(prob_ready, after(U * it + u + 1))
                for g in range(2 if second[u] else 1):
                    pe.wait_ge(probT_ready[g], after((U if g == 0 else seconds) * it + (u if g == 0 else sum(second[:u]))))
                    for c in range(512 * g, min(512 * g + 512, keys[i]), P):
                        last = pe.transpose(turn[g][:, c - 512 * g:c - 512 * g + P], prob[u % 2][:, c:c + P], ident[:])
                    last.then_inc(turned[g], 1)

            def values(it, u):
                b, i, hd = all_units[u]
                pe.wait_ge(probT_ready[0], after(U * it + u + 1))
                if second[u]:
                    pe.wait_ge(probT_ready[1], after(seconds * it + sum(second[:u + 1])))
                pe.wait_ge(o_ready, after(U * it + u))
                at = P * (i % 2) + DH * hd
                blocks = keys[i] // P
                for c in range(blocks):
                    last = pe.matmul(ops[:, at:at + DH], probT[u % 2][:, P * c:P * c + P],
                                     v[b][:, i + 1 - blocks + c, DH * hd:DH * hd + DH], start=c == 0, stop=c == blocks - 1)
                last.then_inc(out_ready[b], 1)

            def turn_out(it, u):
                b, i, hd = all_units[u]
                if hd == 0:
                    return
                pe.wait_ge(o_ready, after(U * it + u + 1))
                if i == 0:
                    pe.wait_ge(oT_copied[1 - b], after(TILES * (it + b)))
                else:
                    pe.wait_ge(oT_copied[b], after(TILES * it + i))
                pe.transpose(oTps[:, 0:P], o[i % 2][:], ident[:]).then_inc(oT_ready, 1)

            with pe.Fori(0, pairs // 2) as it:
                for s in range(U + 3):
                    if s < U:
                        scores(it, s)
                    if 0 <= s - 1 < U:
                        turns(it, s - 1)
                    if 0 <= s - 2 < U:
                        values(it, s - 2)
                    if 0 <= s - 3 < U:
                        turn_out(it, s - 3)

        @block.vector
        def _(dve):
            def logit(it, u):
                b, i, hd = all_units[u]
                waits = [(dots_ready, U * it + u + 1)]
                if mask is not None:
                    waits.append((extra_ready, U * it + u + 1))
                    add = extra[u % 2][:, 0:keys[i]]
                else:
                    if u % units == 0:
                        waits.append((band_masked[b], 2 * it + 2))
                    add = bias[b][:, hd, width - keys[i]:width]
                wait_apart(dve, *waits, (turned[0], U * it + max(u - 1, 0)),
                           (turned[1], seconds * it + sum(second[:max(u - 1, 0)])))
                dve.tensor_tensor_reduce(prob[u % 2][:, 0:keys[i]], dots[u % 2][:, 0:keys[i]], add, 1.0, -3.0e38,
                                         ALU.add, ALU.max, top[:, u:u + 1]).then_inc(logits, 1)
                dve.wait_ge(logits, after(U * it + u + 1))
                dve.tensor_scalar(ntop[:, u:u + 1], top[:, u:u + 1], -DH ** -0.5, None, ALU.mult).then_inc(ntop_ready, 1)

            def copy(it, u):
                b, i, hd = all_units[u]
                n = min(keys[i], 512)
                dve.wait_ge(turned[0], after(U * it + u + 1))
                if u >= 2:
                    bb = all_units[u - 2][0]
                    dve.wait_ge(out_ready[bb], after(units * it + (u - 2) % units + 1))
                else:
                    dve.wait_ge(out_ready[1], after(units * it))
                dve.tensor_copy(probT[u % 2][:, 0:n], turn[0][:, 0:n]).then_inc(probT_ready[0], 1)

            def norm(it, u):
                b, i, hd = all_units[u]
                dve.wait_ge(prob_ready, after(U * it + u + 1))
                dve.reciprocal(inv[:, u:u + 1], total[:, u:u + 1]).then_inc(inv_ready, 1)
                dve.wait_ge(inv_ready, after(U * it + u + 1))
                dve.wait_ge(out_ready[b], after(units * it + u % units + 1))
                dve.wait_ge(oT_ready, after(U // 2 * it + max(u // 2 - 1, 0)))
                at = P * (i % 2) + DH * hd
                dve.tensor_scalar(o[i % 2][:, DH * hd:DH * hd + DH], ops[:, at:at + DH], inv[:, u:u + 1], None,
                                  ALU.mult).then_inc(o_ready, 1)

            with dve.Fori(0, pairs // 2) as it:
                for s in range(U + 2):
                    if s < U:
                        logit(it, s)
                    if 0 <= s - 1 < U:
                        copy(it, s - 1)
                    if 0 <= s - 2 < U:
                        norm(it, s - 2)

        @block.scalar
        def _(act):
            def exp(it, u):
                b, i, hd = all_units[u]
                act.wait_ge(ntop_ready, after(U * it + u + 1))
                act.activation(prob[u % 2][:, 0:keys[i]], prob[u % 2][:, 0:keys[i]], ACT.Exp, bias=ntop[:, u:u + 1],
                               scale=DH ** -0.5, accum_out=total[:, u:u + 1]).then_inc(prob_ready, 1)

            def copy(it, u):
                b, i, hd = all_units[u]
                if second[u]:
                    act.wait_ge(turned[1], after(seconds * it + sum(second[:u + 1])))
                    if u >= 2:
                        bb = all_units[u - 2][0]
                        act.wait_ge(out_ready[bb], after(units * it + (u - 2) % units + 1))
                    else:
                        act.wait_ge(out_ready[1], after(units * it))
                    act.activation(probT[u % 2][:, 512:keys[i]], turn[1][:, 0:keys[i] - 512], ACT.Copy
                                   ).then_inc(probT_ready[1], 1)

            def out(it, u):
                b, i, hd = all_units[u]
                if hd == 0:
                    return
                act.wait_ge(oT_ready, after(U // 2 * it + u // 2 + 1))
                if i == 0:
                    act.wait_ge(stored[b], after(16 * it))
                act.activation(oT[b][:, P * i:P * i + P], oTps[:, 0:P], ACT.Copy).then_inc(oT_copied[b], 1)
                if i == TILES - 1:
                    act.wait_ge(oT_copied[b], after(TILES * it + TILES))
                    act.dma_start(mix[2 * it + b][:, 0:T], oT[b][:]).then_inc(stored[b], 16)

            with act.Fori(0, pairs // 2) as it:
                for s in range(U + 3):
                    if s < U:
                        exp(it, s)
                    if 0 <= s - 1 < U:
                        copy(it, s - 1)
                    if 0 <= s - 3 < U:
                        out(it, s - 3)
            for b in range(2):
                act.wait_ge(stored[b], after(16 * (pairs // 2)))


def sample_attention_phase(nc, name, io, z, q0, k0, vt, v0, k_past, v_past, past, skew, length, shift, heads, mask_dram,
                           ident, mix):
    groups = heads // 4
    keys = past + S
    blocks = past // P + 1
    pieces = [(lo, min(lo + 1024, keys)) for lo in range(0, keys, 1024)]
    quads = [(lo, min(lo + 4, blocks)) for lo in range(0, blocks, 4)]
    with Tools(nc) as m:
        q = [m.sb(f"{name}_q{b}", [P, 2, S]) for b in range(2)]
        k = [m.sb(f"{name}_k{b}", [P, 2, keys]) for b in range(2)]
        v = [m.sb(f"{name}_v{b}", [P, blocks, 256]) for b in range(2)]
        bias = [m.sb(f"{name}_bias{b}", [P, keys]) for b in range(2)]
        mask = m.sb(f"{name}_mask", [P, keys]) if mask_dram is not None else None
        prob = m.sb(f"{name}_prob", [P, keys])
        probT = m.sb(f"{name}_probT", [P, blocks, P])
        top = m.sb(f"{name}_max", [P, 8])
        total, inv = m.sb(f"{name}_sum", [P, 1]), m.sb(f"{name}_inv", [P, 1])
        o, oT = m.sb(f"{name}_o", [P, DH]), m.sb(f"{name}_oT", [DH, P])
        dots = [m.ps(f"{name}_dots{a}", [P, 1024]) for a in range(2)]
        turn = [m.ps(f"{name}_turn{a}", [P, 512]) for a in range(2)]
        ops, oTps = m.ps(f"{name}_out", [P, 512]), m.ps(f"{name}_outT", [P, 512])
        loaded = [m.sem(f"{name}_in{b}") for b in range(2)]
        mask_in, bias_ready = m.sem(f"{name}_mask_in"), m.sem(f"{name}_bias")
        dots_ready, logits, top_ready, ntop_ready, prob_ready = (
            m.sem(f"{name}_{x}") for x in ("dots", "logits", "top", "ntop", "prob"))
        turned, probT_ready, out_ready, inv_ready, o_ready, oT_ready, oT_copied, stored = (
            m.sem(f"{name}_{x}") for x in ("turned", "probT", "out", "inv", "o", "oT", "oT_copied", "stored"))
        block = m.block()

        @block.sync
        def _(sp):
            if mask is not None:
                for j in range(4):
                    sp.dma_start(mask[S * j:S * j + S, :], mask_dram).then_inc(mask_in, 16)
            for g in range(groups):
                b = g % 2
                if g >= 2:
                    sp.wait_ge(out_ready, after(g - 1))
                sp.dma_start(q[b][:], z[q0 + 2 * g:q0 + 2 * g + 2, :, T:N].rearrange("c p n -> p c n")
                             ).then_inc(loaded[b], 16)
                sp.dma_start(k[b][:, :, 0:past], k_past[2 * g:2 * g + 2].rearrange("c p n -> p c n")
                             ).then_inc(loaded[b], 16)
                sp.dma_start(k[b][:, :, past:keys], z[k0 + 2 * g:k0 + 2 * g + 2, :, T:N].rearrange("c p n -> p c n")
                             ).then_inc(loaded[b], 16)
                for j in range(4):
                    sp.dma_start(bias[b][S * j:S * j + S, :], shifted(skew[4 * g + j:4 * g + j + 1], S, length, shift, keys)
                                 .rearrange("p h n -> p (h n)")).then_inc(loaded[b], 16)
                sp.dma_start(v[b][:, 0:blocks - 1, :], v_past[:, 256 * g:256 * g + 256]
                             .rearrange("(i p) n -> p i n", p=P)).then_inc(loaded[b], 16)
                sp.dma_start(v[b][0:S, blocks - 1, :], vt[T:N, v0 + 256 * g:v0 + 256 * g + 256]
                             ).then_inc(loaded[b], 16)

        IN = 16 * 9

        @block.gpsimd
        def _(pool):
            if mask is not None:
                pool.wait_ge(mask_in, after(64))
                for g in range(groups):
                    b = g % 2
                    pool.wait_ge(loaded[b], after(IN * (g // 2 + 1)))
                    pool.tensor_tensor(bias[b][:], bias[b][:], mask[:], ALU.add).then_inc(bias_ready, 1)

        @block.tensor
        def _(pe):
            n_dots = n_turn = 0
            for g in range(groups):
                b = g % 2
                pe.wait_ge(loaded[b], after(IN * (g // 2 + 1)))
                for lo, hi in pieces:
                    if n_dots >= 2:
                        pe.wait_ge(logits, after(n_dots - 1))
                    for j in range(4):
                        half = slice(DH * (j % 2), DH * (j % 2) + DH)
                        for c in range(lo, hi, 512):
                            e = min(c + 512, hi)
                            last = pe.matmul(dots[n_dots % 2][S * j:S * j + S, c - lo:e - lo], q[b][half, j // 2, :],
                                             k[b][half, j // 2, c:e], start=True, stop=True)
                    last.then_inc(dots_ready, 1)
                    n_dots += 1
                pe.wait_ge(prob_ready, after(g + 1))
                for lo, hi in quads:
                    if n_turn >= 2:
                        pe.wait_ge(probT_ready, after(n_turn - 1))
                    for c in range(lo, hi):
                        n = P if c < blocks - 1 else S
                        last = pe.transpose(turn[n_turn % 2][0:n, P * (c - lo):P * (c - lo) + P],
                                            prob[:, P * c:P * c + n], ident[:])
                    last.then_inc(turned, 1)
                    n_turn += 1
                pe.wait_ge(probT_ready, after(n_turn))
                if g >= 1:
                    pe.wait_ge(o_ready, after(g))
                for j in range(4):
                    for c in range(blocks):
                        n = P if c < blocks - 1 else S
                        last = pe.matmul(ops[S * j:S * j + S, 0:DH], probT[0:n, c, S * j:S * j + S],
                                         v[b][0:n, c, DH * j:DH * j + DH], start=c == 0, stop=c == blocks - 1)
                last.then_inc(out_ready, 1)
                pe.wait_ge(o_ready, after(g + 1))
                if g >= 1:
                    pe.wait_ge(oT_copied, after(g))
                pe.transpose(oTps[0:DH, 0:P], o[:], ident[:]).then_inc(oT_ready, 1)

        @block.vector
        def _(dve):
            n_dots = n_turn = 0
            for g in range(groups):
                b = g % 2
                if mask is not None:
                    dve.wait_ge(bias_ready, after(g + 1))
                else:
                    dve.wait_ge(loaded[b], after(IN * (g // 2 + 1)))
                if g >= 1:
                    dve.wait_ge(turned, after(len(quads) * g))
                for c, (lo, hi) in enumerate(pieces):
                    n_dots += 1
                    dve.wait_ge(dots_ready, after(n_dots))
                    dve.tensor_tensor_reduce(prob[:, lo:hi], dots[(n_dots - 1) % 2][:, 0:hi - lo], bias[b][:, lo:hi],
                                             1.0, -3.0e38, ALU.add, ALU.max, top[:, c:c + 1]).then_inc(logits, 1)
                dve.wait_ge(logits, after(n_dots))
                dve.tensor_reduce(top[:, 4:5], top[:, 0:len(pieces)], AX_X, ALU.max).then_inc(top_ready, 1)
                dve.wait_ge(top_ready, after(g + 1))
                dve.tensor_scalar(top[:, 5:6], top[:, 4:5], -DH ** -0.5, None, ALU.mult).then_inc(ntop_ready, 1)
                if g >= 1:
                    dve.wait_ge(out_ready, after(g))
                for lo, hi in quads:
                    n_turn += 1
                    dve.wait_ge(turned, after(n_turn))
                    full = min(hi, blocks - 1)
                    bank = turn[(n_turn - 1) % 2]
                    if full > lo:
                        last = dve.tensor_copy(probT[:, lo:full, :], bank[:, 0:P * (full - lo)]
                                               .rearrange("p (c n) -> p c n", n=P))
                    if hi == blocks:
                        last = dve.tensor_copy(probT[0:S, blocks - 1, :], bank[0:S, P * (full - lo):P * (full - lo) + P])
                    last.then_inc(probT_ready, 1)
                dve.wait_ge(prob_ready, after(g + 1))
                dve.reciprocal(inv[:], total[:]).then_inc(inv_ready, 1)
                dve.wait_ge(inv_ready, after(g + 1))
                dve.wait_ge(out_ready, after(g + 1))
                if g >= 1:
                    dve.wait_ge(oT_ready, after(g))
                dve.tensor_scalar(o[:], ops[:, 0:DH], inv[:], None, ALU.mult).then_inc(o_ready, 1)

        @block.scalar
        def _(act):
            for g in range(groups):
                act.wait_ge(ntop_ready, after(g + 1))
                if g >= 1:
                    act.wait_ge(inv_ready, after(g))
                act.activation(prob[:], prob[:], ACT.Exp, bias=top[:, 5:6], scale=DH ** -0.5,
                               accum_out=total[:]).then_inc(prob_ready, 1)
                act.wait_ge(oT_ready, after(g + 1))
                if g >= 1:
                    act.wait_ge(stored, after(64 * g))
                act.activation(oT[:], oTps[0:DH, 0:P], ACT.Copy).then_inc(oT_copied, 1)
                act.wait_ge(oT_copied, after(g + 1))
                for j in range(4):
                    act.dma_start(mix[2 * g + j // 2, DH * (j % 2):DH * (j % 2) + DH, T:N], oT[:, S * j:S * j + S]
                                  ).then_inc(stored, 16)
            act.wait_ge(stored, after(64 * groups))
LEVELS = 7


def recurrence_phase(nc, io, ident, o):
    TP = (TILES + 1) * P
    W = HB * P
    ALL = LEVELS + 2
    TO_END, FROM_START = LEVELS, LEVELS + 1
    with Tools(nc) as m:
        raw = m.sb("hg_raw", [P, HB, N])
        q = m.sb("hg_q", [P, HB, TP])
        k = m.sb("hg_k", [P, HB, TP])
        g = m.sb("hg_g", [P, HB, TP])
        v = m.sb("hg_v", [P, TILES + 1, W])
        lb2 = m.sb("hg_lb2", [P, 2, HB])
        lbt = m.sb("hg_lbt", [P, 4, HB])
        masks = m.sb("hg_masks", [P, LEVELS + 1, P])
        one = m.sb("hg_one", [P, P])
        kept = m.sb("hg_kept", [P, HB, P])
        dec = m.sb("hg_decayed", [P, ALL, W])
        last_decay = m.sb("hg_last_decay", [P, HB])
        att = m.sb("hg_att", [P, LEVELS + 1, P])
        attT = [m.sb(f"hg_attT{a}", [P, P]) for a in range(2)]
        kT = m.sb("hg_kT", [P, W])
        state = m.sb("hg_state", [P, HB, P])
        pairs = [m.ps(f"hg_pairs{a}", [P, 1024]) for a in range(2)]
        kTps, dS, ops = m.ps("hg_kTps", [P, 512]), m.ps("hg_dS", [P, 512]), [m.ps(f"hg_ops{a}", [P, 512]) for a in range(2)]
        small_in, f_in, q_in, v_in = m.sem("hg_small_in"), m.sem("hg_f_in"), m.sem("hg_q_in"), m.sem("hg_v_in")
        lb_steps, f_sig, f_done, g_done, q_done, k_done = (m.sem(f"hg_{x}") for x in ("lb", "sig", "f", "g", "q", "k"))
        setup_done = m.sem("hg_setup")
        summed, diffs, decays, decayed, kept_s = (m.sem(f"hg_{x}") for x in ("summed", "diffs", "decays", "decayed", "kept"))
        pairs_ready, masked, attT_ready, kT_turned, kT_ready = (
            m.sem(f"hg_{x}") for x in ("pairs", "masked", "attT", "kT_turned", "kT_copied"))
        out_ready, out_copied, dS_ready, state_ready, state_io = (
            m.sem(f"hg_{x}") for x in ("out", "out_copied", "dS", "state", "state_io"))
        decayed_v, last_ready = m.sem("hg_decayed_levels"), m.sem("hg_last_decay_ready")
        block = m.block()

        def tiles(eng, body):
            with eng.Fori(0, TILES) as c:
                body(c, False)
            body(TILES, True)

        @block.sync
        def _(sp):
            sp.dma_start(lb2[:], io["lb"]).then_inc(small_in, 16)
            sp.dma_start(masks[:], io["hg_masks"]).then_inc(small_in, 16)
            sp.dma_start(raw[:], io["z0"][FB:FB + HB].rearrange("c p n -> p c n")).then_inc(f_in, 16)
            sp.dma_start(q[:, :, 0:N], io["z0"][QB:QB + HB].rearrange("c p n -> p c n")).then_inc(q_in, 16)
            sp.dma_start(v[:, 0:TILES, :], io["zt0"][0:T, 512:1024].rearrange("(i p) n -> p i n", p=P)).then_inc(v_in, 16)
            sp.wait_ge(setup_done, after(1))
            sp.dma_start(v[0:S, TILES, :], io["zt0"][T:N, 512:1024]).then_inc(v_in, 16)
            sp.wait_ge(state_ready, after(HB * TILES))
            sp.dma_start(io["state_p"].rearrange("h k v -> k h v"), state[:]).then_inc(state_io, 16)
            sp.wait_ge(state_io, after(16))
            sp.wait_ge(out_ready, after(HB * TILES))
            sp.dma_start(state[:], io["state_in"].rearrange("h k v -> k h v")).then_inc(state_io, 16)
            sp.wait_ge(state_ready, after(HB * (TILES + 1)))
            sp.dma_start(io["state_s"].rearrange("h k v -> k h v"), state[:]).then_inc(state_io, 16)
            sp.wait_ge(state_io, after(48))

        @block.scalar
        def _(act):
            act.wait_ge(q_in, after(16))
            act.activation(q[:, :, 0:N], q[:, :, 0:N], ACT.Silu).then_inc(q_done, 1)
            act.wait_ge(f_in, after(16))
            act.activation(raw[:], raw[:], ACT.Sigmoid).then_inc(f_sig, 1)
            act.wait_ge(lb_steps, after(2))
            act.activation(lbt[:, 1:3, :], lb2[:], ACT.Exp).then_inc(lb_steps, 1)
            act.wait_ge(f_done, after(HB))
            act.activation(g[:, :, 0:N], raw[:], ACT.Ln).then_inc(g_done, 1)

            def body(c, sample):
                act.wait_ge(diffs, after(c + 1))
                act.activation(dec[:], dec[:], ACT.Exp).then_inc(decays, 1)
                act.wait_ge(kT_turned, after(c + 1))
                act.wait_ge(dS_ready, after(HB * c))
                act.activation(kT[:], kTps[:], ACT.Copy).then_inc(kT_ready, 1)
                for hd in range(HB):
                    act.wait_ge(out_ready, after(HB * c + hd + 1))
                    act.activation(o[:, bass.ds(c, 1), P * hd:P * hd + P], ops[hd % 2][:, 0:P].unsqueeze(1), ACT.Copy
                                   ).then_inc(out_copied, 1)
            tiles(act, body)

        @block.gpsimd
        def _(pool):
            pool.memset(one[:], 1.0)
            pool.memset(v[:, TILES, :], 0.0)
            pool.memset(q[:, :, N:TP], 0.0)
            pool.memset(k[:, :, N:TP], 0.0)
            pool.memset(g[:, :, N:TP], 0.0)
            pool.memset(state[:], 0.0).then_inc(setup_done, 1)

            def body(c, sample):
                qv, kv = q[:, :, bass.ds(c * P, P)], k[:, :, bass.ds(c * P, P)]
                pool.wait_ge(decays, after(c + 1))
                pool.wait_ge(out_ready, after(HB * c))
                pool.tensor_copy(kept[:], kv).then_inc(kept_s, 1)
                pool.tensor_tensor(dec[:, TO_END, :].rearrange("p (h n) -> p h n", h=HB),
                                   dec[:, TO_END, :].rearrange("p (h n) -> p h n", h=HB), kv, ALU.mult).then_inc(decayed, 1)
                pool.wait_ge(last_ready, after(c + 1))
                pool.tensor_tensor(dec[:, FROM_START, :].rearrange("p (h n) -> p h n", h=HB),
                                   dec[:, FROM_START, :].rearrange("p (h n) -> p h n", h=HB), qv, ALU.mult).then_inc(decayed, 1)
            pool.wait_ge(k_done, after(HB))
            pool.wait_ge(q_done, after(1))
            tiles(pool, body)

        def halves(view, level, side):
            return view.rearrange("p (b s m) -> p b s m", s=2, m=1 << level)[:, :, side, :]

        @block.vector
        def _(dve):
            dve.wait_ge(small_in, after(32))
            dve.tensor_tensor(lbt[:, 0, :], lb2[:, 0, :], lb2[:, 1, :], ALU.max).then_inc(lb_steps, 1)
            dve.wait_ge(lb_steps, after(1))
            dve.tensor_tensor(lb2[:], lb2[:], lbt[:, 0, :].unsqueeze(1).to_broadcast([P, 2, HB]), ALU.subtract
                              ).then_inc(lb_steps, 1)
            dve.wait_ge(lb_steps, after(3))
            dve.tensor_tensor(lbt[:, 3, :], lbt[:, 1, :], lbt[:, 2, :], ALU.add).then_inc(lb_steps, 1)
            dve.wait_ge(lb_steps, after(4))
            dve.reciprocal(lbt[:, 0, :], lbt[:, 3, :]).then_inc(lb_steps, 1)
            dve.wait_ge(lb_steps, after(5))
            dve.tensor_tensor(lbt[:, 1, :], lbt[:, 1, :], lbt[:, 0, :], ALU.mult).then_inc(lb_steps, 1)
            dve.wait_ge(lb_steps, after(6))
            dve.tensor_scalar(lbt[:, 2, :], lbt[:, 1, :], -1.0, 1.0, ALU.mult, ALU.add).then_inc(lb_steps, 1)
            dve.wait_ge(lb_steps, after(7))
            dve.wait_ge(f_sig, after(1))
            for hd in range(HB):
                dve.tensor_scalar(raw[:, hd, :], raw[:, hd, :], lbt[:, 2, hd:hd + 1], lbt[:, 1, hd:hd + 1],
                                  ALU.mult, ALU.add).then_inc(f_done, 1)
            dve.wait_ge(f_done, after(HB))
            for hd in range(HB):
                dve.tensor_scalar(k[:, hd, 0:N], raw[:, hd, :], -1.0, 1.0, ALU.mult, ALU.add).then_inc(k_done, 1)
            dve.wait_ge(setup_done, after(1))
            dve.wait_ge(g_done, after(1))
            dve.wait_ge(k_done, after(HB))
            dve.wait_ge(q_done, after(1))

            def body(c, sample):
                start = dec[:, FROM_START, :]
                dve.wait_ge(out_ready, after(HB * c))
                dve.wait_ge(state_ready, after(HB * c))
                for hd in range(HB):
                    dve.tensor_tensor_scan(dec[:, FROM_START, P * hd:P * hd + P], one[:],
                                           g[:, hd, bass.ds(c * P, P)], 0.0, ALU.mult, ALU.add).then_inc(summed, 1)
                dve.wait_ge(summed, after(HB * (c + 1)))
                for lv in range(LEVELS):
                    half = 1 << lv
                    first, second = halves(start, lv, 0), halves(start, lv, 1)
                    mid = first[:, :, half - 1:half].to_broadcast([P, W // (2 * half), half])
                    dve.tensor_tensor(halves(dec[:, lv, :], lv, 1), second, mid, ALU.subtract)
                    dve.tensor_tensor(halves(dec[:, lv, :], lv, 0), mid, first, ALU.subtract)
                byhead = start.rearrange("p (h n) -> p h n", h=HB)
                end = byhead[:, :, P - 1:P].to_broadcast([P, HB, P])
                dve.tensor_tensor(dec[:, TO_END, :].rearrange("p (h n) -> p h n", h=HB), end, byhead, ALU.subtract
                                  ).then_inc(diffs, 1)
                dve.wait_ge(decays, after(c + 1))
                dve.tensor_copy(last_decay[:].unsqueeze(2), byhead[:, :, P - 1:P]).then_inc(last_ready, 1)
                for lv in range(LEVELS):
                    for side, src in ((0, k), (1, q)):
                        sv = src[:, :, bass.ds(c * P, P)]
                        d4 = dec[:, lv, :].rearrange("p (h b s m) -> p h b s m", h=HB, s=2, m=1 << lv)[:, :, :, side, :]
                        s4 = sv.rearrange("p h (b s m) -> p h b s m", s=2, m=1 << lv)[:, :, :, side, :]
                        last = dve.tensor_tensor(d4, d4, s4, ALU.mult)
                last.then_inc(decayed_v, 1)
                for hd in range(HB):
                    n = HB * c + hd
                    dve.wait_ge(pairs_ready, after(n + 1))
                    dve.wait_ge(attT_ready, after(n))
                    dve.tensor_tensor(att[:], pairs[hd % 2][:].rearrange("p (l n) -> p l n", l=LEVELS + 1), masks[:],
                                      ALU.mult).then_inc(masked, 1)
                    dve.wait_ge(masked, after(n + 1))
                    if hd < 2:
                        dve.wait_ge(out_ready, after(HB * c))
                    else:
                        dve.wait_ge(out_ready, after(HB * c + hd - 1))
                    dve.tensor_reduce(attT[hd % 2][:], att[:].rearrange("p l n -> p n l"), AX_X, ALU.add
                                      ).then_inc(attT_ready, 1)
                    dve.wait_ge(dS_ready, after(n + 1))
                    dve.wait_ge(out_ready, after(n + 1))
                    dve.scalar_tensor_tensor(out=state[:, hd, :], in0=state[:, hd, :], scalar=last_decay[:, hd:hd + 1],
                                             in1=dS[:, P * hd:P * hd + P], op0=ALU.mult, op1=ALU.add).then_inc(state_ready, 1)
            tiles(dve, body)

        @block.tensor
        def _(pe):
            pe.wait_ge(v_in, after(32))
            pe.wait_ge(small_in, after(32))

            def body(c, sample):
                pe.wait_ge(decayed_v, after(c + 1))
                pe.wait_ge(decayed, after(2 * c + 2))
                pe.wait_ge(kept_s, after(c + 1))
                pe.wait_ge(kT_ready, after(c))
                for hd in range(HB):
                    h = slice(P * hd, P * hd + P)
                    last = pe.transpose(kTps[:, h], dec[:, TO_END, h], ident[:])
                last.then_inc(kT_turned, 1)

                def products(hd):
                    n = HB * c + hd
                    h = slice(P * hd, P * hd + P)
                    pe.wait_ge(masked, after(HB * c + max(hd - 1, 0)))
                    for lv in range(LEVELS):
                        pe.matmul(pairs[hd % 2][:, P * lv:P * lv + P], dec[:, lv, h], dec[:, lv, h], start=True, stop=True)
                    pe.matmul(pairs[hd % 2][:, P * LEVELS:], kept[:, hd, :], q[:, hd, bass.ds(c * P, P)],
                              start=True, stop=True).then_inc(pairs_ready, 1)

                products(0)
                for hd in range(HB):
                    if hd + 1 < HB:
                        products(hd + 1)
                    n = HB * c + hd
                    h = slice(P * hd, P * hd + P)
                    pe.wait_ge(kT_ready, after(c + 1))
                    pe.wait_ge(state_ready, after(n))
                    vv = v[:, bass.ds(c, 1), h].rearrange("p c n -> p (c n)")
                    pe.matmul(dS[:, h], kT[:, h], vv, start=True, stop=True).then_inc(dS_ready, 1)
                    pe.wait_ge(attT_ready, after(n + 1))
                    pe.wait_ge(out_copied, after(HB * c + max(hd - 1, 0)))
                    if sample and hd == 0:
                        pe.wait_ge(state_io, after(32))
                    pe.matmul(ops[hd % 2][:, 0:P], attT[hd % 2][:], vv, start=True, stop=False)
                    pe.matmul(ops[hd % 2][:, 0:P], dec[:, FROM_START, h], state[:, hd, :], start=False, stop=True
                              ).then_inc(out_ready, 1)
            tiles(pe, body)


def recurrence_out_phase(nc, io, ident, o, mix):
    TC = TILES + 1
    with Tools(nc) as m:
        gate = m.sb("ho_gate", [P, HB, N])
        gnorm = m.sb("ho_gnorm", [P, HB])
        squares = m.sb("ho_squares", [P, P])
        rstd = m.sb("ho_rstd", [P, TC * HB])
        eps = m.sb("ho_eps", [P, 1])
        out = m.sb("ho_out", [P, HB, N])
        turn = [m.ps(f"ho_turn{a}", [P, 512]) for a in range(2)]
        loaded, gated, eps_set = m.sem("ho_in"), m.sem("ho_gated"), m.sem("ho_eps_set")
        summed, root, inv, normed = (m.sem(f"ho_{x}") for x in ("summed", "root", "inv", "normed"))
        turned, done, stored = (m.sem(f"ho_{x}") for x in ("turned", "done", "stored"))
        units = [(hd, lo, min(lo + 4, TC)) for hd in range(HB) for lo in range(0, TC, 4)]
        block = m.block()

        @block.sync
        def _(sp):
            sp.dma_start(gate[:], io["z0"][GB:GB + HB].rearrange("c p n -> p c n")).then_inc(loaded, 16)
            sp.dma_start(gnorm[:], io["norm_b"]).then_inc(loaded, 16)
            for hd in range(HB):
                sp.wait_ge(done, after(3 * (hd + 1)))
                sp.dma_start(mix[HB + hd], out[:, hd, :]).then_inc(stored, 16)
            sp.wait_ge(stored, after(16 * HB))

        @block.scalar
        def _(act):
            act.wait_ge(loaded, after(32))
            act.activation(gate[:], gate[:], ACT.Silu).then_inc(gated, 1)
            for n in range(TC * HB):
                if n:
                    act.wait_ge(summed, after(n))
                act.activation(squares[:], o[:, n // HB, P * (n % HB):P * (n % HB) + P], ACT.Square,
                               accum_out=rstd[:, n:n + 1]).then_inc(summed, 1)
            act.wait_ge(summed, after(TC * HB))
            act.wait_ge(eps_set, after(1))
            act.activation(rstd[:], rstd[:], ACT.Sqrt, bias=eps[:, 0:1], scale=1.0 / P).then_inc(root, 1)

        @block.vector
        def _(dve):
            dve.memset(eps[:], EPS).then_inc(eps_set, 1)
            dve.wait_ge(root, after(1))
            dve.reciprocal(rstd[:], rstd[:]).then_inc(inv, 1)
            dve.wait_ge(inv, after(1))
            ov = o[:].rearrange("p c (h n) -> p (c h) n", h=HB)
            dve.tensor_tensor(ov, ov, rstd[:].unsqueeze(2).to_broadcast([P, TC * HB, P]), ALU.mult).then_inc(normed, 1)
            dve.wait_ge(loaded, after(32))
            dve.wait_ge(gated, after(1))
            for u, (hd, lo, hi) in enumerate(units):
                cols = slice(P * lo, min(P * hi, N))
                n = cols.stop - cols.start
                dve.wait_ge(turned, after(u + 1))
                dve.scalar_tensor_tensor(out=out[:, hd, cols], in0=turn[u % 2][:, 0:n], scalar=gnorm[:, hd:hd + 1],
                                         in1=gate[:, hd, cols], op0=ALU.mult, op1=ALU.mult).then_inc(done, 1)

        @block.tensor
        def _(pe):
            pe.wait_ge(normed, after(1))
            for u, (hd, lo, hi) in enumerate(units):
                if u >= 2:
                    pe.wait_ge(done, after(u - 1))
                for c in range(lo, hi):
                    last = pe.transpose(turn[u % 2][:, P * (c - lo):P * (c - lo) + P], o[:, c, P * hd:P * hd + P], ident[:])
                last.then_inc(turned, 1)


def even_mixer(nc, io, h, x, ident, mix):
    with Tools(nc) as f:
        loads, products, copies = projection(f, "z0a", io["w0"], 0, Z0_FIRST, h, io["z0"])
        block = f.block()
        block.sync(loads)
        block.tensor(products)
        block.scalar(copies)
    token_major_phase(nc, "tok0", io["wt0"], 2, h, io["zt0"])
    with Tools(nc) as s:
        score = s.sb("score", [P, SAMPLE_AT + SAMPLE_KEYS])
        index_phase(nc, io, score)
        with Tools(nc) as f:
            loads, products, copies = projection(f, "z0b", io["w0"], Z0_FIRST, Z0_CHUNKS - Z0_FIRST, h, io["z0"])
            choose, store = choosing(f, score, io["mask_s"])
            block = f.block()

            @block.sync
            def _(sp):
                loads(sp)
                store(sp)

            block.tensor(products)
            block.scalar(copies)
            block.vector(choose)
        prompt_attention_phase(nc, "pa", io, io["z0"], QA, KA, io["zt0"], 0, io["skew_a"], T, HA, None, score, ident, mix)
    sample_attention_phase(nc, "sa", io, io["z0"], QA, KA, io["zt0"], 0, io["ka_past"], io["va_past"], PAST, io["skew_s"],
                           SKEW_S, S - 1, HA, io["mask_s"], ident, mix)
    with Tools(nc) as s:
        o = s.sb("hg_o", [P, TILES + 1, HB * P])
        recurrence_phase(nc, io, ident, o)
        recurrence_out_phase(nc, io, ident, o, mix)


def odd_mixer(nc, io, h, x, ident, mix):
    with Tools(nc) as f:
        loads, products, copies = projection(f, "z1", io["w1"], 0, Z1_CHUNKS, h, io["z1"])
        block = f.block()
        block.sync(loads)
        block.tensor(products)
        block.scalar(copies)
    token_major_phase(nc, "tok1", io["wt1"], 2, h, io["zt1"])
    prompt_attention_phase(nc, "pc", io, io["z1"], 0, 8, io["zt1"], 0, io["skew_c"], BAND_KEYS, HC, 4, None, ident, mix)
    sample_attention_phase(nc, "sc", io, io["z1"], 0, 8, io["zt1"], 0, io["kc_past"], io["vc_past"], BACK, io["skew_c"],
                           SKEW_C, P - 1, HC, None, ident, mix)


def build_program(nc, io):
    def dram(name, shape):
        io[name] = nc.dram_tensor(f"scratch_{name}", shape, F32, kind="Internal").ap()

    dram("skew_a", [HA, P * SKEW_A])
    dram("skew_s", [HA, S * SKEW_S])
    dram("skew_c", [HC, P * SKEW_C])
    dram("mask_s", [S, SAMPLE_KEYS])
    dram("mix0", [KD, P, N])
    dram("mix1", [KD, P, N])
    with Tools(nc) as m:
        h = m.sb("h", [P, KD, N])
        mod = m.sb("mod", [P, 2, 6, KD, 2])
        cols = m.sb("cols", [P, 4, KD, 2])
        gfin = m.sb("gfin", [P, KD])
        ident = m.sb("ident", [P, P])
        ones = m.sb("ones", [P, P])
        with Tools(nc) as s:
            x = s.sb("x0", [P, KD, N])
            setup_phase(nc, io, x, mod, cols, gfin, ident, ones)
            bias_phase(nc, io)
            norm_phase(nc, "n00", x, h, cols[:, 0], mod[:, 0, 0], ones)
        even_mixer(nc, io, h, None, ident, io["mix0"])
        x = m.sb("x", [P, KD, N])
        with Tools(nc) as s:
            x_in = s.sem("x_back")
            block = s.block()

            @block.sync
            def _(sp):
                sp.dma_start(x[:], io["xT"]).then_inc(x_in, 16)
                sp.wait_ge(x_in, after(16))
        for l in range(2):
            if l == 1:
                norm_phase(nc, "n10", x, h, cols[:, 2], mod[:, 1, 0], ones)
                odd_mixer(nc, io, h, x, ident, io["mix1"])
            residual_phase(nc, f"out{l}", io["w_out"][l], KD, h, x, mod[:, l, 2], io[f"mix{l}"])
            norm_phase(nc, f"n{l}1", x, h, cols[:, 2 * l + 1], mod[:, l, 3], ones)
            with Tools(nc) as f:
                a = f.sb(f"ffn{l}", [P, KF, N])
                ffn_up_phase(nc, f"up{l}", io["w_gate"][l], io["w_up"][l], h, a)
                residual_phase(nc, f"down{l}", io["w_down"][l], KF, a, x, mod[:, l, 5])
        norm_phase(nc, "nf", x, h, gfin, None, ones, store=io["yT"])


def blocks_of(w, k):
    return np.ascontiguousarray(w.reshape(k, P, -1, P).transpose(2, 1, 0, 3))


def wide_blocks_of(w, n):
    return w.reshape(KD, P, n, 512).transpose(2, 1, 0, 3)


def features(a):
    return np.ascontiguousarray(a.T.reshape(KD, P, -1).transpose(1, 0, 2))


def arrays_of(i):
    i = {k: np.asarray(v) for k, v in i.items()}
    w = i["w_in_even"][0]
    qa, ka, va, qi, ki, wi, qb, fb, ib, gb = np.split(w, np.cumsum([512, 512, 512, 512, 64, 8, 512, 512, 512]), axis=1)
    wt0 = np.zeros((3, P, KD, 512), w.dtype)
    wt0[:2] = wide_blocks_of(np.concatenate([va, ib], 1), 2)
    wt0[2, :, :, :HA] = wi.reshape(KD, P, HA).transpose(1, 0, 2)
    w1 = i["w_in_odd"][0]
    return {
        "xT": features(np.concatenate([i["x_prompt"][0], i["x_sample"][0]])),
        "cT": features(np.concatenate([i["c_prompt"], i["c_sample"]])),
        "w_ada": np.ascontiguousarray(i["w_ada"].reshape(2, KD, P, 12, 4, P).transpose(0, 3, 2, 4, 1, 5)
                                      .reshape(24, P, 4, KD, P)),
        "b_ada": np.ascontiguousarray(i["b_ada"].reshape(96, P).T),
        "norms": np.ascontiguousarray(np.stack([i["norm_mix"][0], i["norm_ffn"][0], i["norm_mix"][1],
                                                i["norm_ffn"][1], i["norm_final"]])
                                      .reshape(5, KD, P).transpose(2, 0, 1)),
        "w0": blocks_of(np.concatenate([qa, ka, qi, ki, ki, qb, fb, gb], 1), KD),
        "wt0": wt0,
        "w1": blocks_of(w1[:, :2048], KD),
        "wt1": np.ascontiguousarray(wide_blocks_of(w1[:, 2048:], 2)),
        "w_out": np.stack([blocks_of(i["w_out_even"][0], KD), blocks_of(i["w_out_odd"][0], KD)]),
        "w_gate": np.stack([blocks_of(v, KD) for v in i["w_ffn_gate"]]),
        "w_up": np.stack([blocks_of(v, KD) for v in i["w_ffn_up"]]),
        "w_down": np.stack([blocks_of(v, KF) for v in i["w_ffn_down"]]),
            "t5": i["t5_table"],
        "t5_onehot": t5_onehot(),
        "rel_rev": np.ascontiguousarray(i["rel_table_c"][0].T[:, ::-1]),
        "lb": np.ascontiguousarray(i["lb_logits"].reshape(2, HB, P).transpose(2, 0, 1)),
        "norm_b": np.ascontiguousarray(i["norm_b_out"][0].reshape(HB, P).T),
        "hg_masks": halving_masks(),
        "state_in": i["state_b"][0, 0],
        "ki_past": np.ascontiguousarray(np.concatenate([i["cache_a_kidx"][0, 0].T] * 2)),
        "ka_past": np.ascontiguousarray(i["cache_a_k"][0, 0].reshape(PAST, 4, P).transpose(1, 2, 0)),
        "va_past": i["cache_a_v"][0, 0].reshape(PAST, HA * DH),
        "kc_past": np.ascontiguousarray(i["cache_c_k"][0, 0].reshape(BACK, 8, P).transpose(1, 2, 0)),
        "vc_past": i["cache_c_v"][0, 0].reshape(BACK, HC * DH),
    }


def t5_onehot():
    rel = np.arange(T5_LEN) - (PAST + S - 1)
    n = np.abs(rel)
    large = 8 + (np.log(np.maximum(n, 1).astype(np.float32) / 8) / np.log(1024 / 8) * 8).astype(np.int32)
    bucket = np.where(rel > 0, 16, 0) + np.where(n < 8, n, np.minimum(large, 15))
    return (np.arange(32)[:, None] == bucket[None, :]).astype(np.float32)


def halving_masks():
    s, t = np.arange(P)[:, None], np.arange(P)[None, :]
    out = [(s >> lv + 1 == t >> lv + 1) & (s >> lv & 1 == 0) & (t >> lv & 1 == 1) for lv in range(LEVELS)]
    return np.ascontiguousarray(np.stack(out + [s == t], 1).astype(np.float32))


_OUTS = [("z0", (Z0_CHUNKS, P, N)), ("zt0", (N, 1024 + HA)), ("z1", (Z1_CHUNKS, P, N)), ("zt1", (N, 1024)),
         ("state_p", (HB, P, P)), ("state_s", (HB, P, P)), ("yT", (P, KD, N))]


def kernel(**inputs):
    import concourse.bacc as _bacc
    from concourse.bass_utils import run_bass_kernel_spmd as _run

    nc = _bacc.Bacc("TRN2", target_bir_lowering=False, num_devices=1)
    arrays, io = {}, {}
    for name, a in arrays_of(inputs).items():
        arrays[f"in_{name}_dram"] = a = np.ascontiguousarray(a)
        io[name] = nc.dram_tensor(f"in_{name}_dram", a.shape, mybir.dt.from_np(a.dtype), kind="ExternalInput").ap()
    for name, shape in _OUTS:
        io[name] = nc.dram_tensor(f"out_{name}_dram", shape, F32, kind="ExternalOutput").ap()
    build_program(nc, io)
    r = _run(nc, [arrays], core_ids=[0]).results[0]
    r = {name: r[f"out_{name}_dram"] for name, _ in _OUTS}

    def rows(z):
        return z.reshape(-1, N).T

    y = r["yT"].transpose(2, 1, 0).reshape(N, D)
    ka, kidx, kc = rows(r["z0"][KA:KA + 4]), rows(r["z0"][KI])[:, :DH], rows(r["z1"][8:16])
    va, vc = r["zt0"][:, :512], r["zt1"]

    def out(a, lo, hi, *shape):
        return np.ascontiguousarray(a[lo:hi]).reshape(shape)

    return (out(y, 0, T, 1, T, D), out(y, T, N, 1, S, D),
            out(ka, 0, T, 1, 1, T, HA, DH), out(va, 0, T, 1, 1, T, HA, DH), out(kidx, 0, T, 1, 1, T, DH),
            r["state_p"].reshape(1, 1, HB, P, P),
            out(kc, T - BACK, T, 1, 1, BACK, HC, DH), out(vc, T - BACK, T, 1, 1, BACK, HC, DH),
            out(ka, T, N, 1, 1, S, HA, DH), out(va, T, N, 1, 1, S, HA, DH), out(kidx, T, N, 1, 1, S, DH),
            r["state_s"].reshape(1, 1, HB, P, P),
            out(kc, T, N, 1, 1, S, HC, DH), out(vc, T, N, 1, 1, S, HC, DH))
```

```python
from contextlib import ExitStack

import numpy as np

import concourse.bass as bass
from concourse import mybir

F32 = mybir.dt.float32
ACT = mybir.ActivationFunctionType
ALU = mybir.AluOpType
AX_X = mybir.AxisListType.X

P = 128
D = 1024
KD = D // P
T = 1024
S = 32
N = T + S
PAST = 2048
EPS = 1e-6
DH = 64
HA = 8
HC = 16
HB = 4
KTOP = 256
FF = 2816
KF = FF // P
CHUNK = 64
BACK = 8 * CHUNK
TILES = T // P
THIRD = N // 3
THIRDS = [(t * THIRD, (t + 1) * THIRD) for t in range(3)]
SPANS = [(0, THIRD, 0), (THIRD, 2 * THIRD, 0), (2 * THIRD, T, 0), (T, N, 1)]
MASKED = -1e30
OUT_OF_REACH = -3.0e38
TAKEN = -3.4e38
QA, KA, QI, KI, QB, FB, GB, Z0_CHUNKS = 0, 4, 8, 12, 13, 17, 21, 25
Z0_FIRST = 13
Z1_CHUNKS = 16
T5_LEN = PAST + S - 1 + P
BAND_KEYS = BACK + P
REL = 128
BAND_LEN = 768
SKEW_A, SKEW_C, SKEW_S = T + P - 1, BAND_KEYS + P - 1, PAST + S + S - 1


class Tools:

    def __init__(self, nc):
        self.nc, self.stack, self.sems = nc, ExitStack(), []

    def sb(self, name, shape, dt=F32):
        return self.stack.enter_context(self.nc.sbuf_tensor(name, shape, dt))

    def ps(self, name, shape, dt=F32):
        return self.stack.enter_context(self.nc.psum_tensor(name, shape, dt))

    def sem(self, name):
        self.sems.append(self.nc.alloc_semaphore(name))
        return self.sems[-1]

    def block(self):
        for sem in self.sems:
            self.nc.gpsimd.sem_inc(sem, START)
        self.nc.all_engine_barrier()
        return self.stack.enter_context(self.nc.Block())

    def __enter__(self):
        self.stack.__enter__()
        return self

    def __exit__(self, *a):
        self.stack.__exit__(*a)
        if self.sems:
            self.nc.clear_and_free_semaphores(self.sems)


START = 1


def after(count):
    return START + count


def wait_apart(eng, *waits):
    for _, count in waits:
        if not isinstance(count, int):
            eng.to_reg(after(count))
    eng.wait_ge(waits[0][0], after(0))
    for sem, count in waits:
        eng.wait_ge(sem, after(count))


ADA_GROUP = 4
ADA_GROUPS = 2 * 6 * KD // ADA_GROUP
ADA_FIRST = 2 * KD // ADA_GROUP


def modulation(m, name, w_dram, silu_c, b_ada, mod):
    w = [m.sb(f"{name}_w{b}", [P, ADA_GROUP, KD, P]) for b in range(2)]
    acc = [m.ps(f"{name}_acc{b}", [P, 512]) for b in range(2)]
    w_in = [m.sem(f"{name}_w_in{b}") for b in range(2)]
    acc_ready = [m.sem(f"{name}_acc{b}") for b in range(2)]
    acc_read = [m.sem(f"{name}_acc_read{b}") for b in range(2)]
    modf = mod[:].rearrange("p l j k s -> p (l j k) s")

    def load(sp, g, b, n):
        sp.wait_ge(acc_ready[b], after(n))
        sp.dma_start(w[b][:], w_dram[g]).then_inc(w_in[b], 16)

    def products(pe, b, n):
        pe.wait_ge(w_in[b], after(16 * n + 16))
        pe.wait_ge(acc_read[b], after(n))
        for c in range(ADA_GROUP):
            for k in range(KD):
                last = pe.matmul(acc[b][:, 2 * c:2 * c + 2], w[b][:, c, k, :], silu_c[:, k, :],
                                 start=k == 0, stop=k == KD - 1)
        last.then_inc(acc_ready[b], 1)

    def add(act, g, b, n):
        act.wait_ge(acc_ready[b], after(n + 1))
        for c in range(ADA_GROUP):
            at = g * ADA_GROUP + c
            last = act.activation(modf[:, bass.ds(at, 1), :], acc[b][:, 2 * c:2 * c + 2].unsqueeze(1), ACT.Identity,
                                  bias=b_ada[:, bass.ds(at, 1)])
        last.then_inc(acc_read[b], 1)

    return load, products, add, acc_read


def gain_columns(dve, which, mod, norms, gains, step):
    for n in which:
        dve.tensor_scalar(gains[:, n], mod[:, n // 2, 3 * (n % 2) + 1], 1.0, None, ALU.add).then_inc(step, 1)
    dve.wait_ge(step, after(len(which)))
    for n in which:
        dve.tensor_tensor(gains[:, n], gains[:, n], norms[:, n].unsqueeze(2).to_broadcast([P, KD, 2]), ALU.mult)


def setup_phase(nc, io, x, consts):
    c = consts
    with Tools(nc) as m:
        small_in, x_in, silu_ready = m.sem("small_in"), m.sem("x_in"), m.sem("silu_c_ready")
        ident_zero, gain_step = m.sem("ident_zero"), m.sem("gain_step")
        load, products, add, acc_read = modulation(m, "ada0", io["w_ada"], c.silu_c, c.b_ada, c.mod)
        block = m.block()

        @block.sync
        def _(sp):
            for g in range(ADA_FIRST):
                load(sp, g, g % 2, g // 2)

        @block.gpsimd
        def _(pool):
            pool.memset(c.ones[:], 1.0)
            pool.memset(c.ident[:], 0.0).then_inc(ident_zero, 1)
            pool.wait_ge(ident_zero, after(1))
            pool.affine_select(out=c.ident[:], in_=c.ident[:], compare_op=ALU.not_equal, fill=1.0,
                               base=0, pattern=[[-1, P]], channel_multiplier=1)

        @block.scalar
        def _(act):
            act.dma_start(c.silu_c[:], io["cT"]).then_inc(small_in, 16)
            act.dma_start(c.b_ada[:], io["b_ada"]).then_inc(small_in, 16)
            act.dma_start(c.norms[:], io["norms"]).then_inc(small_in, 16)
            act.dma_start(x[:], io["xT"]).then_inc(x_in, 16)
            act.wait_ge(small_in, after(48))
            act.activation(c.silu_c[:], c.silu_c[:], ACT.Silu).then_inc(silu_ready, 1)
            for g in range(ADA_FIRST):
                add(act, g, g % 2, g // 2)
            act.wait_ge(x_in, after(16))

        @block.tensor
        def _(pe):
            pe.wait_ge(silu_ready, after(1))
            for g in range(ADA_FIRST):
                products(pe, g % 2, g // 2)

        @block.vector
        def _(dve):
            for b in range(2):
                dve.wait_ge(acc_read[b], after(ADA_FIRST // 2))
            gain_columns(dve, (0,), c.mod, c.norms, c.gains, gain_step)


def norm_phase(nc, name, x, out, gain, shift, ones, store=None):
    with Tools(nc) as m:
        sq = [m.sb(f"{name}_sq{b}", [P, THIRD]) for b in range(4)]
        rstd = m.sb(f"{name}_rstd", [P, N])
        eps = m.sb(f"{name}_eps", [P, 1])
        ssq = [m.ps(f"{name}_ssq{t}", [P, 512]) for t in range(3)]
        eps_set = m.sem(f"{name}_eps")
        sq_ready = [m.sem(f"{name}_sq{a}") for a in range(2)]
        summed = m.sem(f"{name}_summed")
        root, rstd_ready = m.sem(f"{name}_root"), m.sem(f"{name}_rstd")
        scaled, done = m.sem(f"{name}_scaled"), m.sem(f"{name}_stored")
        block = m.block()

        def square(eng, t, k):
            n = KD * t + k
            if n >= 4:
                eng.wait_ge(summed, after(n - 3))
            lo, hi = THIRDS[t]
            if k % 2 == 0:
                eng.activation(sq[n % 4][:], x[:, k, lo:hi], ACT.Square).then_inc(sq_ready[0], 1)
            else:
                eng.tensor_tensor(sq[n % 4][:], x[:, k, lo:hi], x[:, k, lo:hi], ALU.mult).then_inc(sq_ready[1], 1)

        @block.gpsimd
        def _(pool):
            for t in range(3):
                for k in range(1, KD, 2):
                    square(pool, t, k)

        @block.scalar
        def _(act):
            def add_shift(n):
                if shift is not None:
                    a, b, s = SPANS[n]
                    for k in range(KD):
                        act.wait_ge(scaled, after(KD * n + k + 1))
                        act.activation(out[:, k, a:b], out[:, k, a:b], ACT.Identity, bias=shift[:, k, s:s + 1])

            act.wait_ge(eps_set, after(1))
            for t in range(4):
                if t < 3:
                    for k in range(0, KD, 2):
                        square(act, t, k)
                if t:
                    lo, hi = THIRDS[t - 1]
                    act.wait_ge(summed, after(KD * t))
                    act.activation(rstd[:, lo:hi], ssq[t - 1][:, 0:THIRD], ACT.Sqrt, bias=eps[:, 0:1],
                                   scale=1.0 / D).then_inc(root, 1)
            for n in range(len(SPANS)):
                add_shift(n)

        @block.tensor
        def _(pe):
            for t in range(3):
                for k in range(KD):
                    n = KD * t + k
                    pe.wait_ge(sq_ready[k % 2], after(n // 2 + 1))
                    pe.matmul(ssq[t][:, 0:THIRD], ones[:], sq[n % 4][:], start=k == 0, stop=k == KD - 1
                              ).then_inc(summed, 1)

        @block.vector
        def _(dve):
            dve.memset(eps[:], EPS).then_inc(eps_set, 1)
            for n, (a, b, s) in enumerate(SPANS):
                if n < 3:
                    lo, hi = THIRDS[n]
                    dve.wait_ge(root, after(n + 1))
                    dve.reciprocal(rstd[:, lo:hi], rstd[:, lo:hi]).then_inc(rstd_ready, 1)
                    dve.wait_ge(rstd_ready, after(n + 1))
                for k in range(KD):
                    dve.scalar_tensor_tensor(out=out[:, k, a:b], in0=x[:, k, a:b],
                                             scalar=gain[:, k, s:s + 1] if shift is not None else gain[:, k:k + 1],
                                             in1=rstd[:, a:b], op0=ALU.mult, op1=ALU.mult).then_inc(scaled, 1)

        @block.sync
        def _(sp):
            if store is not None:
                sp.wait_ge(scaled, after(KD * len(SPANS)))
                sp.dma_start(store, out[:]).then_inc(done, 16)
                sp.wait_ge(done, after(16))


def over_chunks(eng, count, body):
    if count >= 2:
        with eng.Fori(0, count // 2) as i:
            for b in range(2):
                body(i, b)
    if count % 2:
        body(count // 2, 0)


def projection(m, name, w_dram, first, count, src, z_dram, beside=None):
    w = [m.sb(f"{name}_w{b}", [P, KD, P]) for b in range(2)]
    stage = [m.sb(f"{name}_stage{b}", [P, N]) for b in range(2)]
    acc = [[m.ps(f"{name}_acc{b}{t}", [P, 512]) for t in range(3)] for b in range(2)]
    w_in = [m.sem(f"{name}_w_in{b}") for b in range(2)]
    acc_ready = [m.sem(f"{name}_acc{b}") for b in range(2)]
    acc_read = [m.sem(f"{name}_acc_read{b}") for b in range(2)]
    stored = [m.sem(f"{name}_stored{b}") for b in range(2)]

    def loads(sp):
        def body(i, b):
            sp.wait_ge(acc_ready[b], after(3 * i))
            sp.dma_start(w[b][:], w_dram[first + 2 * i + b]).then_inc(w_in[b], 16)
            if beside:
                beside[0][0](sp, beside[1] + 2 * i + b, b, i)
        over_chunks(sp, count, body)

    def products(pe):
        def body(i, b):
            pe.wait_ge(w_in[b], after(16 * i + 16))
            for t, (lo, hi) in enumerate(THIRDS):
                pe.wait_ge(acc_read[b], after(3 * i))
                for k in range(KD):
                    last = pe.matmul(acc[b][t][:, 0:THIRD], w[b][:, k, :], src[:, k, lo:hi],
                                     start=k == 0, stop=k == KD - 1)
                last.then_inc(acc_ready[b], 1)
            if beside:
                beside[0][1](pe, b, i)
        over_chunks(pe, count, body)

    def copies(act):
        def body(i, b):
            act.wait_ge(stored[b], after(16 * i))
            for t, (lo, hi) in enumerate(THIRDS):
                act.wait_ge(acc_ready[b], after(3 * i + t + 1))
                act.activation(stage[b][:, lo:hi], acc[b][t][:, 0:THIRD], ACT.Copy).then_inc(acc_read[b], 1)
            act.wait_ge(acc_read[b], after(3 * i + 3))
            act.dma_start(z_dram[first + 2 * i + b], stage[b][:]).then_inc(stored[b], 16)
            if beside:
                beside[0][2](act, beside[1] + 2 * i + b, b, i)
        over_chunks(act, count, body)
        act.wait_ge(stored[0], after(16 * ((count + 1) // 2)))
        if count >= 2:
            act.wait_ge(stored[1], after(16 * (count // 2)))

    return loads, products, copies, acc, acc_read


def token_major(m, name, w_dram, blocks, src, out_dram, acc, beside=None):
    w = [m.sb(f"{name}_w{c}", [P, KD, n]) for c, n in blocks]
    banks = len(acc)
    stage = [m.sb(f"{name}_stage{a}", [P, 512]) for a in range(banks)]
    w_in = [m.sem(f"{name}_w_in{c}") for c, _ in blocks]
    acc_ready, acc_read = m.sem(f"{name}_acc"), m.sem(f"{name}_acc_read")
    stored = [m.sem(f"{name}_stored{a}") for a in range(banks)]
    units = [(j, c, n, lo, min(lo + P, N)) for j, (c, n) in enumerate(blocks) for lo in range(0, N, P)]

    def group(u, step, eng):
        if beside and u % 2 and u // 2 < beside[2]:
            g = u // 2
            args = (eng, g % 2, beside[3] + g // 2) if step == 1 else (eng, beside[1] + g, g % 2, beside[3] + g // 2)
            beside[0][step](*args)

    def weights(sp):
        for j, (c, n) in enumerate(blocks):
            sp.dma_start(w[j][:], w_dram[c][:, :, 0:n]).then_inc(w_in[j], 16)

    def stores(sp):
        for u, (j, c, n, lo, hi) in enumerate(units):
            group(u, 0, sp)
            sp.wait_ge(acc_read, after(u + 1))
            sp.dma_start(out_dram[lo:hi, 512 * c:512 * c + n], stage[u % banks][0:hi - lo, 0:n]
                         ).then_inc(stored[u % banks], 16)
        for a in range(banks):
            sp.wait_ge(stored[a], after(16 * ((len(units) - a + banks - 1) // banks)))

    def products(pe):
        for u, (j, c, n, lo, hi) in enumerate(units):
            if lo == 0:
                pe.wait_ge(w_in[j], after(16))
            if u >= banks:
                pe.wait_ge(acc_read, after(u - banks + 1))
            for k in range(KD):
                last = pe.matmul(acc[u % banks][0:hi - lo, 0:n], src[:, k, lo:hi], w[j][:, k, :],
                                 start=k == 0, stop=k == KD - 1)
            last.then_inc(acc_ready, 1)
            group(u, 1, pe)

    def copies(act):
        for u, (j, c, n, lo, hi) in enumerate(units):
            act.wait_ge(acc_ready, after(u + 1))
            if u >= banks:
                act.wait_ge(stored[u % banks], after(16 * (u // banks)))
            act.activation(stage[u % banks][0:hi - lo, 0:n], acc[u % banks][0:hi - lo, 0:n], ACT.Copy
                           ).then_inc(acc_read, 1)
            group(u, 2, act)

    return weights, stores, products, copies


def residual_phase(nc, name, w_dram, nk, src, x, gate, src_dram=None):
    with Tools(nc) as m:
        w = [m.sb(f"{name}_w{b}", [P, nk, P]) for b in range(2)]
        acc = [[m.ps(f"{name}_acc{b}{t}", [P, 512]) for t in range(3)] for b in range(2)]
        w_in = [m.sem(f"{name}_w_in{b}") for b in range(2)]
        src_in = m.sem(f"{name}_src_in")
        acc_ready = [m.sem(f"{name}_acc{b}") for b in range(2)]
        acc_read = [m.sem(f"{name}_acc_read{b}") for b in range(2)]
        block = m.block()

        @block.sync
        def _(sp):
            with sp.Fori(0, KD // 2) as i:
                for b in range(2):
                    sp.wait_ge(acc_ready[b], after(3 * i))
                    sp.dma_start(w[b][:], w_dram[2 * i + b]).then_inc(w_in[b], 16)

        @block.scalar
        def _(act):
            if src_dram is not None:
                act.dma_start(src[:], src_dram.rearrange("k p n -> p k n")).then_inc(src_in, 16)
                act.wait_ge(src_in, after(16))

        @block.tensor
        def _(pe):
            if src_dram is not None:
                pe.wait_ge(src_in, after(16))
            with pe.Fori(0, KD // 2) as i:
                for b in range(2):
                    pe.wait_ge(w_in[b], after(16 * i + 16))
                    pe.wait_ge(acc_read[b], after(4 * i))
                    for t, (lo, hi) in enumerate(THIRDS):
                        for k in range(nk):
                            last = pe.matmul(acc[b][t][:, 0:THIRD], w[b][:, k, :], src[:, k, lo:hi],
                                             start=k == 0, stop=k == nk - 1)
                        last.then_inc(acc_ready[b], 1)

        @block.vector
        def _(dve):
            with dve.Fori(0, KD // 2) as i:
                for b in range(2):
                    c = 2 * i + b
                    for n, (lo, hi, s) in enumerate(SPANS):
                        t = min(n, 2)
                        dve.wait_ge(acc_ready[b], after(3 * i + t + 1))
                        dve.scalar_tensor_tensor(out=x[:, bass.ds(c, 1), lo:hi],
                                                 in0=acc[b][t][:, lo - t * THIRD:hi - t * THIRD].unsqueeze(1),
                                                 scalar=gate[:, bass.ds(c, 1), s], in1=x[:, bass.ds(c, 1), lo:hi],
                                                 op0=ALU.mult, op1=ALU.add).then_inc(acc_read[b], 1)


def ffn_up_phase(nc, name, wg_dram, wu_dram, src, out):
    with Tools(nc) as m:
        wg = [m.sb(f"{name}_wg{b}", [P, KD, P]) for b in range(2)]
        wu = [m.sb(f"{name}_wu{b}", [P, KD, P]) for b in range(2)]
        gate = [m.ps(f"{name}_gate{t}", [P, 512]) for t in range(3)]
        up = [m.ps(f"{name}_up{t}", [P, 512]) for t in range(3)]
        silu = [m.sb(f"{name}_silu{t}", [P, THIRD]) for t in range(3)]
        w_in = [m.sem(f"{name}_w_in{b}") for b in range(2)]
        acc_ready = [[m.sem(f"{name}_acc{b}{t}") for t in range(3)] for b in range(2)]
        gated = [m.sem(f"{name}_gated{t}") for t in range(3)]
        acc_read = [[m.sem(f"{name}_acc_read{b}{t}") for t in range(3)] for b in range(2)]
        block = m.block()

        @block.sync
        def _(sp):
            with sp.Fori(0, KF // 2) as i:
                for b in range(2):
                    sp.wait_ge(acc_ready[b][2], after(i))
                    sp.dma_start(wg[b][:], wg_dram[2 * i + b]).then_inc(w_in[b], 16)
                    sp.dma_start(wu[b][:], wu_dram[2 * i + b]).then_inc(w_in[b], 16)

        @block.tensor
        def _(pe):
            with pe.Fori(0, KF // 2) as i:
                for b in range(2):
                    pe.wait_ge(w_in[b], after(32 * i + 32))
                    for t, (lo, hi) in enumerate(THIRDS):
                        pe.wait_ge(acc_read[1 - b][t], after(i + b))
                        for w, acc in ((wg, gate), (wu, up)):
                            for k in range(KD):
                                last = pe.matmul(acc[t][:, 0:THIRD], w[b][:, k, :], src[:, k, lo:hi],
                                                 start=k == 0, stop=k == KD - 1)
                        last.then_inc(acc_ready[b][t], 1)

        @block.scalar
        def _(act):
            with act.Fori(0, KF // 2) as i:
                for b in range(2):
                    for t in range(3):
                        act.wait_ge(acc_ready[b][t], after(i + 1))
                        act.wait_ge(acc_read[1 - b][t], after(i + b))
                        act.activation(silu[t][:], gate[t][:, 0:THIRD], ACT.Silu).then_inc(gated[t], 1)

        @block.vector
        def _(dve):
            with dve.Fori(0, KF // 2) as i:
                for b in range(2):
                    for t, (lo, hi) in enumerate(THIRDS):
                        dve.wait_ge(gated[t], after(2 * i + b + 1))
                        dve.tensor_tensor(out[:, bass.ds(2 * i + b, 1), lo:hi], silu[t][:].unsqueeze(1),
                                          up[t][:, 0:THIRD].unsqueeze(1), ALU.mult).then_inc(acc_read[b][t], 1)


def bias_phase(nc, io):
    with Tools(nc) as m:
        t5 = m.sb("t5", [32, HA])
        onehot = m.sb("onehot", [32, T5_LEN])
        fa = m.sb("t5_by_distance", [HA, T5_LEN])
        rel = m.sb("rel_reversed", [HC, 2 * REL + 1])
        fc = m.sb("rel_by_distance", [HC, BAND_LEN])
        acc = [m.ps(f"t5_acc{c}", [HA, 512]) for c in range(5)]
        loaded, acc_ready, fa_ready, fc_ready = m.sem("bias_in"), m.sem("t5_acc"), m.sem("t5_ready"), m.sem("rel_ready")
        lines_out = m.sem("bias_lines_out")
        pieces = [(lo, min(lo + 512, T5_LEN)) for lo in range(0, T5_LEN, 512)]
        block = m.block()

        @block.sync
        def _(sp):
            sp.dma_start(t5[:], io["t5"]).then_inc(loaded, 16)
            sp.dma_start(onehot[:], io["t5_onehot"]).then_inc(loaded, 16)
            sp.dma_start(rel[:], io["rel_rev"]).then_inc(loaded, 16)
            for name, line, ready, heads, rows, first, length in (
                    ("skew_a", fa, (fa_ready, len(pieces)), HA, P, T5_LEN - SKEW_A, SKEW_A),
                    ("skew_s", fa, (fa_ready, len(pieces)), HA, S, 0, SKEW_S),
                    ("skew_c", fc, (fc_ready, 2), HC, P, 0, SKEW_C)):
                sp.wait_ge(ready[0], after(ready[1]))
                sp.dma_start(io[name].rearrange("h (p n) -> h p n", p=rows),
                             line[:, first:first + length].unsqueeze(1).to_broadcast([heads, rows, length])
                             ).then_inc(lines_out, 16)
            sp.wait_ge(lines_out, after(48))

        @block.tensor
        def _(pe):
            pe.wait_ge(loaded, after(48))
            for c, (lo, hi) in enumerate(pieces):
                pe.matmul(acc[c][:, 0:hi - lo], t5[:], onehot[:, lo:hi], start=True, stop=True).then_inc(acc_ready, 1)

        @block.vector
        def _(dve):
            for c, (lo, hi) in enumerate(pieces):
                dve.wait_ge(acc_ready, after(c + 1))
                dve.tensor_scalar(fa[:, lo:hi], acc[c][:, 0:hi - lo], DH ** 0.5, None, ALU.mult).then_inc(fa_ready, 1)
            far = BAND_LEN - 1 - 2 * REL
            dve.tensor_scalar(fc[:, 0:far], rel[:, 0:1].to_broadcast([HC, far]), DH ** 0.5, None, ALU.mult).then_inc(fc_ready, 1)
            dve.tensor_scalar(fc[:, far:BAND_LEN], rel[:], DH ** 0.5, None, ALU.mult).then_inc(fc_ready, 1)


def shifted(skew, rows, length, shift, keys):
    return skew[:, shift:shift + rows * (length - 1)].rearrange(
        "h (p n) -> p h n", n=length - 1)[:, :, 0:keys]


def score_offset(i):
    return P * i * (i + 1) // 2


SAMPLE_KEYS = PAST + S
SAMPLE_AT = score_offset(TILES)


def index_phase(nc, io, score):
    with Tools(nc) as m:
        qi = m.sb("qi", [P, HA, N])
        ki = m.sb("ki", [P, N])
        ki_past = m.sb("ki_past", [P, PAST])
        w = m.sb("w_index", [P, TILES + 1, HA])
        relu = [m.sb(f"relu{b}", [P, 1024]) for b in range(2)]
        dots = [m.ps(f"dots{b}", [P, 1024]) for b in range(2)]
        loaded, w_scaled, halves_zero = m.sem("index_in"), m.sem("w_index_scaled"), m.sem("index_halves_zero")
        dots_ready, relu_ready, added = m.sem("dots"), m.sem("relu"), m.sem("score_added")
        units = [(i, P, hd, ki, 0, P * (i + 1), score_offset(i)) for i in range(2, TILES) for hd in range(HA)]
        for src, lo, n, at in ((ki_past, 0, 1024, 0), (ki_past, 1024, 1024, 1024), (ki, T, S, PAST)):
            units += [(TILES, S, hd, src, lo, n, SAMPLE_AT + at) for hd in range(HA)]
        block = m.block()

        @block.sync
        def _(sp):
            for hd in range(2):
                half = slice(DH * hd, DH * hd + DH)
                sp.dma_start(qi[half, hd::2, :], io["z0"][QI:QI + 4, half].rearrange("c p n -> p c n")).then_inc(loaded, 16)
            sp.dma_start(ki[:], io["z0"][KI]).then_inc(loaded, 16)
            sp.dma_start(ki_past[:], io["ki_past"]).then_inc(loaded, 16)
            sp.dma_start(w[:, 0:TILES, :], io["zt0"][0:T, 1024:1024 + HA].rearrange("(i p) h -> p i h", p=P)
                         ).then_inc(loaded, 16)
            sp.dma_start(w[0:S, TILES, :], io["zt0"][T:N, 1024:1024 + HA]).then_inc(loaded, 16)

        @block.gpsimd
        def _(pool):
            pool.memset(qi[0:DH, 1::2, :], 0.0).then_inc(halves_zero, 1)
            pool.memset(qi[DH:P, 0::2, :], 0.0).then_inc(halves_zero, 1)

        @block.tensor
        def _(pe):
            pe.wait_ge(loaded, after(96))
            pe.wait_ge(halves_zero, after(2))
            for u, (i, rows, hd, src, lo, n, at) in enumerate(units):
                if u >= 2:
                    pe.wait_ge(relu_ready, after(u - 1))
                for c in range(0, n, 512):
                    e = min(c + 512, n)
                    last = pe.matmul(dots[u % 2][0:rows, c:e], qi[:, hd, P * i:P * i + rows],
                                     src[:, lo + c:lo + e], start=True, stop=True)
                last.then_inc(dots_ready, 1)

        @block.scalar
        def _(act):
            for u, (i, rows, hd, src, lo, n, at) in enumerate(units):
                act.wait_ge(dots_ready, after(u + 1))
                if u >= 2:
                    act.wait_ge(added, after(u - 1))
                act.activation(relu[u % 2][0:rows, 0:n], dots[u % 2][0:rows, 0:n], ACT.Relu,
                               scale=DH ** -0.5).then_inc(relu_ready, 1)

        @block.vector
        def _(dve):
            dve.wait_ge(loaded, after(96))
            dve.tensor_scalar(w[:, 0:TILES, :], w[:, 0:TILES, :], HA ** -0.5, None, ALU.mult).then_inc(w_scaled, 1)
            dve.tensor_scalar(w[0:S, TILES, :], w[0:S, TILES, :], HA ** -0.5, None, ALU.mult).then_inc(w_scaled, 1)
            dve.wait_ge(w_scaled, after(2))
            for u, (i, rows, hd, src, lo, n, at) in enumerate(units):
                dve.wait_ge(relu_ready, after(u + 1))
                out = score[0:rows, at:at + n]
                if hd == 0:
                    dve.tensor_scalar(out, relu[u % 2][0:rows, 0:n], w[0:rows, i, 0:1], None, ALU.mult
                                      ).then_inc(added, 1)
                else:
                    dve.wait_ge(added, after(u))
                    dve.scalar_tensor_tensor(out=out, in0=relu[u % 2][0:rows, 0:n], scalar=w[0:rows, i, hd:hd + 1],
                                             in1=out, op0=ALU.mult, op1=ALU.add).then_inc(added, 1)
            dve.wait_ge(added, after(len(units)))
            for i in range(2, TILES):
                end = score_offset(i + 1)
                dve.memset(score[0:CHUNK, end - CHUNK:end], OUT_OF_REACH)


def choosing(m, score, mask_sample_dram):
    rounds = KTOP // 8
    lists = [[(P, score_offset(i), P * (i + 1)) for i in pair] for pair in ((2, 3), (4, 5), (6, 7))]
    lists.append([(S, SAMPLE_AT, SAMPLE_KEYS)])
    top = [m.sb(f"top{a}", [P, 8]) for a in range(2)]
    found = [[m.sem(f"top_found{n}{a}") for a in range(len(rows))] for n, rows in enumerate(lists)]
    taken = [[m.sem(f"top_taken{n}{a}") for a in range(len(rows))] for n, rows in enumerate(lists)]
    masked, stored = m.sem("mask_ready"), m.sem("mask_stored")

    def choose(dve):
        for n, rows in enumerate(lists):
            with dve.Fori(0, rounds) as r:
                for a, (p, at, width) in enumerate(rows):
                    wait_apart(dve, (taken[n][a], r))
                    dve.max(top[a][0:p, :], score[0:p, at:at + width]).then_inc(found[n][a], 1)
                for a, (p, at, width) in enumerate(rows):
                    wait_apart(dve, (found[n][a], r + 1))
                    dve.match_replace(score[0:p, at:at + width], top[a][0:p, :], score[0:p, at:at + width],
                                      TAKEN).then_inc(taken[n][a], 1)
            for a, (p, at, width) in enumerate(rows):
                dve.wait_ge(taken[n][a], after(rounds))
                dve.tensor_scalar(score[0:p, at:at + width], score[0:p, at:at + width], (TAKEN + OUT_OF_REACH) / 2,
                                  MASKED, ALU.is_gt, ALU.mult).then_inc(masked, 1)
        for i in range(2):
            end = score_offset(i + 1)
            dve.memset(score[:, score_offset(i):end], 0.0).then_inc(masked, 1)
            dve.wait_ge(masked, after(8 + i))
            dve.memset(score[0:CHUNK, end - CHUNK:end], MASKED)

    def store(sp):
        sp.wait_ge(masked, after(7))
        sp.dma_start(mask_sample_dram, score[0:S, SAMPLE_AT:SAMPLE_AT + SAMPLE_KEYS]).then_inc(stored, 16)
        sp.wait_ge(stored, after(16))

    return choose, store


def prompt_attention_phase(nc, name, io, z, q0, k0, vt, v0, skew, width, heads, back, mask, ident, mix):
    pairs = heads // 2
    units = 2 * TILES
    keys = [P * min(i + 1, (back or TILES) + 1) for i in range(TILES)]
    with Tools(nc) as m:
        q = [m.sb(f"{name}_q{b}", [P, 2, T]) for b in range(2)]
        k = [m.sb(f"{name}_k{b}", [P, T]) for b in range(2)]
        v = [m.sb(f"{name}_v{b}", [P, TILES, P]) for b in range(2)]
        bias = [m.sb(f"{name}_bias{b}", [P, 2, width]) for b in range(2)]
        extra = [m.sb(f"{name}_extra{a}", [P, T]) for a in range(2)] if mask is not None else None
        prob = [m.sb(f"{name}_prob{a}", [P, max(keys)]) for a in range(2)]
        probT = [m.sb(f"{name}_probT{a}", [P, max(keys)]) for a in range(2)]
        top, ntop, total, inv = (m.sb(f"{name}_{x}", [P, 2 * units]) for x in ("max", "nmax", "sum", "inv"))
        o = [m.sb(f"{name}_o{a}", [P, P]) for a in range(2)]
        oT = [m.sb(f"{name}_oT{b}", [P, T]) for b in range(2)]
        dots = [m.ps(f"{name}_dots{a}", [P, 1024]) for a in range(2)]
        turn = [m.ps(f"{name}_turn{g}", [P, 512]) for g in range(2)]
        ops = m.ps(f"{name}_out", [P, 512])
        oTps = m.ps(f"{name}_outT", [P, 512])
        loaded = [m.sem(f"{name}_in{b}") for b in range(2)]
        halves_zero = m.sem(f"{name}_halves_zero")
        band_masked = [m.sem(f"{name}_band{b}") for b in range(2)]
        dots_ready, extra_ready, logits, ntop_ready = (m.sem(f"{name}_{x}") for x in ("dots", "extra", "logits", "nmax"))
        prob_ready, inv_ready, o_ready, oT_ready = (m.sem(f"{name}_{x}") for x in ("prob", "inv", "o", "outT"))
        turned = [m.sem(f"{name}_turned{g}") for g in range(2)]
        probT_ready = [m.sem(f"{name}_probT{g}") for g in range(2)]
        out_ready = [m.sem(f"{name}_out{b}") for b in range(2)]
        oT_copied = [m.sem(f"{name}_oT{b}") for b in range(2)]
        stored = [m.sem(f"{name}_stored{b}") for b in range(2)]
        all_units = [(b, i, hd) for b in range(2) for i in range(TILES) for hd in range(2)]
        U = len(all_units)
        second = [keys[i] > 512 for _, i, _ in all_units]
        seconds = sum(second)
        block = m.block()

        @block.sync
        def _(sp):
            with sp.Fori(0, pairs // 2) as it:
                for b in range(2):
                    g = 2 * it + b
                    sp.wait_ge(out_ready[b], after(units * it))
                    for hd in range(2):
                        half = slice(DH * hd, DH * hd + DH)
                        sp.dma_start(q[b][half, hd, :], z[q0 + g][half, 0:T]).then_inc(loaded[b], 16)
                    sp.dma_start(k[b][:], z[k0 + g][:, 0:T]).then_inc(loaded[b], 16)
                    sp.dma_start(bias[b][:], shifted(skew[bass.ds(2 * g, 2)], P, width + P - 1, P - 1, width)
                                 ).then_inc(loaded[b], 16)
                    sp.dma_start(v[b][:], vt[0:T, bass.ds(v0 + P * g, P)].rearrange("(i p) n -> p i n", p=P)
                                 ).then_inc(loaded[b], 16)

        @block.gpsimd
        def _(pool):
            for b in range(2):
                for hd in range(2):
                    pool.memset(q[b][DH * (1 - hd):DH * (2 - hd), hd, :], 0.0).then_inc(halves_zero, 1)
            pool.wait_ge(halves_zero, after(4))
            with pool.Fori(0, pairs // 2) as it:
                for b in range(2):
                    if mask is None:
                        wait_apart(pool, (loaded[b], 80 * it + 80))
                        pool.memset(bias[b][0:CHUNK, :, width - CHUNK:width], MASKED).then_inc(band_masked[b], 1)
                        pool.memset(bias[b][CHUNK:P, :, 0:CHUNK], MASKED).then_inc(band_masked[b], 1)
                    else:
                        pool.wait_ge(loaded[b], after(80 * it + 80))
                        for i in range(TILES):
                            for hd in range(2):
                                u = units * b + 2 * i + hd
                                pool.wait_ge(logits, after(U * it + max(u - 1, 0)))
                                pool.tensor_tensor(extra[u % 2][:, 0:keys[i]], bias[b][:, hd, width - keys[i]:width],
                                                   mask[:, score_offset(i):score_offset(i + 1)], ALU.add
                                                   ).then_inc(extra_ready, 1)

        @block.tensor
        def _(pe):
            def scores(it, u):
                b, i, hd = all_units[u]
                if u % units == 0:
                    pe.wait_ge(loaded[b], after(80 * it + 80))
                pe.wait_ge(logits, after(U * it + max(u - 1, 0)))
                first = P * (i + 1) - keys[i]
                for c in range(0, keys[i], 512):
                    e = min(c + 512, keys[i])
                    last = pe.matmul(dots[u % 2][:, c:e], q[b][:, hd, P * i:P * i + P],
                                     k[b][:, first + c:first + e], start=True, stop=True)
                last.then_inc(dots_ready, 1)

            def turns(it, u):
                b, i, hd = all_units[u]
                pe.wait_ge(prob_ready, after(U * it + u + 1))
                for g in range(2 if second[u] else 1):
                    pe.wait_ge(probT_ready[g], after((U if g == 0 else seconds) * it + (u if g == 0 else sum(second[:u]))))
                    for c in range(512 * g, min(512 * g + 512, keys[i]), P):
                        last = pe.transpose(turn[g][:, c - 512 * g:c - 512 * g + P], prob[u % 2][:, c:c + P], ident[:])
                    last.then_inc(turned[g], 1)

            def values(it, u):
                b, i, hd = all_units[u]
                pe.wait_ge(probT_ready[0], after(U * it + u + 1))
                if second[u]:
                    pe.wait_ge(probT_ready[1], after(seconds * it + sum(second[:u + 1])))
                pe.wait_ge(o_ready, after(U * it + u))
                at = P * (i % 2) + DH * hd
                blocks = keys[i] // P
                for c in range(blocks):
                    last = pe.matmul(ops[:, at:at + DH], probT[u % 2][:, P * c:P * c + P],
                                     v[b][:, i + 1 - blocks + c, DH * hd:DH * hd + DH], start=c == 0, stop=c == blocks - 1)
                last.then_inc(out_ready[b], 1)

            def turn_out(it, u):
                b, i, hd = all_units[u]
                if hd == 0:
                    return
                pe.wait_ge(o_ready, after(U * it + u + 1))
                if i == 0:
                    pe.wait_ge(oT_copied[1 - b], after(TILES * (it + b)))
                else:
                    pe.wait_ge(oT_copied[b], after(TILES * it + i))
                pe.transpose(oTps[:, 0:P], o[i % 2][:], ident[:]).then_inc(oT_ready, 1)

            pe.wait_ge(halves_zero, after(4))
            with pe.Fori(0, pairs // 2) as it:
                for s in range(U + 3):
                    if s < U:
                        scores(it, s)
                    if 0 <= s - 1 < U:
                        turns(it, s - 1)
                    if 0 <= s - 2 < U:
                        values(it, s - 2)
                    if 0 <= s - 3 < U:
                        turn_out(it, s - 3)

        @block.vector
        def _(dve):
            def logit(it, u):
                b, i, hd = all_units[u]
                waits = [(dots_ready, U * it + u + 1)]
                if mask is not None:
                    waits.append((extra_ready, U * it + u + 1))
                    add = extra[u % 2][:, 0:keys[i]]
                else:
                    if u % units == 0:
                        waits.append((band_masked[b], 2 * it + 2))
                    add = bias[b][:, hd, width - keys[i]:width]
                wait_apart(dve, *waits, (turned[0], U * it + max(u - 1, 0)),
                           (turned[1], seconds * it + sum(second[:max(u - 1, 0)])))
                dve.tensor_tensor_reduce(prob[u % 2][:, 0:keys[i]], dots[u % 2][:, 0:keys[i]], add, 1.0, -3.0e38,
                                         ALU.add, ALU.max, top[:, u:u + 1]).then_inc(logits, 1)
                dve.wait_ge(logits, after(U * it + u + 1))
                dve.tensor_scalar(ntop[:, u:u + 1], top[:, u:u + 1], -DH ** -0.5, None, ALU.mult).then_inc(ntop_ready, 1)

            def copy(it, u):
                b, i, hd = all_units[u]
                n = min(keys[i], 512)
                dve.wait_ge(turned[0], after(U * it + u + 1))
                if u >= 2:
                    bb = all_units[u - 2][0]
                    dve.wait_ge(out_ready[bb], after(units * it + (u - 2) % units + 1))
                else:
                    dve.wait_ge(out_ready[1], after(units * it))
                dve.tensor_copy(probT[u % 2][:, 0:n], turn[0][:, 0:n]).then_inc(probT_ready[0], 1)

            def norm(it, u):
                b, i, hd = all_units[u]
                dve.wait_ge(prob_ready, after(U * it + u + 1))
                dve.reciprocal(inv[:, u:u + 1], total[:, u:u + 1]).then_inc(inv_ready, 1)
                dve.wait_ge(inv_ready, after(U * it + u + 1))
                dve.wait_ge(out_ready[b], after(units * it + u % units + 1))
                dve.wait_ge(oT_ready, after(U // 2 * it + max(u // 2 - 1, 0)))
                at = P * (i % 2) + DH * hd
                dve.tensor_scalar(o[i % 2][:, DH * hd:DH * hd + DH], ops[:, at:at + DH], inv[:, u:u + 1], None,
                                  ALU.mult).then_inc(o_ready, 1)

            with dve.Fori(0, pairs // 2) as it:
                for s in range(U + 2):
                    if s < U:
                        logit(it, s)
                    if 0 <= s - 1 < U:
                        copy(it, s - 1)
                    if 0 <= s - 2 < U:
                        norm(it, s - 2)

        @block.scalar
        def _(act):
            def exp(it, u):
                b, i, hd = all_units[u]
                act.wait_ge(ntop_ready, after(U * it + u + 1))
                act.activation(prob[u % 2][:, 0:keys[i]], prob[u % 2][:, 0:keys[i]], ACT.Exp, bias=ntop[:, u:u + 1],
                               scale=DH ** -0.5, accum_out=total[:, u:u + 1]).then_inc(prob_ready, 1)

            def copy(it, u):
                b, i, hd = all_units[u]
                if second[u]:
                    act.wait_ge(turned[1], after(seconds * it + sum(second[:u + 1])))
                    if u >= 2:
                        bb = all_units[u - 2][0]
                        act.wait_ge(out_ready[bb], after(units * it + (u - 2) % units + 1))
                    else:
                        act.wait_ge(out_ready[1], after(units * it))
                    act.activation(probT[u % 2][:, 512:keys[i]], turn[1][:, 0:keys[i] - 512], ACT.Copy
                                   ).then_inc(probT_ready[1], 1)

            def out(it, u):
                b, i, hd = all_units[u]
                if hd == 0:
                    return
                act.wait_ge(oT_ready, after(U // 2 * it + u // 2 + 1))
                if i == 0:
                    act.wait_ge(stored[b], after(16 * it))
                act.activation(oT[b][:, P * i:P * i + P], oTps[:, 0:P], ACT.Copy).then_inc(oT_copied[b], 1)
                if i == TILES - 1:
                    act.wait_ge(oT_copied[b], after(TILES * it + TILES))
                    act.dma_start(mix[2 * it + b][:, 0:T], oT[b][:]).then_inc(stored[b], 16)

            with act.Fori(0, pairs // 2) as it:
                for s in range(U + 3):
                    if s < U:
                        exp(it, s)
                    if 0 <= s - 1 < U:
                        copy(it, s - 1)
                    if 0 <= s - 3 < U:
                        out(it, s - 3)
            for b in range(2):
                act.wait_ge(stored[b], after(16 * (pairs // 2)))


def sample_attention_phase(nc, name, io, z, q0, k0, vt, v0, k_past, v_past, past, skew, length, shift, heads, mask_dram,
                           ident, mix):
    groups = heads // 4
    keys = past + S
    blocks = past // P + 1
    pieces = [(lo, min(lo + 1024, keys)) for lo in range(0, keys, 1024)]
    quads = [(lo, min(lo + 4, blocks)) for lo in range(0, blocks, 4)]
    with Tools(nc) as m:
        q = [m.sb(f"{name}_q{b}", [P, 4, S]) for b in range(2)]
        k = [m.sb(f"{name}_k{b}", [P, 2, keys]) for b in range(2)]
        v = [m.sb(f"{name}_v{b}", [P, blocks, 256]) for b in range(2)]
        bias = [m.sb(f"{name}_bias{b}", [P, keys]) for b in range(2)]
        mask = m.sb(f"{name}_mask", [P, keys]) if mask_dram is not None else None
        prob = m.sb(f"{name}_prob", [P, keys])
        probT = m.sb(f"{name}_probT", [P, blocks, P])
        top = m.sb(f"{name}_max", [P, 8])
        total, inv = m.sb(f"{name}_sum", [P, 1]), m.sb(f"{name}_inv", [P, 1])
        o, oT = m.sb(f"{name}_o", [P, DH]), m.sb(f"{name}_oT", [DH, P])
        dots = [m.ps(f"{name}_dots{a}", [P, 1024]) for a in range(2)]
        turn = [m.ps(f"{name}_turn{a}", [P, 512]) for a in range(2)]
        ops, oTps = m.ps(f"{name}_out", [P, 512]), m.ps(f"{name}_outT", [P, 512])
        loaded = [m.sem(f"{name}_in{b}") for b in range(2)]
        halves_zero = m.sem(f"{name}_halves_zero")
        mask_in, bias_ready = m.sem(f"{name}_mask_in"), m.sem(f"{name}_bias")
        dots_ready, logits, top_ready, ntop_ready, prob_ready = (
            m.sem(f"{name}_{x}") for x in ("dots", "logits", "top", "ntop", "prob"))
        turned, probT_ready, out_ready, inv_ready, o_ready, oT_ready, oT_copied, stored = (
            m.sem(f"{name}_{x}") for x in ("turned", "probT", "out", "inv", "o", "oT", "oT_copied", "stored"))
        block = m.block()

        @block.sync
        def _(sp):
            if mask is not None:
                for j in range(4):
                    sp.dma_start(mask[S * j:S * j + S, :], mask_dram).then_inc(mask_in, 16)
            for g in range(groups):
                b = g % 2
                if g >= 2:
                    sp.wait_ge(out_ready, after(g - 1))
                for hd in range(2):
                    half = slice(DH * hd, DH * hd + DH)
                    sp.dma_start(q[b][half, hd::2, :], z[q0 + 2 * g:q0 + 2 * g + 2, half, T:N]
                                 .rearrange("c p n -> p c n")).then_inc(loaded[b], 16)
                sp.dma_start(k[b][:, :, 0:past], k_past[2 * g:2 * g + 2].rearrange("c p n -> p c n")
                             ).then_inc(loaded[b], 16)
                sp.dma_start(k[b][:, :, past:keys], z[k0 + 2 * g:k0 + 2 * g + 2, :, T:N].rearrange("c p n -> p c n")
                             ).then_inc(loaded[b], 16)
                for j in range(4):
                    sp.dma_start(bias[b][S * j:S * j + S, :], shifted(skew[4 * g + j:4 * g + j + 1], S, length, shift, keys)
                                 .rearrange("p h n -> p (h n)")).then_inc(loaded[b], 16)
                sp.dma_start(v[b][:, 0:blocks - 1, :], v_past[:, 256 * g:256 * g + 256]
                             .rearrange("(i p) n -> p i n", p=P)).then_inc(loaded[b], 16)
                sp.dma_start(v[b][0:S, blocks - 1, :], vt[T:N, v0 + 256 * g:v0 + 256 * g + 256]
                             ).then_inc(loaded[b], 16)

        IN = 16 * 10

        @block.gpsimd
        def _(pool):
            for b in range(2):
                for hd in range(2):
                    pool.memset(q[b][DH * (1 - hd):DH * (2 - hd), hd::2, :], 0.0).then_inc(halves_zero, 1)
            pool.wait_ge(halves_zero, after(4))
            if mask is not None:
                pool.wait_ge(mask_in, after(64))
                for g in range(groups):
                    b = g % 2
                    pool.wait_ge(loaded[b], after(IN * (g // 2 + 1)))
                    pool.tensor_tensor(bias[b][:], bias[b][:], mask[:], ALU.add).then_inc(bias_ready, 1)

        @block.tensor
        def _(pe):
            n_dots = n_turn = 0
            pe.wait_ge(halves_zero, after(4))
            for g in range(groups):
                b = g % 2
                pe.wait_ge(loaded[b], after(IN * (g // 2 + 1)))
                for lo, hi in pieces:
                    if n_dots >= 2:
                        pe.wait_ge(logits, after(n_dots - 1))
                    for j in range(4):
                        for c in range(lo, hi, 512):
                            e = min(c + 512, hi)
                            last = pe.matmul(dots[n_dots % 2][S * j:S * j + S, c - lo:e - lo], q[b][:, j, :],
                                             k[b][:, j // 2, c:e], start=True, stop=True)
                    last.then_inc(dots_ready, 1)
                    n_dots += 1
                pe.wait_ge(prob_ready, after(g + 1))
                for lo, hi in quads:
                    if n_turn >= 2:
                        pe.wait_ge(probT_ready, after(n_turn - 1))
                    for c in range(lo, hi):
                        n = P if c < blocks - 1 else S
                        last = pe.transpose(turn[n_turn % 2][0:n, P * (c - lo):P * (c - lo) + P],
                                            prob[:, P * c:P * c + n], ident[:])
                    last.then_inc(turned, 1)
                    n_turn += 1
                pe.wait_ge(probT_ready, after(n_turn))
                if g >= 1:
                    pe.wait_ge(o_ready, after(g))
                for j in range(4):
                    for c in range(blocks):
                        n = P if c < blocks - 1 else S
                        last = pe.matmul(ops[S * j:S * j + S, 0:DH], probT[0:n, c, S * j:S * j + S],
                                         v[b][0:n, c, DH * j:DH * j + DH], start=c == 0, stop=c == blocks - 1)
                last.then_inc(out_ready, 1)
                pe.wait_ge(o_ready, after(g + 1))
                if g >= 1:
                    pe.wait_ge(oT_copied, after(g))
                pe.transpose(oTps[0:DH, 0:P], o[:], ident[:]).then_inc(oT_ready, 1)

        @block.vector
        def _(dve):
            n_dots = n_turn = 0
            for g in range(groups):
                b = g % 2
                if mask is not None:
                    dve.wait_ge(bias_ready, after(g + 1))
                else:
                    dve.wait_ge(loaded[b], after(IN * (g // 2 + 1)))
                if g >= 1:
                    dve.wait_ge(turned, after(len(quads) * g))
                for c, (lo, hi) in enumerate(pieces):
                    n_dots += 1
                    dve.wait_ge(dots_ready, after(n_dots))
                    dve.tensor_tensor_reduce(prob[:, lo:hi], dots[(n_dots - 1) % 2][:, 0:hi - lo], bias[b][:, lo:hi],
                                             1.0, -3.0e38, ALU.add, ALU.max, top[:, c:c + 1]).then_inc(logits, 1)
                dve.wait_ge(logits, after(n_dots))
                dve.tensor_reduce(top[:, 4:5], top[:, 0:len(pieces)], AX_X, ALU.max).then_inc(top_ready, 1)
                dve.wait_ge(top_ready, after(g + 1))
                dve.tensor_scalar(top[:, 5:6], top[:, 4:5], -DH ** -0.5, None, ALU.mult).then_inc(ntop_ready, 1)
                if g >= 1:
                    dve.wait_ge(out_ready, after(g))
                for lo, hi in quads:
                    n_turn += 1
                    dve.wait_ge(turned, after(n_turn))
                    full = min(hi, blocks - 1)
                    bank = turn[(n_turn - 1) % 2]
                    if full > lo:
                        last = dve.tensor_copy(probT[:, lo:full, :], bank[:, 0:P * (full - lo)]
                                               .rearrange("p (c n) -> p c n", n=P))
                    if hi == blocks:
                        last = dve.tensor_copy(probT[0:S, blocks - 1, :], bank[0:S, P * (full - lo):P * (full - lo) + P])
                    last.then_inc(probT_ready, 1)
                dve.wait_ge(prob_ready, after(g + 1))
                dve.reciprocal(inv[:], total[:]).then_inc(inv_ready, 1)
                dve.wait_ge(inv_ready, after(g + 1))
                dve.wait_ge(out_ready, after(g + 1))
                if g >= 1:
                    dve.wait_ge(oT_ready, after(g))
                dve.tensor_scalar(o[:], ops[:, 0:DH], inv[:], None, ALU.mult).then_inc(o_ready, 1)

        @block.scalar
        def _(act):
            for g in range(groups):
                act.wait_ge(ntop_ready, after(g + 1))
                if g >= 1:
                    act.wait_ge(inv_ready, after(g))
                act.activation(prob[:], prob[:], ACT.Exp, bias=top[:, 5:6], scale=DH ** -0.5,
                               accum_out=total[:]).then_inc(prob_ready, 1)
                act.wait_ge(oT_ready, after(g + 1))
                if g >= 1:
                    act.wait_ge(stored, after(64 * g))
                act.activation(oT[:], oTps[0:DH, 0:P], ACT.Copy).then_inc(oT_copied, 1)
                act.wait_ge(oT_copied, after(g + 1))
                for j in range(4):
                    act.dma_start(mix[2 * g + j // 2, DH * (j % 2):DH * (j % 2) + DH, T:N], oT[:, S * j:S * j + S]
                                  ).then_inc(stored, 16)
            act.wait_ge(stored, after(64 * groups))
LEVELS = 7


def recurrence_phase(nc, io, ident, o, raw):
    TP = (TILES + 1) * P
    W = HB * P
    ALL = LEVELS + 2
    TO_END, FROM_START = LEVELS, LEVELS + 1
    with Tools(nc) as m:
        q = m.sb("hg_q", [P, HB, TP])
        k = m.sb("hg_k", [P, HB, TP])
        g = m.sb("hg_g", [P, HB, TP])
        v = m.sb("hg_v", [P, TILES + 1, W])
        lb2 = m.sb("hg_lb2", [P, 2, HB])
        lbt = m.sb("hg_lbt", [P, 4, HB])
        masks = m.sb("hg_masks", [P, LEVELS + 1, P])
        one = m.sb("hg_one", [P, P])
        kept = m.sb("hg_kept", [P, HB, P])
        dec = m.sb("hg_decayed", [P, ALL, W])
        last_decay = m.sb("hg_last_decay", [P, HB])
        att = m.sb("hg_att", [P, LEVELS + 1, P])
        attT = [m.sb(f"hg_attT{a}", [P, P]) for a in range(2)]
        kT = m.sb("hg_kT", [P, W])
        state = m.sb("hg_state", [P, HB, P])
        pairs = [m.ps(f"hg_pairs{a}", [P, 1024]) for a in range(2)]
        kTps, dS, ops = m.ps("hg_kTps", [P, 512]), m.ps("hg_dS", [P, 512]), [m.ps(f"hg_ops{a}", [P, 512]) for a in range(2)]
        small_in, f_in, q_in, v_in = m.sem("hg_small_in"), m.sem("hg_f_in"), m.sem("hg_q_in"), m.sem("hg_v_in")
        lb_steps, f_sig, f_done, g_done, q_done, k_done = (m.sem(f"hg_{x}") for x in ("lb", "sig", "f", "g", "q", "k"))
        setup_done = m.sem("hg_setup")
        summed, diffs, decays, decayed, kept_s = (m.sem(f"hg_{x}") for x in ("summed", "diffs", "decays", "decayed", "kept"))
        pairs_ready, masked, attT_ready, kT_turned, kT_ready = (
            m.sem(f"hg_{x}") for x in ("pairs", "masked", "attT", "kT_turned", "kT_copied"))
        out_ready, out_copied, dS_ready, state_ready, state_io = (
            m.sem(f"hg_{x}") for x in ("out", "out_copied", "dS", "state", "state_io"))
        decayed_v, last_ready = m.sem("hg_decayed_levels"), m.sem("hg_last_decay_ready")
        block = m.block()

        def tiles(eng, body):
            with eng.Fori(0, TILES) as c:
                body(c, False)
            body(TILES, True)

        @block.sync
        def _(sp):
            sp.dma_start(lb2[:], io["lb"]).then_inc(small_in, 16)
            sp.dma_start(masks[:], io["hg_masks"]).then_inc(small_in, 16)
            sp.dma_start(raw, io["z0"][FB:FB + HB].rearrange("c p n -> p c n")).then_inc(f_in, 16)
            sp.dma_start(q[:, :, 0:N], io["z0"][QB:QB + HB].rearrange("c p n -> p c n")).then_inc(q_in, 16)
            sp.dma_start(v[:, 0:TILES, :], io["zt0"][0:T, 512:1024].rearrange("(i p) n -> p i n", p=P)).then_inc(v_in, 16)
            sp.wait_ge(setup_done, after(1))
            sp.dma_start(v[0:S, TILES, :], io["zt0"][T:N, 512:1024]).then_inc(v_in, 16)
            sp.wait_ge(state_ready, after(HB * TILES))
            sp.dma_start(io["state_p"].rearrange("h k v -> k h v"), state[:]).then_inc(state_io, 16)
            sp.wait_ge(state_io, after(16))
            sp.wait_ge(out_ready, after(HB * TILES))
            sp.dma_start(state[:], io["state_in"].rearrange("h k v -> k h v")).then_inc(state_io, 16)
            sp.wait_ge(state_ready, after(HB * (TILES + 1)))
            sp.dma_start(io["state_s"].rearrange("h k v -> k h v"), state[:]).then_inc(state_io, 16)
            sp.wait_ge(state_io, after(48))

        @block.scalar
        def _(act):
            act.wait_ge(q_in, after(16))
            act.activation(q[:, :, 0:N], q[:, :, 0:N], ACT.Silu).then_inc(q_done, 1)
            act.wait_ge(f_in, after(16))
            act.activation(raw, raw, ACT.Sigmoid).then_inc(f_sig, 1)
            act.wait_ge(lb_steps, after(2))
            act.activation(lbt[:, 1:3, :], lb2[:], ACT.Exp).then_inc(lb_steps, 1)
            act.wait_ge(f_done, after(HB))
            act.activation(g[:, :, 0:N], raw, ACT.Ln).then_inc(g_done, 1)

            def body(c, sample):
                act.wait_ge(diffs, after(c + 1))
                act.activation(dec[:], dec[:], ACT.Exp).then_inc(decays, 1)
                act.wait_ge(kT_turned, after(c + 1))
                act.wait_ge(dS_ready, after(HB * c))
                act.activation(kT[:], kTps[:], ACT.Copy).then_inc(kT_ready, 1)
                for hd in range(HB):
                    act.wait_ge(out_ready, after(HB * c + hd + 1))
                    act.activation(o[:, bass.ds(c, 1), P * hd:P * hd + P], ops[hd % 2][:, 0:P].unsqueeze(1), ACT.Copy
                                   ).then_inc(out_copied, 1)
            tiles(act, body)

        @block.gpsimd
        def _(pool):
            pool.memset(one[:], 1.0)
            pool.memset(v[:, TILES, :], 0.0)
            pool.memset(q[:, :, N:TP], 0.0)
            pool.memset(k[:, :, N:TP], 0.0)
            pool.memset(g[:, :, N:TP], 0.0)
            pool.memset(state[:], 0.0).then_inc(setup_done, 1)

            def body(c, sample):
                qv, kv = q[:, :, bass.ds(c * P, P)], k[:, :, bass.ds(c * P, P)]
                pool.wait_ge(decays, after(c + 1))
                pool.wait_ge(out_ready, after(HB * c))
                pool.tensor_copy(kept[:], kv).then_inc(kept_s, 1)
                pool.tensor_tensor(dec[:, TO_END, :].rearrange("p (h n) -> p h n", h=HB),
                                   dec[:, TO_END, :].rearrange("p (h n) -> p h n", h=HB), kv, ALU.mult).then_inc(decayed, 1)
                pool.wait_ge(last_ready, after(c + 1))
                pool.tensor_tensor(dec[:, FROM_START, :].rearrange("p (h n) -> p h n", h=HB),
                                   dec[:, FROM_START, :].rearrange("p (h n) -> p h n", h=HB), qv, ALU.mult).then_inc(decayed, 1)
            pool.wait_ge(k_done, after(HB))
            pool.wait_ge(q_done, after(1))
            tiles(pool, body)

        def halves(view, level, side):
            return view.rearrange("p (b s m) -> p b s m", s=2, m=1 << level)[:, :, side, :]

        @block.vector
        def _(dve):
            dve.wait_ge(small_in, after(32))
            dve.tensor_tensor(lbt[:, 0, :], lb2[:, 0, :], lb2[:, 1, :], ALU.max).then_inc(lb_steps, 1)
            dve.wait_ge(lb_steps, after(1))
            dve.tensor_tensor(lb2[:], lb2[:], lbt[:, 0, :].unsqueeze(1).to_broadcast([P, 2, HB]), ALU.subtract
                              ).then_inc(lb_steps, 1)
            dve.wait_ge(lb_steps, after(3))
            dve.tensor_tensor(lbt[:, 3, :], lbt[:, 1, :], lbt[:, 2, :], ALU.add).then_inc(lb_steps, 1)
            dve.wait_ge(lb_steps, after(4))
            dve.reciprocal(lbt[:, 0, :], lbt[:, 3, :]).then_inc(lb_steps, 1)
            dve.wait_ge(lb_steps, after(5))
            dve.tensor_tensor(lbt[:, 1, :], lbt[:, 1, :], lbt[:, 0, :], ALU.mult).then_inc(lb_steps, 1)
            dve.wait_ge(lb_steps, after(6))
            dve.tensor_scalar(lbt[:, 2, :], lbt[:, 1, :], -1.0, 1.0, ALU.mult, ALU.add).then_inc(lb_steps, 1)
            dve.wait_ge(lb_steps, after(7))
            dve.wait_ge(f_sig, after(1))
            for hd in range(HB):
                dve.tensor_scalar(raw[:, hd, :], raw[:, hd, :], lbt[:, 2, hd:hd + 1], lbt[:, 1, hd:hd + 1],
                                  ALU.mult, ALU.add).then_inc(f_done, 1)
            dve.wait_ge(f_done, after(HB))
            for hd in range(HB):
                dve.tensor_scalar(k[:, hd, 0:N], raw[:, hd, :], -1.0, 1.0, ALU.mult, ALU.add).then_inc(k_done, 1)
            dve.wait_ge(setup_done, after(1))
            dve.wait_ge(g_done, after(1))
            dve.wait_ge(k_done, after(HB))
            dve.wait_ge(q_done, after(1))

            def body(c, sample):
                start = dec[:, FROM_START, :]
                dve.wait_ge(out_ready, after(HB * c))
                dve.wait_ge(state_ready, after(HB * c))
                for hd in range(HB):
                    dve.tensor_tensor_scan(dec[:, FROM_START, P * hd:P * hd + P], one[:],
                                           g[:, hd, bass.ds(c * P, P)], 0.0, ALU.mult, ALU.add).then_inc(summed, 1)
                dve.wait_ge(summed, after(HB * (c + 1)))
                for lv in range(LEVELS):
                    half = 1 << lv
                    first, second = halves(start, lv, 0), halves(start, lv, 1)
                    mid = first[:, :, half - 1:half].to_broadcast([P, W // (2 * half), half])
                    dve.tensor_tensor(halves(dec[:, lv, :], lv, 1), second, mid, ALU.subtract)
                    dve.tensor_tensor(halves(dec[:, lv, :], lv, 0), mid, first, ALU.subtract)
                byhead = start.rearrange("p (h n) -> p h n", h=HB)
                end = byhead[:, :, P - 1:P].to_broadcast([P, HB, P])
                dve.tensor_tensor(dec[:, TO_END, :].rearrange("p (h n) -> p h n", h=HB), end, byhead, ALU.subtract
                                  ).then_inc(diffs, 1)
                dve.wait_ge(decays, after(c + 1))
                dve.tensor_copy(last_decay[:].unsqueeze(2), byhead[:, :, P - 1:P]).then_inc(last_ready, 1)
                for lv in range(LEVELS):
                    for side, src in ((0, k), (1, q)):
                        sv = src[:, :, bass.ds(c * P, P)]
                        d4 = dec[:, lv, :].rearrange("p (h b s m) -> p h b s m", h=HB, s=2, m=1 << lv)[:, :, :, side, :]
                        s4 = sv.rearrange("p h (b s m) -> p h b s m", s=2, m=1 << lv)[:, :, :, side, :]
                        last = dve.tensor_tensor(d4, d4, s4, ALU.mult)
                last.then_inc(decayed_v, 1)
                for hd in range(HB):
                    n = HB * c + hd
                    dve.wait_ge(pairs_ready, after(n + 1))
                    dve.wait_ge(attT_ready, after(n))
                    dve.tensor_tensor(att[:], pairs[hd % 2][:].rearrange("p (l n) -> p l n", l=LEVELS + 1), masks[:],
                                      ALU.mult).then_inc(masked, 1)
                    dve.wait_ge(masked, after(n + 1))
                    if hd < 2:
                        dve.wait_ge(out_ready, after(HB * c))
                    else:
                        dve.wait_ge(out_ready, after(HB * c + hd - 1))
                    dve.tensor_reduce(attT[hd % 2][:], att[:].rearrange("p l n -> p n l"), AX_X, ALU.add
                                      ).then_inc(attT_ready, 1)
                    dve.wait_ge(dS_ready, after(n + 1))
                    dve.wait_ge(out_ready, after(n + 1))
                    dve.scalar_tensor_tensor(out=state[:, hd, :], in0=state[:, hd, :], scalar=last_decay[:, hd:hd + 1],
                                             in1=dS[:, P * hd:P * hd + P], op0=ALU.mult, op1=ALU.add).then_inc(state_ready, 1)
            tiles(dve, body)

        @block.tensor
        def _(pe):
            pe.wait_ge(v_in, after(32))
            pe.wait_ge(small_in, after(32))

            def body(c, sample):
                pe.wait_ge(decayed_v, after(c + 1))
                pe.wait_ge(decayed, after(2 * c + 2))
                pe.wait_ge(kept_s, after(c + 1))
                pe.wait_ge(kT_ready, after(c))
                for hd in range(HB):
                    h = slice(P * hd, P * hd + P)
                    last = pe.transpose(kTps[:, h], dec[:, TO_END, h], ident[:])
                last.then_inc(kT_turned, 1)

                def products(hd):
                    n = HB * c + hd
                    h = slice(P * hd, P * hd + P)
                    pe.wait_ge(masked, after(HB * c + max(hd - 1, 0)))
                    for lv in range(LEVELS):
                        pe.matmul(pairs[hd % 2][:, P * lv:P * lv + P], dec[:, lv, h], dec[:, lv, h], start=True, stop=True)
                    pe.matmul(pairs[hd % 2][:, P * LEVELS:], kept[:, hd, :], q[:, hd, bass.ds(c * P, P)],
                              start=True, stop=True).then_inc(pairs_ready, 1)

                products(0)
                for hd in range(HB):
                    if hd + 1 < HB:
                        products(hd + 1)
                    n = HB * c + hd
                    h = slice(P * hd, P * hd + P)
                    pe.wait_ge(kT_ready, after(c + 1))
                    pe.wait_ge(state_ready, after(n))
                    vv = v[:, bass.ds(c, 1), h].rearrange("p c n -> p (c n)")
                    pe.matmul(dS[:, h], kT[:, h], vv, start=True, stop=True).then_inc(dS_ready, 1)
                    pe.wait_ge(attT_ready, after(n + 1))
                    pe.wait_ge(out_copied, after(HB * c + max(hd - 1, 0)))
                    if sample and hd == 0:
                        pe.wait_ge(state_io, after(32))
                    pe.matmul(ops[hd % 2][:, 0:P], attT[hd % 2][:], vv, start=True, stop=False)
                    pe.matmul(ops[hd % 2][:, 0:P], dec[:, FROM_START, h], state[:, hd, :], start=False, stop=True
                              ).then_inc(out_ready, 1)
            tiles(pe, body)


def recurrence_out_phase(nc, io, consts, o, mix, x):
    ident = consts.ident
    TC = TILES + 1
    with Tools(nc) as m:
        gate = m.sb("ho_gate", [P, HB, N])
        gnorm = m.sb("ho_gnorm", [P, HB])
        squares = m.sb("ho_squares", [P, P])
        rstd = m.sb("ho_rstd", [P, TC * HB])
        eps = m.sb("ho_eps", [P, 1])
        out = m.sb("ho_out", [P, HB, N])
        turn = [m.ps(f"ho_turn{a}", [P, 512]) for a in range(2)]
        loaded, gated, eps_set = m.sem("ho_in"), m.sem("ho_gated"), m.sem("ho_eps_set")
        summed, root, inv, normed = (m.sem(f"ho_{x}") for x in ("summed", "root", "inv", "normed"))
        turned, done, stored, x_in, gain_step = (m.sem(f"ho_{x}") for x in ("turned", "done", "stored", "x_in", "gain"))
        units = [(hd, lo, min(lo + 4, TC)) for hd in range(HB) for lo in range(0, TC, 4)]
        block = m.block()

        @block.sync
        def _(sp):
            sp.dma_start(gate[:], io["z0"][GB:GB + HB].rearrange("c p n -> p c n")).then_inc(loaded, 16)
            sp.dma_start(gnorm[:], io["norm_b"]).then_inc(loaded, 16)
            sp.dma_start(x[:], io["xT"]).then_inc(x_in, 16)
            for hd in range(HB):
                sp.wait_ge(done, after(3 * (hd + 1)))
                sp.dma_start(mix[HB + hd], out[:, hd, :]).then_inc(stored, 16)
            sp.wait_ge(stored, after(16 * HB))
            sp.wait_ge(x_in, after(16))

        @block.scalar
        def _(act):
            act.wait_ge(loaded, after(32))
            act.activation(gate[:], gate[:], ACT.Silu).then_inc(gated, 1)
            for n in range(TC * HB):
                if n:
                    act.wait_ge(summed, after(n))
                act.activation(squares[:], o[:, n // HB, P * (n % HB):P * (n % HB) + P], ACT.Square,
                               accum_out=rstd[:, n:n + 1]).then_inc(summed, 1)
            act.wait_ge(summed, after(TC * HB))
            act.wait_ge(eps_set, after(1))
            act.activation(rstd[:], rstd[:], ACT.Sqrt, bias=eps[:, 0:1], scale=1.0 / P).then_inc(root, 1)

        @block.vector
        def _(dve):
            dve.memset(eps[:], EPS).then_inc(eps_set, 1)
            gain_columns(dve, (1, 2, 3), consts.mod, consts.norms, consts.gains, gain_step)
            dve.wait_ge(root, after(1))
            dve.reciprocal(rstd[:], rstd[:]).then_inc(inv, 1)
            dve.wait_ge(inv, after(1))
            ov = o[:].rearrange("p c (h n) -> p (c h) n", h=HB)
            dve.tensor_tensor(ov, ov, rstd[:].unsqueeze(2).to_broadcast([P, TC * HB, P]), ALU.mult).then_inc(normed, 1)
            dve.wait_ge(loaded, after(32))
            dve.wait_ge(gated, after(1))
            for u, (hd, lo, hi) in enumerate(units):
                cols = slice(P * lo, min(P * hi, N))
                n = cols.stop - cols.start
                dve.wait_ge(turned, after(u + 1))
                dve.scalar_tensor_tensor(out=out[:, hd, cols], in0=turn[u % 2][:, 0:n], scalar=gnorm[:, hd:hd + 1],
                                         in1=gate[:, hd, cols], op0=ALU.mult, op1=ALU.mult).then_inc(done, 1)

        @block.tensor
        def _(pe):
            pe.wait_ge(normed, after(1))
            for u, (hd, lo, hi) in enumerate(units):
                if u >= 2:
                    pe.wait_ge(done, after(u - 1))
                for c in range(lo, hi):
                    last = pe.transpose(turn[u % 2][:, P * (c - lo):P * (c - lo) + P], o[:, c, P * hd:P * hd + P], ident[:])
                last.then_inc(turned, 1)


class Constants:

    def __init__(self, m):
        self.mod = m.sb("mod", [P, 2, 6, KD, 2])
        self.gains = m.sb("gains", [P, 4, KD, 2])
        self.norms = m.sb("norms", [P, 5, KD])
        self.silu_c = m.sb("silu_c", [P, KD, 2])
        self.b_ada = m.sb("b_ada", [P, 2 * 6 * KD])
        self.ident = m.sb("ident", [P, P])
        self.ones = m.sb("ones", [P, P])


def projection_phase(nc, name, w_dram, count, src, z_dram):
    with Tools(nc) as m:
        loads, products, copies, _, _ = projection(m, name, w_dram, 0, count, src, z_dram)
        block = m.block()
        block.sync(loads)
        block.tensor(products)
        block.scalar(copies)


def token_major_phase(nc, name, w_dram, blocks, src, out_dram):
    with Tools(nc) as m:
        acc = [m.ps(f"{name}_acc{a}", [P, 512]) for a in range(4)]
        weights, stores, products, copies = token_major(m, name, w_dram, blocks, src, out_dram, acc)
        block = m.block()

        @block.sync
        def _(sp):
            weights(sp)
            stores(sp)

        block.tensor(products)
        block.scalar(copies)


def choice_phase(nc, io, h, score, c):
    with Tools(nc) as m:
        steps = modulation(m, "ada1", io["w_ada"], c.silu_c, c.b_ada, c.mod)
        rest = Z0_CHUNKS - Z0_FIRST
        loads, products, copies, acc, acc_read = projection(
            m, "z0b", io["w0"], Z0_FIRST, rest, h, io["z0"], (steps, ADA_FIRST))
        weights, stores, tok_products, tok_copies = token_major(
            m, "tok0b", io["wt0"], [(0, 512), (1, 512)], h, io["zt0"], acc[0] + acc[1],
            (steps, ADA_FIRST + rest, ADA_GROUPS - ADA_FIRST - rest, rest // 2))
        choose, store = choosing(m, score, io["mask_s"])
        block = m.block()

        @block.sync
        def _(sp):
            loads(sp)
            weights(sp)
            stores(sp)
            store(sp)

        @block.tensor
        def _(pe):
            products(pe)
            for b in range(2):
                pe.wait_ge(acc_read[b], after(3 * rest // 2))
            tok_products(pe)

        @block.scalar
        def _(act):
            copies(act)
            tok_copies(act)

        block.vector(choose)


def even_mixer(nc, io, h, c, mix, x):
    projection_phase(nc, "z0a", io["w0"], Z0_FIRST, h, io["z0"])
    token_major_phase(nc, "tok0", io["wt0"], [(2, HA)], h, io["zt0"])
    with Tools(nc) as s:
        score = s.sb("score", [P, SAMPLE_AT + SAMPLE_KEYS])
        index_phase(nc, io, score)
        choice_phase(nc, io, h, score, c)
        prompt_attention_phase(nc, "pa", io, io["z0"], QA, KA, io["zt0"], 0, io["skew_a"], T, HA, None, score, c.ident,
                               mix)
    sample_attention_phase(nc, "sa", io, io["z0"], QA, KA, io["zt0"], 0, io["ka_past"], io["va_past"], PAST,
                           io["skew_s"], SKEW_S, S - 1, HA, io["mask_s"], c.ident, mix)
    with Tools(nc) as s:
        o = s.sb("hg_o", [P, TILES + 1, HB * P])
        recurrence_phase(nc, io, c.ident, o, h[:, 0:HB, :])
        recurrence_out_phase(nc, io, c, o, mix, x)


def odd_mixer(nc, io, h, c, mix):
    projection_phase(nc, "z1", io["w1"], Z1_CHUNKS, h, io["z1"])
    token_major_phase(nc, "tok1", io["wt1"], [(0, 512), (1, 512)], h, io["zt1"])
    prompt_attention_phase(nc, "pc", io, io["z1"], 0, 8, io["zt1"], 0, io["skew_c"], BAND_KEYS, HC, 4, None, c.ident, mix)
    sample_attention_phase(nc, "sc", io, io["z1"], 0, 8, io["zt1"], 0, io["kc_past"], io["vc_past"], BACK,
                           io["skew_c"], SKEW_C, P - 1, HC, None, c.ident, mix)


def build_program(nc, io):
    def dram(name, shape):
        io[name] = nc.dram_tensor(f"scratch_{name}", shape, F32, kind="Internal").ap()

    dram("skew_a", [HA, P * SKEW_A])
    dram("skew_s", [HA, S * SKEW_S])
    dram("skew_c", [HC, P * SKEW_C])
    dram("mask_s", [S, SAMPLE_KEYS])
    dram("mix0", [KD, P, N])
    dram("mix1", [KD, P, N])
    with Tools(nc) as m:
        c = Constants(m)
        x = m.sb("x", [P, KD, N])
        h = m.sb("h", [P, KD, N])
        setup_phase(nc, io, x, c)
        bias_phase(nc, io)
        norm_phase(nc, "n00", x, h, c.gains[:, 0], c.mod[:, 0, 0], c.ones)
        even_mixer(nc, io, h, c, io["mix0"], x)
        for l in range(2):
            if l == 1:
                norm_phase(nc, "n10", x, h, c.gains[:, 2], c.mod[:, 1, 0], c.ones)
                odd_mixer(nc, io, h, c, io["mix1"])
            residual_phase(nc, f"out{l}", io["w_out"][l], KD, h, x, c.mod[:, l, 2], io[f"mix{l}"])
            norm_phase(nc, f"n{l}1", x, h, c.gains[:, 2 * l + 1], c.mod[:, l, 3], c.ones)
            with Tools(nc) as f:
                a = f.sb(f"ffn{l}", [P, KF, N])
                ffn_up_phase(nc, f"up{l}", io["w_gate"][l], io["w_up"][l], h, a)
                residual_phase(nc, f"down{l}", io["w_down"][l], KF, a, x, c.mod[:, l, 5])
        norm_phase(nc, "nf", x, h, c.norms[:, 4], None, c.ones, store=io["yT"])


def blocks_of(w, k):
    return np.ascontiguousarray(w.reshape(k, P, -1, P).transpose(2, 1, 0, 3))


def wide_blocks_of(w, n):
    return w.reshape(KD, P, n, 512).transpose(2, 1, 0, 3)


def features(a):
    return np.ascontiguousarray(a.T.reshape(KD, P, -1).transpose(1, 0, 2))


def arrays_of(i):
    i = {k: np.asarray(v) for k, v in i.items()}
    w = i["w_in_even"][0]
    qa, ka, va, qi, ki, wi, qb, fb, ib, gb = np.split(w, np.cumsum([512, 512, 512, 512, 64, 8, 512, 512, 512]), axis=1)
    wt0 = np.zeros((3, P, KD, 512), w.dtype)
    wt0[:2] = wide_blocks_of(np.concatenate([va, ib], 1), 2)
    wt0[2, :, :, :HA] = wi.reshape(KD, P, HA).transpose(1, 0, 2)
    w1 = i["w_in_odd"][0]
    return {
        "xT": features(np.concatenate([i["x_prompt"][0], i["x_sample"][0]])),
        "cT": features(np.concatenate([i["c_prompt"], i["c_sample"]])),
        "w_ada": np.ascontiguousarray(i["w_ada"].reshape(2, KD, P, 12, 4, P).transpose(0, 3, 2, 4, 1, 5)
                                      .reshape(24, P, 4, KD, P)),
        "b_ada": np.ascontiguousarray(i["b_ada"].reshape(96, P).T),
        "norms": np.ascontiguousarray(np.stack([i["norm_mix"][0], i["norm_ffn"][0], i["norm_mix"][1],
                                                i["norm_ffn"][1], i["norm_final"]])
                                      .reshape(5, KD, P).transpose(2, 0, 1)),
        "w0": blocks_of(np.concatenate([qa, ka, qi, ki, ki, qb, fb, gb], 1), KD),
        "wt0": wt0,
        "w1": blocks_of(w1[:, :2048], KD),
        "wt1": np.ascontiguousarray(wide_blocks_of(w1[:, 2048:], 2)),
        "w_out": np.stack([blocks_of(i["w_out_even"][0], KD), blocks_of(i["w_out_odd"][0], KD)]),
        "w_gate": np.stack([blocks_of(v, KD) for v in i["w_ffn_gate"]]),
        "w_up": np.stack([blocks_of(v, KD) for v in i["w_ffn_up"]]),
        "w_down": np.stack([blocks_of(v, KF) for v in i["w_ffn_down"]]),
            "t5": i["t5_table"],
        "t5_onehot": t5_onehot(),
        "rel_rev": np.ascontiguousarray(i["rel_table_c"][0].T[:, ::-1]),
        "lb": np.ascontiguousarray(i["lb_logits"].reshape(2, HB, P).transpose(2, 0, 1)),
        "norm_b": np.ascontiguousarray(i["norm_b_out"][0].reshape(HB, P).T),
        "hg_masks": halving_masks(),
        "state_in": i["state_b"][0, 0],
        "ki_past": np.ascontiguousarray(np.concatenate([i["cache_a_kidx"][0, 0].T] * 2)),
        "ka_past": np.ascontiguousarray(i["cache_a_k"][0, 0].reshape(PAST, 4, P).transpose(1, 2, 0)),
        "va_past": i["cache_a_v"][0, 0].reshape(PAST, HA * DH),
        "kc_past": np.ascontiguousarray(i["cache_c_k"][0, 0].reshape(BACK, 8, P).transpose(1, 2, 0)),
        "vc_past": i["cache_c_v"][0, 0].reshape(BACK, HC * DH),
    }


def t5_onehot():
    rel = np.arange(T5_LEN) - (PAST + S - 1)
    n = np.abs(rel)
    large = 8 + (np.log(np.maximum(n, 1).astype(np.float32) / 8) / np.log(1024 / 8) * 8).astype(np.int32)
    bucket = np.where(rel > 0, 16, 0) + np.where(n < 8, n, np.minimum(large, 15))
    return (np.arange(32)[:, None] == bucket[None, :]).astype(np.float32)


def halving_masks():
    s, t = np.arange(P)[:, None], np.arange(P)[None, :]
    out = [(s >> lv + 1 == t >> lv + 1) & (s >> lv & 1 == 0) & (t >> lv & 1 == 1) for lv in range(LEVELS)]
    return np.ascontiguousarray(np.stack(out + [s == t], 1).astype(np.float32))


_OUTS = [("z0", (Z0_CHUNKS, P, N)), ("zt0", (N, 1024 + HA)), ("z1", (Z1_CHUNKS, P, N)), ("zt1", (N, 1024)),
         ("state_p", (HB, P, P)), ("state_s", (HB, P, P)), ("yT", (P, KD, N))]


def kernel(**inputs):
    import concourse.bacc as _bacc
    from concourse.bass_utils import run_bass_kernel_spmd as _run

    nc = _bacc.Bacc("TRN2", target_bir_lowering=False, num_devices=1)
    arrays, io = {}, {}
    for name, a in arrays_of(inputs).items():
        arrays[f"in_{name}_dram"] = a = np.ascontiguousarray(a)
        io[name] = nc.dram_tensor(f"in_{name}_dram", a.shape, mybir.dt.from_np(a.dtype), kind="ExternalInput").ap()
    for name, shape in _OUTS:
        io[name] = nc.dram_tensor(f"out_{name}_dram", shape, F32, kind="ExternalOutput").ap()
    build_program(nc, io)
    r = _run(nc, [arrays], core_ids=[0]).results[0]
    r = {name: r[f"out_{name}_dram"] for name, _ in _OUTS}

    def rows(z):
        return z.reshape(-1, N).T

    y = r["yT"].transpose(2, 1, 0).reshape(N, D)
    ka, kidx, kc = rows(r["z0"][KA:KA + 4]), rows(r["z0"][KI])[:, :DH], rows(r["z1"][8:16])
    va, vc = r["zt0"][:, :512], r["zt1"]

    def out(a, lo, hi, *shape):
        return np.ascontiguousarray(a[lo:hi]).reshape(shape)

    return (out(y, 0, T, 1, T, D), out(y, T, N, 1, S, D),
            out(ka, 0, T, 1, 1, T, HA, DH), out(va, 0, T, 1, 1, T, HA, DH), out(kidx, 0, T, 1, 1, T, DH),
            r["state_p"].reshape(1, 1, HB, P, P),
            out(kc, T - BACK, T, 1, 1, BACK, HC, DH), out(vc, T - BACK, T, 1, 1, BACK, HC, DH),
            out(ka, T, N, 1, 1, S, HA, DH), out(va, T, N, 1, 1, S, HA, DH), out(kidx, T, N, 1, 1, S, DH),
            r["state_s"].reshape(1, 1, HB, P, P),
            out(kc, T, N, 1, 1, S, HC, DH), out(vc, T, N, 1, 1, S, HC, DH))
```

```python
from contextlib import ExitStack

import numpy as np

import concourse.bass as bass
from concourse import mybir

F32 = mybir.dt.float32
F32R = mybir.dt.float32r
ACT = mybir.ActivationFunctionType
ALU = mybir.AluOpType
AX_X = mybir.AxisListType.X

P = 128
D = 1024
KD = D // P
T = 1024
S = 32
N = T + S
PAST = 2048
EPS = 1e-6
DH = 64
HA = 8
HC = 16
HB = 4
KTOP = 256
FF = 2816
KF = FF // P
CHUNK = 64
BACK = 8 * CHUNK
TILES = T // P
THIRD = N // 3
THIRDS = [(t * THIRD, (t + 1) * THIRD) for t in range(3)]
SPANS = [(0, THIRD, 0), (THIRD, 2 * THIRD, 0), (2 * THIRD, T, 0), (T, N, 1)]
MASKED = -1e30
OUT_OF_REACH = -3.0e38
TAKEN = -3.4e38
QA, KA, QI, KI, QB, FB, GB, Z0_CHUNKS = 0, 4, 8, 12, 13, 17, 21, 25
Z0_FIRST = 13
Z1_CHUNKS = 16
T5_LEN = PAST + S - 1 + P
BAND_KEYS = BACK + P
REL = 128
BAND_LEN = 768
SKEW_A, SKEW_C, SKEW_S = T + P - 1, BAND_KEYS + P - 1, PAST + S + S - 1


class Tools:

    def __init__(self, nc):
        self.nc, self.stack, self.sems = nc, ExitStack(), []

    def sb(self, name, shape, dt=F32):
        return self.stack.enter_context(self.nc.sbuf_tensor(name, shape, dt))

    def ps(self, name, shape, dt=F32):
        return self.stack.enter_context(self.nc.psum_tensor(name, shape, dt))

    def sem(self, name):
        self.sems.append(self.nc.alloc_semaphore(name))
        return self.sems[-1]

    def block(self):
        for sem in self.sems:
            self.nc.gpsimd.sem_inc(sem, START)
        self.nc.all_engine_barrier()
        return self.stack.enter_context(self.nc.Block())

    def __enter__(self):
        self.stack.__enter__()
        return self

    def __exit__(self, *a):
        self.stack.__exit__(*a)
        if self.sems:
            self.nc.clear_and_free_semaphores(self.sems)


class Halves:

    def __init__(self, m, name, shape):
        self.hi, self.lo = m.sb(f"{name}_hi", shape, F32R), m.sb(f"{name}_lo", shape, F32R)

    def rest(self, at):
        return self.hi[at].bitcast(F32)


def product(pe, out, blocks):
    for k, (w_hi, w_lo, hi, lo) in enumerate(blocks):
        pe.matmul(out, w_hi, hi, start=k == 0, stop=False)
        pe.matmul(out, w_hi, lo, start=False, stop=False)
        last = pe.matmul(out, w_lo, hi, start=False, stop=k == len(blocks) - 1)
    return last


def halve(pool, raw, hi, lo, step, n, done, free):
    wait_apart(pool, *free)
    pool.tensor_copy(hi, raw).then_inc(step, 1)
    wait_apart(pool, (step, n + 1))
    pool.tensor_tensor(lo, raw, hi.bitcast(F32), ALU.subtract).then_inc(done, 1)


START = 1


def after(count):
    return START + count


def wait_apart(eng, *waits):
    for _, count in waits:
        if not isinstance(count, int):
            eng.to_reg(after(count))
    eng.wait_ge(waits[0][0], after(0))
    for sem, count in waits:
        eng.wait_ge(sem, after(count))


ADA_GROUP = 4
ADA_GROUPS = 2 * 6 * KD // ADA_GROUP
ADA_FIRST = 2 * KD // ADA_GROUP


def modulation(m, name, w_dram, silu_c, b_ada, mod):
    w = [m.sb(f"{name}_w{b}", [P, ADA_GROUP, KD, P]) for b in range(2)]
    acc = [m.ps(f"{name}_acc{b}", [P, 512]) for b in range(2)]
    w_in = [m.sem(f"{name}_w_in{b}") for b in range(2)]
    acc_ready = [m.sem(f"{name}_acc{b}") for b in range(2)]
    acc_read = [m.sem(f"{name}_acc_read{b}") for b in range(2)]
    modf = mod[:].rearrange("p l j k s -> p (l j k) s")

    def load(sp, g, b, n):
        sp.wait_ge(acc_ready[b], after(n))
        sp.dma_start(w[b][:], w_dram[g]).then_inc(w_in[b], 16)

    def products(pe, b, n):
        pe.wait_ge(w_in[b], after(16 * n + 16))
        pe.wait_ge(acc_read[b], after(n))
        for c in range(ADA_GROUP):
            for k in range(KD):
                last = pe.matmul(acc[b][:, 2 * c:2 * c + 2], w[b][:, c, k, :], silu_c[:, k, :],
                                 start=k == 0, stop=k == KD - 1)
        last.then_inc(acc_ready[b], 1)

    def add(act, g, b, n):
        act.wait_ge(acc_ready[b], after(n + 1))
        for c in range(ADA_GROUP):
            at = g * ADA_GROUP + c
            last = act.activation(modf[:, bass.ds(at, 1), :], acc[b][:, 2 * c:2 * c + 2].unsqueeze(1), ACT.Identity,
                                  bias=b_ada[:, bass.ds(at, 1)])
        last.then_inc(acc_read[b], 1)

    return load, products, add, acc_read


def gain_columns(dve, which, mod, norms, gains, step):
    for n in which:
        dve.tensor_scalar(gains[:, n], mod[:, n // 2, 3 * (n % 2) + 1], 1.0, None, ALU.add).then_inc(step, 1)
    dve.wait_ge(step, after(len(which)))
    for n in which:
        dve.tensor_tensor(gains[:, n], gains[:, n], norms[:, n].unsqueeze(2).to_broadcast([P, KD, 2]), ALU.mult)


def setup_phase(nc, io, x, consts):
    c = consts
    with Tools(nc) as m:
        small_in, x_in, silu_ready = m.sem("small_in"), m.sem("x_in"), m.sem("silu_c_ready")
        ident_zero, gain_step = m.sem("ident_zero"), m.sem("gain_step")
        load, products, add, acc_read = modulation(m, "ada0", io["w_ada"], c.silu_c, c.b_ada, c.mod)
        block = m.block()

        @block.sync
        def _(sp):
            for g in range(ADA_FIRST):
                load(sp, g, g % 2, g // 2)

        @block.gpsimd
        def _(pool):
            pool.memset(c.ones[:], 1.0)
            pool.memset(c.ident[:], 0.0).then_inc(ident_zero, 1)
            pool.wait_ge(ident_zero, after(1))
            pool.affine_select(out=c.ident[:], in_=c.ident[:], compare_op=ALU.not_equal, fill=1.0,
                               base=0, pattern=[[-1, P]], channel_multiplier=1)

        @block.scalar
        def _(act):
            act.dma_start(c.silu_c[:], io["cT"]).then_inc(small_in, 16)
            act.dma_start(c.b_ada[:], io["b_ada"]).then_inc(small_in, 16)
            act.dma_start(c.norms[:], io["norms"]).then_inc(small_in, 16)
            act.dma_start(x[:], io["xT"]).then_inc(x_in, 16)
            act.wait_ge(small_in, after(48))
            act.activation(c.silu_c[:], c.silu_c[:], ACT.Silu).then_inc(silu_ready, 1)
            for g in range(ADA_FIRST):
                add(act, g, g % 2, g // 2)
            act.wait_ge(x_in, after(16))

        @block.tensor
        def _(pe):
            pe.wait_ge(silu_ready, after(1))
            for g in range(ADA_FIRST):
                products(pe, g % 2, g // 2)

        @block.vector
        def _(dve):
            for b in range(2):
                dve.wait_ge(acc_read[b], after(ADA_FIRST // 2))
            gain_columns(dve, (0,), c.mod, c.norms, c.gains, gain_step)


def norm_phase(nc, name, x, out, gain, shift, ones, store=None, halves=None):
    with Tools(nc) as m:
        if out is None:
            out = m.sb(f"{name}_out", [P, KD, N])
        sq = [m.sb(f"{name}_sq{b}", [P, THIRD]) for b in range(4)]
        rstd = m.sb(f"{name}_rstd", [P, N])
        eps = m.sb(f"{name}_eps", [P, 1])
        ssq = [m.ps(f"{name}_ssq{t}", [P, 512]) for t in range(3)]
        eps_set = m.sem(f"{name}_eps")
        sq_ready = [m.sem(f"{name}_sq{a}") for a in range(2)]
        summed = m.sem(f"{name}_summed")
        root, rstd_ready = m.sem(f"{name}_root"), m.sem(f"{name}_rstd")
        scaled, done, hi_ready = m.sem(f"{name}_scaled"), m.sem(f"{name}_stored"), m.sem(f"{name}_hi")
        block = m.block()

        def square(eng, t, k):
            n = KD * t + k
            if n >= 4:
                eng.wait_ge(summed, after(n - 3))
            lo, hi = THIRDS[t]
            if k % 2 == 0:
                eng.activation(sq[n % 4][:], x[:, k, lo:hi], ACT.Square).then_inc(sq_ready[0], 1)
            else:
                eng.tensor_tensor(sq[n % 4][:], x[:, k, lo:hi], x[:, k, lo:hi], ALU.mult).then_inc(sq_ready[1], 1)

        def rest(dve, n):
            a, b, s = SPANS[n]
            for k in range(KD):
                dve.wait_ge(hi_ready, after(KD * n + k + 1))
                dve.scalar_tensor_tensor(out=halves.lo[:, k, a:b], in0=out[:, k, a:b], scalar=shift[:, k, s:s + 1],
                                         in1=halves.rest((slice(None), k, slice(a, b))), op0=ALU.add,
                                         op1=ALU.subtract)

        @block.gpsimd
        def _(pool):
            for t in range(3):
                for k in range(1, KD, 2):
                    square(pool, t, k)

        @block.scalar
        def _(act):
            def add_shift(n):
                if shift is not None:
                    a, b, s = SPANS[n]
                    for k in range(KD):
                        act.wait_ge(scaled, after(KD * n + k + 1))
                        act.activation((halves.hi if halves else out)[:, k, a:b], out[:, k, a:b], ACT.Identity,
                                       bias=shift[:, k, s:s + 1]).then_inc(hi_ready, 1)

            act.wait_ge(eps_set, after(1))
            for t in range(4):
                if t < 3:
                    for k in range(0, KD, 2):
                        square(act, t, k)
                if t:
                    lo, hi = THIRDS[t - 1]
                    act.wait_ge(summed, after(KD * t))
                    act.activation(rstd[:, lo:hi], ssq[t - 1][:, 0:THIRD], ACT.Sqrt, bias=eps[:, 0:1],
                                   scale=1.0 / D).then_inc(root, 1)
            for n in range(len(SPANS)):
                add_shift(n)

        @block.tensor
        def _(pe):
            for t in range(3):
                for k in range(KD):
                    n = KD * t + k
                    pe.wait_ge(sq_ready[k % 2], after(n // 2 + 1))
                    pe.matmul(ssq[t][:, 0:THIRD], ones[:], sq[n % 4][:], start=k == 0, stop=k == KD - 1
                              ).then_inc(summed, 1)

        @block.vector
        def _(dve):
            dve.memset(eps[:], EPS).then_inc(eps_set, 1)
            for n, (a, b, s) in enumerate(SPANS):
                if n < 3:
                    lo, hi = THIRDS[n]
                    dve.wait_ge(root, after(n + 1))
                    dve.reciprocal(rstd[:, lo:hi], rstd[:, lo:hi]).then_inc(rstd_ready, 1)
                    dve.wait_ge(rstd_ready, after(n + 1))
                for k in range(KD):
                    dve.scalar_tensor_tensor(out=out[:, k, a:b], in0=x[:, k, a:b],
                                             scalar=gain[:, k, s:s + 1] if shift is not None else gain[:, k:k + 1],
                                             in1=rstd[:, a:b], op0=ALU.mult, op1=ALU.mult).then_inc(scaled, 1)
                if halves and n:
                    rest(dve, n - 1)
            if halves:
                rest(dve, len(SPANS) - 1)

        @block.sync
        def _(sp):
            if store is not None:
                sp.wait_ge(scaled, after(KD * len(SPANS)))
                sp.dma_start(store, out[:]).then_inc(done, 16)
                sp.wait_ge(done, after(16))


def over_chunks(eng, count, body):
    if count >= 2:
        with eng.Fori(0, count // 2) as i:
            for b in range(2):
                body(i, b)
    if count % 2:
        body(count // 2, 0)


def projection(m, name, w_dram, first, count, src, z_dram, beside=None, halved=False):
    raw = [m.sb(f"{name}_w{b}", [P, KD, P]) for b in range(2)]
    stage = [m.sb(f"{name}_stage{b}", [P, N]) for b in range(2)]
    acc = [[m.ps(f"{name}_acc{b}{t}", [P, 512]) for t in range(3)] for b in range(2)]
    w_in = [m.sem(f"{name}_w_in{b}") for b in range(2)]
    acc_ready = [m.sem(f"{name}_acc{b}") for b in range(2)]
    acc_read = [m.sem(f"{name}_acc_read{b}") for b in range(2)]
    stored = [m.sem(f"{name}_stored{b}") for b in range(2)]
    if halved:
        w = [Halves(m, f"{name}_w{b}", [P, KD, P]) for b in range(2)]
        w_hi = [m.sem(f"{name}_w_hi{b}") for b in range(2)]
        w_ready = [m.sem(f"{name}_w_ready{b}") for b in range(2)]

    def loads(sp):
        def body(i, b):
            if halved:
                sp.wait_ge(w_ready[b], after(i))
            else:
                sp.wait_ge(acc_ready[b], after(3 * i))
            sp.dma_start(raw[b][:], w_dram[first + 2 * i + b]).then_inc(w_in[b], 16)
            if beside:
                beside[0][0](sp, beside[1] + 2 * i + b, b, i)
        over_chunks(sp, count, body)

    def halving(pool):
        def body(i, b):
            halve(pool, raw[b][:], w[b].hi[:], w[b].lo[:], w_hi[b], i, w_ready[b],
                  ((w_in[b], 16 * i + 16), (acc_ready[b], 3 * i)))
        over_chunks(pool, count, body)

    def products(pe):
        def body(i, b):
            if halved:
                pe.wait_ge(w_ready[b], after(i + 1))
            else:
                pe.wait_ge(w_in[b], after(16 * i + 16))
            for t, (lo, hi) in enumerate(THIRDS):
                pe.wait_ge(acc_read[b], after(3 * i))
                out = acc[b][t][:, 0:THIRD]
                if halved:
                    last = product(pe, out, [(w[b].hi[:, k, :], w[b].lo[:, k, :], src.hi[:, k, lo:hi],
                                              src.lo[:, k, lo:hi]) for k in range(KD)])
                else:
                    for k in range(KD):
                        last = pe.matmul(out, raw[b][:, k, :], src[:, k, lo:hi], start=k == 0, stop=k == KD - 1)
                last.then_inc(acc_ready[b], 1)
            if beside:
                beside[0][1](pe, b, i)
        over_chunks(pe, count, body)

    def copies(act):
        def body(i, b):
            act.wait_ge(stored[b], after(16 * i))
            for t, (lo, hi) in enumerate(THIRDS):
                act.wait_ge(acc_ready[b], after(3 * i + t + 1))
                act.activation(stage[b][:, lo:hi], acc[b][t][:, 0:THIRD], ACT.Copy).then_inc(acc_read[b], 1)
            act.wait_ge(acc_read[b], after(3 * i + 3))
            act.dma_start(z_dram[first + 2 * i + b], stage[b][:]).then_inc(stored[b], 16)
            if beside:
                beside[0][2](act, beside[1] + 2 * i + b, b, i)
        over_chunks(act, count, body)
        act.wait_ge(stored[0], after(16 * ((count + 1) // 2)))
        if count >= 2:
            act.wait_ge(stored[1], after(16 * (count // 2)))

    return loads, products, copies, acc, acc_read, halving if halved else None


def token_major(m, name, w_dram, blocks, src, out_dram, acc, beside=None, halved=False):
    if halved:
        halves = [Halves(m, f"{name}_w{c}", [P, KD, n]) for c, n in blocks]
        w_hi = [[m.sem(f"{name}_w_hi{c}{k}") for k in range(KD)] for c, _ in blocks]
        w_ready = [[m.sem(f"{name}_w_ready{c}{k}") for k in range(KD)] for c, _ in blocks]
    w = [m.sb(f"{name}_w{c}", [P, KD, n]) for c, n in blocks]
    banks = len(acc)
    stage = [m.sb(f"{name}_stage{a}", [P, 512]) for a in range(banks)]
    w_in = [m.sem(f"{name}_w_in{c}") for c, _ in blocks]
    acc_ready, acc_read = m.sem(f"{name}_acc"), m.sem(f"{name}_acc_read")
    stored = [m.sem(f"{name}_stored{a}") for a in range(banks)]
    units = [(j, c, n, lo, min(lo + P, N)) for j, (c, n) in enumerate(blocks) for lo in range(0, N, P)]

    def group(u, step, eng):
        if beside and u % 2 and u // 2 < beside[2]:
            g = u // 2
            args = (eng, g % 2, beside[3] + g // 2) if step == 1 else (eng, beside[1] + g, g % 2, beside[3] + g // 2)
            beside[0][step](*args)

    def weights(sp):
        for j, (c, n) in enumerate(blocks):
            sp.dma_start(w[j][:], w_dram[c][:, :, 0:n]).then_inc(w_in[j], 16)

    def halving(pool):
        for j in range(len(blocks)):
            for k in range(KD):
                halve(pool, w[j][:, k, :], halves[j].hi[:, k, :], halves[j].lo[:, k, :], w_hi[j][k], 0,
                      w_ready[j][k], ((w_in[j], 16),))

    def stores(sp):
        for u, (j, c, n, lo, hi) in enumerate(units):
            group(u, 0, sp)
            sp.wait_ge(acc_read, after(u + 1))
            sp.dma_start(out_dram[lo:hi, 512 * c:512 * c + n], stage[u % banks][0:hi - lo, 0:n]
                         ).then_inc(stored[u % banks], 16)
        for a in range(banks):
            sp.wait_ge(stored[a], after(16 * ((len(units) - a + banks - 1) // banks)))

    def products(pe):
        for u, (j, c, n, lo, hi) in enumerate(units):
            if lo == 0:
                pe.wait_ge(w_in[j], after(16))
            if u >= banks:
                pe.wait_ge(acc_read, after(u - banks + 1))
            out = acc[u % banks][0:hi - lo, 0:n]
            if halved:
                if lo == 0:
                    for k in range(KD):
                        pe.wait_ge(w_ready[j][k], after(1))
                last = product(pe, out, [(src.hi[:, k, lo:hi], src.lo[:, k, lo:hi], halves[j].hi[:, k, :],
                                          halves[j].lo[:, k, :]) for k in range(KD)])
            else:
                for k in range(KD):
                    last = pe.matmul(out, src[:, k, lo:hi], w[j][:, k, :], start=k == 0, stop=k == KD - 1)
            last.then_inc(acc_ready, 1)
            group(u, 1, pe)

    def copies(act):
        for u, (j, c, n, lo, hi) in enumerate(units):
            act.wait_ge(acc_ready, after(u + 1))
            if u >= banks:
                act.wait_ge(stored[u % banks], after(16 * (u // banks)))
            act.activation(stage[u % banks][0:hi - lo, 0:n], acc[u % banks][0:hi - lo, 0:n], ACT.Copy
                           ).then_inc(acc_read, 1)
            group(u, 2, act)

    return weights, stores, products, copies, halving


def out_phase(nc, name, w_dram, src_dram, x, gate):
    with Tools(nc) as m:
        raw = [m.sb(f"{name}_w{b}", [P, KD, P]) for b in range(2)]
        w = [Halves(m, f"{name}_w{b}", [P, KD, P]) for b in range(2)]
        src = m.sb(f"{name}_src", [P, KD, N])
        halves = Halves(m, f"{name}_src", [P, KD, N])
        acc = [[m.ps(f"{name}_acc{b}{t}", [P, 512]) for t in range(3)] for b in range(2)]
        w_in = [m.sem(f"{name}_w_in{b}") for b in range(2)]
        w_hi = [m.sem(f"{name}_w_hi{b}") for b in range(2)]
        w_ready = [m.sem(f"{name}_w_ready{b}") for b in range(2)]
        src_in = [m.sem(f"{name}_src_in{k}") for k in range(KD)]
        src_hi, src_ready = m.sem(f"{name}_src_hi"), m.sem(f"{name}_src_ready")
        acc_ready = [m.sem(f"{name}_acc{b}") for b in range(2)]
        acc_read = [m.sem(f"{name}_acc_read{b}") for b in range(2)]
        block = m.block()

        @block.sync
        def _(sp):
            with sp.Fori(0, KD // 2) as i:
                for b in range(2):
                    sp.wait_ge(w_ready[b], after(i))
                    sp.dma_start(raw[b][:], w_dram[2 * i + b]).then_inc(w_in[b], 16)

        @block.gpsimd
        def _(pool):
            with pool.Fori(0, KD // 2) as i:
                for b in range(2):
                    halve(pool, raw[b][:], w[b].hi[:], w[b].lo[:], w_hi[b], i, w_ready[b],
                          ((w_in[b], 16 * i + 16), (acc_ready[b], 3 * i)))

        @block.scalar
        def _(act):
            for k in range(KD):
                act.dma_start(src[:, k, :], src_dram[k]).then_inc(src_in[k], 16)
            for k in range(KD):
                act.wait_ge(src_in[k], after(16))
                act.activation(halves.hi[:, k, :], src[:, k, :], ACT.Copy).then_inc(src_hi, 1)

        @block.tensor
        def _(pe):
            pe.wait_ge(src_ready, after(KD))
            with pe.Fori(0, KD // 2) as i:
                for b in range(2):
                    pe.wait_ge(w_ready[b], after(i + 1))
                    pe.wait_ge(acc_read[b], after(4 * i))
                    for t, (lo, hi) in enumerate(THIRDS):
                        product(pe, acc[b][t][:, 0:THIRD],
                                [(w[b].hi[:, k, :], w[b].lo[:, k, :], halves.hi[:, k, lo:hi], halves.lo[:, k, lo:hi])
                                 for k in range(KD)]).then_inc(acc_ready[b], 1)

        @block.vector
        def _(dve):
            for k in range(KD):
                dve.wait_ge(src_hi, after(k + 1))
                dve.tensor_tensor(halves.lo[:, k, :], src[:, k, :], halves.rest((slice(None), k)), ALU.subtract
                                  ).then_inc(src_ready, 1)
            with dve.Fori(0, KD // 2) as i:
                for b in range(2):
                    c = 2 * i + b
                    for n, (lo, hi, s) in enumerate(SPANS):
                        t = min(n, 2)
                        dve.wait_ge(acc_ready[b], after(3 * i + t + 1))
                        dve.scalar_tensor_tensor(out=x[:, bass.ds(c, 1), lo:hi],
                                                 in0=acc[b][t][:, lo - t * THIRD:hi - t * THIRD].unsqueeze(1),
                                                 scalar=gate[:, bass.ds(c, 1), s], in1=x[:, bass.ds(c, 1), lo:hi],
                                                 op0=ALU.mult, op1=ALU.add).then_inc(acc_read[b], 1)


FF_PARTS = [6, 6, 5, 5]
assert sum(FF_PARTS) == KF


def over_units(eng, base, count, body):
    if count >= 2:
        with eng.Fori(0, count // 2) as i:
            for c in range(2):
                body(2 * i + c, (base + c) % 2, i + (base + c) // 2)
    if count % 2:
        body(count - 1, (base + count - 1) % 2, (base + count - 1) // 2)


def ffn_phase(nc, name, wg_dram, wu_dram, wd_dram, h, x, gate):
    with Tools(nc) as m:
        raw = [m.sb(f"{name}_w{b}", [P, 2, KD, P]) for b in range(2)]
        w = [Halves(m, f"{name}_w{b}", [P, 2, KD, P]) for b in range(2)]
        inner = Halves(m, f"{name}_inner", [P, max(FF_PARTS), N])
        value = [m.sb(f"{name}_value{t}", [P, THIRD]) for t in range(3)]
        acc = [[m.ps(f"{name}_acc{t}{a}", [P, 512]) for a in range(2)] for t in range(3)]
        w_in = [m.sem(f"{name}_w_in{b}") for b in range(2)]
        w_hi = [m.sem(f"{name}_w_hi{b}") for b in range(2)]
        w_ready = [m.sem(f"{name}_w_ready{b}") for b in range(2)]
        per_third = lambda what: [m.sem(f"{name}_{what}{t}") for t in range(3)]
        acc_ready = [per_third(f"acc{b}") for b in range(2)]
        gated, multiplied = per_third("gated"), per_third("multiplied")
        added = per_third("added")
        inner_hi, inner_ready = per_third("inner_hi"), per_third("inner_ready")
        parts, base, start = [], 0, 0
        for nk in FF_PARTS:
            parts.append((base, start, nk))
            base, start = base + nk + KD // 2, start + nk
        block = m.block()

        @block.sync
        def _(sp):
            for base, start, nk in parts:
                def up(j, b, n):
                    sp.wait_ge(w_ready[b], after(n))
                    sp.dma_start(raw[b][:, 0], wg_dram[start + j]).then_inc(w_in[b], 16)
                    sp.dma_start(raw[b][:, 1], wu_dram[start + j]).then_inc(w_in[b], 16)

                def down(j, b, n):
                    sp.wait_ge(w_ready[b], after(n))
                    for a in range(2):
                        sp.dma_start(raw[b][:, a, 0:nk], wd_dram[2 * j + a][:, start:start + nk, :]
                                     ).then_inc(w_in[b], 16)

                over_units(sp, base, nk, up)
                over_units(sp, base + nk, KD // 2, down)

        @block.gpsimd
        def _(pool):
            for base, start, nk in parts:
                for first, count, k in ((base, nk, KD), (base + nk, KD // 2, nk)):
                    def weights(j, b, n):
                        halve(pool, raw[b][:, :, 0:k], w[b].hi[:, :, 0:k], w[b].lo[:, :, 0:k], w_hi[b], n,
                              w_ready[b], ((w_in[b], 32 * n + 32), (acc_ready[b][2], n)))

                    over_units(pool, first, count, weights)

        @block.tensor
        def _(pe):
            def unit(b, n, of, k):
                for t, (lo, hi) in enumerate(THIRDS):
                    yield t
                    for a in range(2):
                        last = product(pe, acc[t][a][:, 0:THIRD],
                                       [(w[b].hi[:, a, c, :], w[b].lo[:, a, c, :], of.hi[:, c, lo:hi],
                                         of.lo[:, c, lo:hi]) for c in range(k)])
                    last.then_inc(acc_ready[b][t], 1)

            for part, (base, start, nk) in enumerate(parts):
                def up(j, b, n):
                    pe.wait_ge(w_ready[b], after(n + 1))
                    for t in unit(b, n, h, KD):
                        pe.wait_ge(multiplied[t], after(start + j))
                        pe.wait_ge(added[t], after(part * KD // 2))

                def down(j, b, n):
                    pe.wait_ge(w_ready[b], after(n + 1))
                    for t in unit(b, n, inner, nk):
                        pe.wait_ge(added[t], after(part * KD // 2 + j))
                        pe.wait_ge(inner_ready[t], after(start + nk))

                over_units(pe, base, nk, up)
                over_units(pe, base + nk, KD // 2, down)

        @block.scalar
        def _(act):
            for base, start, nk in parts:
                def up(j, b, n):
                    for t, (lo, hi) in enumerate(THIRDS):
                        act.wait_ge(acc_ready[b][t], after(n + 1))
                        act.wait_ge(inner_ready[t], after(start + j))
                        act.activation(value[t][:], acc[t][0][:, 0:THIRD], ACT.Silu).then_inc(gated[t], 1)
                        act.wait_ge(multiplied[t], after(start + j + 1))
                        act.activation(inner.hi[:, bass.ds(j, 1), lo:hi], value[t][:].unsqueeze(1), ACT.Copy
                                       ).then_inc(inner_hi[t], 1)

                over_units(act, base, nk, up)

        @block.vector
        def _(dve):
            for base, start, nk in parts:
                def up(j, b, n):
                    for t, (lo, hi) in enumerate(THIRDS):
                        dve.wait_ge(gated[t], after(start + j + 1))
                        dve.tensor_tensor(value[t][:], value[t][:], acc[t][1][:, 0:THIRD], ALU.mult
                                          ).then_inc(multiplied[t], 1)
                        dve.wait_ge(multiplied[t], after(start + j + 1))
                        dve.wait_ge(inner_hi[t], after(start + j + 1))
                        dve.tensor_tensor(inner.lo[:, bass.ds(j, 1), lo:hi], value[t][:].unsqueeze(1),
                                          inner.hi[:, bass.ds(j, 1), lo:hi].bitcast(F32), ALU.subtract
                                          ).then_inc(inner_ready[t], 1)

                def down(j, b, n):
                    for span, (lo, hi, s) in enumerate(SPANS):
                        t = min(span, 2)
                        if span < 3:
                            dve.wait_ge(acc_ready[b][t], after(n + 1))
                        for a in range(2):
                            c = bass.ds(2 * j + a, 1)
                            last = dve.scalar_tensor_tensor(
                                out=x[:, c, lo:hi], in0=acc[t][a][:, lo - t * THIRD:hi - t * THIRD].unsqueeze(1),
                                scalar=gate[:, c, s], in1=x[:, c, lo:hi], op0=ALU.mult, op1=ALU.add)
                        if span != 2:
                            last.then_inc(added[t], 1)

                over_units(dve, base, nk, up)
                over_units(dve, base + nk, KD // 2, down)


def bias_phase(nc, io):
    with Tools(nc) as m:
        t5 = m.sb("t5", [32, HA])
        onehot = m.sb("onehot", [32, T5_LEN])
        fa = m.sb("t5_by_distance", [HA, T5_LEN])
        rel = m.sb("rel_reversed", [HC, 2 * REL + 1])
        fc = m.sb("rel_by_distance", [HC, BAND_LEN])
        acc = [m.ps(f"t5_acc{c}", [HA, 512]) for c in range(5)]
        loaded, acc_ready, fa_ready, fc_ready = m.sem("bias_in"), m.sem("t5_acc"), m.sem("t5_ready"), m.sem("rel_ready")
        lines_out = m.sem("bias_lines_out")
        pieces = [(lo, min(lo + 512, T5_LEN)) for lo in range(0, T5_LEN, 512)]
        block = m.block()

        @block.sync
        def _(sp):
            sp.dma_start(t5[:], io["t5"]).then_inc(loaded, 16)
            sp.dma_start(onehot[:], io["t5_onehot"]).then_inc(loaded, 16)
            sp.dma_start(rel[:], io["rel_rev"]).then_inc(loaded, 16)
            for name, line, ready, heads, rows, first, length in (
                    ("skew_a", fa, (fa_ready, len(pieces)), HA, P, T5_LEN - SKEW_A, SKEW_A),
                    ("skew_s", fa, (fa_ready, len(pieces)), HA, S, 0, SKEW_S),
                    ("skew_c", fc, (fc_ready, 2), HC, P, 0, SKEW_C)):
                sp.wait_ge(ready[0], after(ready[1]))
                sp.dma_start(io[name].rearrange("h (p n) -> h p n", p=rows),
                             line[:, first:first + length].unsqueeze(1).to_broadcast([heads, rows, length])
                             ).then_inc(lines_out, 16)
            sp.wait_ge(lines_out, after(48))

        @block.tensor
        def _(pe):
            pe.wait_ge(loaded, after(48))
            for c, (lo, hi) in enumerate(pieces):
                pe.matmul(acc[c][:, 0:hi - lo], t5[:], onehot[:, lo:hi], start=True, stop=True).then_inc(acc_ready, 1)

        @block.vector
        def _(dve):
            for c, (lo, hi) in enumerate(pieces):
                dve.wait_ge(acc_ready, after(c + 1))
                dve.tensor_scalar(fa[:, lo:hi], acc[c][:, 0:hi - lo], DH ** 0.5, None, ALU.mult).then_inc(fa_ready, 1)
            far = BAND_LEN - 1 - 2 * REL
            dve.tensor_scalar(fc[:, 0:far], rel[:, 0:1].to_broadcast([HC, far]), DH ** 0.5, None, ALU.mult).then_inc(fc_ready, 1)
            dve.tensor_scalar(fc[:, far:BAND_LEN], rel[:], DH ** 0.5, None, ALU.mult).then_inc(fc_ready, 1)


def shifted(skew, rows, length, shift, keys):
    return skew[:, shift:shift + rows * (length - 1)].rearrange(
        "h (p n) -> p h n", n=length - 1)[:, :, 0:keys]


def score_offset(i):
    return P * i * (i + 1) // 2


SAMPLE_KEYS = PAST + S
SAMPLE_AT = score_offset(TILES)


def index_phase(nc, io, score):
    with Tools(nc) as m:
        qi = m.sb("qi", [P, HA, N])
        ki = m.sb("ki", [P, N])
        ki_past = m.sb("ki_past", [P, PAST])
        w = m.sb("w_index", [P, TILES + 1, HA])
        relu = [m.sb(f"relu{b}", [P, 1024]) for b in range(2)]
        dots = [m.ps(f"dots{b}", [P, 1024]) for b in range(2)]
        loaded, w_scaled, halves_zero = m.sem("index_in"), m.sem("w_index_scaled"), m.sem("index_halves_zero")
        dots_ready, relu_ready, added = m.sem("dots"), m.sem("relu"), m.sem("score_added")
        units = [(i, P, hd, ki, 0, P * (i + 1), score_offset(i)) for i in range(2, TILES) for hd in range(HA)]
        for src, lo, n, at in ((ki_past, 0, 1024, 0), (ki_past, 1024, 1024, 1024), (ki, T, S, PAST)):
            units += [(TILES, S, hd, src, lo, n, SAMPLE_AT + at) for hd in range(HA)]
        block = m.block()

        @block.sync
        def _(sp):
            for hd in range(2):
                half = slice(DH * hd, DH * hd + DH)
                sp.dma_start(qi[half, hd::2, :], io["z0"][QI:QI + 4, half].rearrange("c p n -> p c n")).then_inc(loaded, 16)
            sp.dma_start(ki[:], io["z0"][KI]).then_inc(loaded, 16)
            sp.dma_start(ki_past[:], io["ki_past"]).then_inc(loaded, 16)
            sp.dma_start(w[:, 0:TILES, :], io["zt0"][0:T, 1024:1024 + HA].rearrange("(i p) h -> p i h", p=P)
                         ).then_inc(loaded, 16)
            sp.dma_start(w[0:S, TILES, :], io["zt0"][T:N, 1024:1024 + HA]).then_inc(loaded, 16)

        @block.gpsimd
        def _(pool):
            pool.memset(qi[0:DH, 1::2, :], 0.0).then_inc(halves_zero, 1)
            pool.memset(qi[DH:P, 0::2, :], 0.0).then_inc(halves_zero, 1)

        @block.tensor
        def _(pe):
            pe.wait_ge(loaded, after(96))
            pe.wait_ge(halves_zero, after(2))
            for u, (i, rows, hd, src, lo, n, at) in enumerate(units):
                if u >= 2:
                    pe.wait_ge(relu_ready, after(u - 1))
                for c in range(0, n, 512):
                    e = min(c + 512, n)
                    last = pe.matmul(dots[u % 2][0:rows, c:e], qi[:, hd, P * i:P * i + rows],
                                     src[:, lo + c:lo + e], start=True, stop=True)
                last.then_inc(dots_ready, 1)

        @block.scalar
        def _(act):
            for u, (i, rows, hd, src, lo, n, at) in enumerate(units):
                act.wait_ge(dots_ready, after(u + 1))
                if u >= 2:
                    act.wait_ge(added, after(u - 1))
                act.activation(relu[u % 2][0:rows, 0:n], dots[u % 2][0:rows, 0:n], ACT.Relu,
                               scale=DH ** -0.5).then_inc(relu_ready, 1)

        @block.vector
        def _(dve):
            dve.wait_ge(loaded, after(96))
            dve.tensor_scalar(w[:, 0:TILES, :], w[:, 0:TILES, :], HA ** -0.5, None, ALU.mult).then_inc(w_scaled, 1)
            dve.tensor_scalar(w[0:S, TILES, :], w[0:S, TILES, :], HA ** -0.5, None, ALU.mult).then_inc(w_scaled, 1)
            dve.wait_ge(w_scaled, after(2))
            for u, (i, rows, hd, src, lo, n, at) in enumerate(units):
                dve.wait_ge(relu_ready, after(u + 1))
                out = score[0:rows, at:at + n]
                if hd == 0:
                    dve.tensor_scalar(out, relu[u % 2][0:rows, 0:n], w[0:rows, i, 0:1], None, ALU.mult
                                      ).then_inc(added, 1)
                else:
                    dve.wait_ge(added, after(u))
                    dve.scalar_tensor_tensor(out=out, in0=relu[u % 2][0:rows, 0:n], scalar=w[0:rows, i, hd:hd + 1],
                                             in1=out, op0=ALU.mult, op1=ALU.add).then_inc(added, 1)
            dve.wait_ge(added, after(len(units)))
            for i in range(2, TILES):
                end = score_offset(i + 1)
                dve.memset(score[0:CHUNK, end - CHUNK:end], OUT_OF_REACH)


def choosing(m, score, mask_sample_dram):
    rounds = KTOP // 8
    lists = [[(P, score_offset(i), P * (i + 1)) for i in pair] for pair in ((2, 3), (4, 5), (6, 7))]
    lists.append([(S, SAMPLE_AT, SAMPLE_KEYS)])
    top = [m.sb(f"top{a}", [P, 8]) for a in range(2)]
    found = [[m.sem(f"top_found{n}{a}") for a in range(len(rows))] for n, rows in enumerate(lists)]
    taken = [[m.sem(f"top_taken{n}{a}") for a in range(len(rows))] for n, rows in enumerate(lists)]
    masked, stored = m.sem("mask_ready"), m.sem("mask_stored")

    def choose(dve):
        for n, rows in enumerate(lists):
            with dve.Fori(0, rounds) as r:
                for a, (p, at, width) in enumerate(rows):
                    wait_apart(dve, (taken[n][a], r))
                    dve.max(top[a][0:p, :], score[0:p, at:at + width]).then_inc(found[n][a], 1)
                for a, (p, at, width) in enumerate(rows):
                    wait_apart(dve, (found[n][a], r + 1))
                    dve.match_replace(score[0:p, at:at + width], top[a][0:p, :], score[0:p, at:at + width],
                                      TAKEN).then_inc(taken[n][a], 1)
            for a, (p, at, width) in enumerate(rows):
                dve.wait_ge(taken[n][a], after(rounds))
                dve.tensor_scalar(score[0:p, at:at + width], score[0:p, at:at + width], (TAKEN + OUT_OF_REACH) / 2,
                                  MASKED, ALU.is_gt, ALU.mult).then_inc(masked, 1)
        for i in range(2):
            end = score_offset(i + 1)
            dve.memset(score[:, score_offset(i):end], 0.0).then_inc(masked, 1)
            dve.wait_ge(masked, after(8 + i))
            dve.memset(score[0:CHUNK, end - CHUNK:end], MASKED)

    def store(sp):
        sp.wait_ge(masked, after(7))
        sp.dma_start(mask_sample_dram, score[0:S, SAMPLE_AT:SAMPLE_AT + SAMPLE_KEYS]).then_inc(stored, 16)
        sp.wait_ge(stored, after(16))

    return choose, store


def prompt_attention_phase(nc, name, io, z, q0, k0, vt, v0, skew, width, heads, back, mask, ident, mix):
    pairs = heads // 2
    units = 2 * TILES
    keys = [P * min(i + 1, (back or TILES) + 1) for i in range(TILES)]
    with Tools(nc) as m:
        q = [m.sb(f"{name}_q{b}", [P, 2, T]) for b in range(2)]
        k = [m.sb(f"{name}_k{b}", [P, T]) for b in range(2)]
        v = [m.sb(f"{name}_v{b}", [P, TILES, P]) for b in range(2)]
        bias = [m.sb(f"{name}_bias{b}", [P, 2, width]) for b in range(2)]
        extra = [m.sb(f"{name}_extra{a}", [P, T]) for a in range(2)] if mask is not None else None
        prob = [m.sb(f"{name}_prob{a}", [P, max(keys)]) for a in range(2)]
        probT = [m.sb(f"{name}_probT{a}", [P, max(keys)]) for a in range(2)]
        top, ntop, total, inv = (m.sb(f"{name}_{x}", [P, 2 * units]) for x in ("max", "nmax", "sum", "inv"))
        o = [m.sb(f"{name}_o{a}", [P, P]) for a in range(2)]
        oT = [m.sb(f"{name}_oT{b}", [P, T]) for b in range(2)]
        dots = [m.ps(f"{name}_dots{a}", [P, 1024]) for a in range(2)]
        turn = [m.ps(f"{name}_turn{g}", [P, 512]) for g in range(2)]
        ops = m.ps(f"{name}_out", [P, 512])
        oTps = m.ps(f"{name}_outT", [P, 512])
        loaded = [m.sem(f"{name}_in{b}") for b in range(2)]
        halves_zero = m.sem(f"{name}_halves_zero")
        band_masked = [m.sem(f"{name}_band{b}") for b in range(2)]
        dots_ready, extra_ready, logits, ntop_ready = (m.sem(f"{name}_{x}") for x in ("dots", "extra", "logits", "nmax"))
        prob_ready, inv_ready, o_ready, oT_ready = (m.sem(f"{name}_{x}") for x in ("prob", "inv", "o", "outT"))
        turned = [m.sem(f"{name}_turned{g}") for g in range(2)]
        probT_ready = [m.sem(f"{name}_probT{g}") for g in range(2)]
        out_ready = [m.sem(f"{name}_out{b}") for b in range(2)]
        oT_copied = [m.sem(f"{name}_oT{b}") for b in range(2)]
        stored = [m.sem(f"{name}_stored{b}") for b in range(2)]
        all_units = [(b, i, hd) for b in range(2) for i in range(TILES) for hd in range(2)]
        U = len(all_units)
        second = [keys[i] > 512 for _, i, _ in all_units]
        seconds = sum(second)
        block = m.block()

        @block.sync
        def _(sp):
            with sp.Fori(0, pairs // 2) as it:
                for b in range(2):
                    g = 2 * it + b
                    sp.wait_ge(out_ready[b], after(units * it))
                    for hd in range(2):
                        half = slice(DH * hd, DH * hd + DH)
                        sp.dma_start(q[b][half, hd, :], z[q0 + g][half, 0:T]).then_inc(loaded[b], 16)
                    sp.dma_start(k[b][:], z[k0 + g][:, 0:T]).then_inc(loaded[b], 16)
                    sp.dma_start(bias[b][:], shifted(skew[bass.ds(2 * g, 2)], P, width + P - 1, P - 1, width)
                                 ).then_inc(loaded[b], 16)
                    sp.dma_start(v[b][:], vt[0:T, bass.ds(v0 + P * g, P)].rearrange("(i p) n -> p i n", p=P)
                                 ).then_inc(loaded[b], 16)

        @block.gpsimd
        def _(pool):
            for b in range(2):
                for hd in range(2):
                    pool.memset(q[b][DH * (1 - hd):DH * (2 - hd), hd, :], 0.0).then_inc(halves_zero, 1)
            pool.wait_ge(halves_zero, after(4))
            with pool.Fori(0, pairs // 2) as it:
                for b in range(2):
                    if mask is None:
                        wait_apart(pool, (loaded[b], 80 * it + 80))
                        pool.memset(bias[b][0:CHUNK, :, width - CHUNK:width], MASKED).then_inc(band_masked[b], 1)
                        pool.memset(bias[b][CHUNK:P, :, 0:CHUNK], MASKED).then_inc(band_masked[b], 1)
                    else:
                        pool.wait_ge(loaded[b], after(80 * it + 80))
                        for i in range(TILES):
                            for hd in range(2):
                                u = units * b + 2 * i + hd
                                pool.wait_ge(logits, after(U * it + max(u - 1, 0)))
                                pool.tensor_tensor(extra[u % 2][:, 0:keys[i]], bias[b][:, hd, width - keys[i]:width],
                                                   mask[:, score_offset(i):score_offset(i + 1)], ALU.add
                                                   ).then_inc(extra_ready, 1)

        @block.tensor
        def _(pe):
            def scores(it, u):
                b, i, hd = all_units[u]
                if u % units == 0:
                    pe.wait_ge(loaded[b], after(80 * it + 80))
                pe.wait_ge(logits, after(U * it + max(u - 1, 0)))
                first = P * (i + 1) - keys[i]
                for c in range(0, keys[i], 512):
                    e = min(c + 512, keys[i])
                    last = pe.matmul(dots[u % 2][:, c:e], q[b][:, hd, P * i:P * i + P],
                                     k[b][:, first + c:first + e], start=True, stop=True)
                last.then_inc(dots_ready, 1)

            def turns(it, u):
                b, i, hd = all_units[u]
                pe.wait_ge(prob_ready, after(U * it + u + 1))
                for g in range(2 if second[u] else 1):
                    pe.wait_ge(probT_ready[g], after((U if g == 0 else seconds) * it + (u if g == 0 else sum(second[:u]))))
                    for c in range(512 * g, min(512 * g + 512, keys[i]), P):
                        last = pe.transpose(turn[g][:, c - 512 * g:c - 512 * g + P], prob[u % 2][:, c:c + P], ident[:])
                    last.then_inc(turned[g], 1)

            def values(it, u):
                b, i, hd = all_units[u]
                pe.wait_ge(probT_ready[0], after(U * it + u + 1))
                if second[u]:
                    pe.wait_ge(probT_ready[1], after(seconds * it + sum(second[:u + 1])))
                pe.wait_ge(o_ready, after(U * it + u))
                at = P * (i % 2) + DH * hd
                blocks = keys[i] // P
                for c in range(blocks):
                    last = pe.matmul(ops[:, at:at + DH], probT[u % 2][:, P * c:P * c + P],
                                     v[b][:, i + 1 - blocks + c, DH * hd:DH * hd + DH], start=c == 0, stop=c == blocks - 1)
                last.then_inc(out_ready[b], 1)

            def turn_out(it, u):
                b, i, hd = all_units[u]
                if hd == 0:
                    return
                pe.wait_ge(o_ready, after(U * it + u + 1))
                if i == 0:
                    pe.wait_ge(oT_copied[1 - b], after(TILES * (it + b)))
                else:
                    pe.wait_ge(oT_copied[b], after(TILES * it + i))
                pe.transpose(oTps[:, 0:P], o[i % 2][:], ident[:]).then_inc(oT_ready, 1)

            pe.wait_ge(halves_zero, after(4))
            with pe.Fori(0, pairs // 2) as it:
                for s in range(U + 3):
                    if s < U:
                        scores(it, s)
                    if 0 <= s - 1 < U:
                        turns(it, s - 1)
                    if 0 <= s - 2 < U:
                        values(it, s - 2)
                    if 0 <= s - 3 < U:
                        turn_out(it, s - 3)

        @block.vector
        def _(dve):
            def logit(it, u):
                b, i, hd = all_units[u]
                waits = [(dots_ready, U * it + u + 1)]
                if mask is not None:
                    waits.append((extra_ready, U * it + u + 1))
                    add = extra[u % 2][:, 0:keys[i]]
                else:
                    if u % units == 0:
                        waits.append((band_masked[b], 2 * it + 2))
                    add = bias[b][:, hd, width - keys[i]:width]
                wait_apart(dve, *waits, (turned[0], U * it + max(u - 1, 0)),
                           (turned[1], seconds * it + sum(second[:max(u - 1, 0)])))
                dve.tensor_tensor_reduce(prob[u % 2][:, 0:keys[i]], dots[u % 2][:, 0:keys[i]], add, 1.0, -3.0e38,
                                         ALU.add, ALU.max, top[:, u:u + 1]).then_inc(logits, 1)
                dve.wait_ge(logits, after(U * it + u + 1))
                dve.tensor_scalar(ntop[:, u:u + 1], top[:, u:u + 1], -DH ** -0.5, None, ALU.mult).then_inc(ntop_ready, 1)

            def copy(it, u):
                b, i, hd = all_units[u]
                n = min(keys[i], 512)
                dve.wait_ge(turned[0], after(U * it + u + 1))
                if u >= 2:
                    bb = all_units[u - 2][0]
                    dve.wait_ge(out_ready[bb], after(units * it + (u - 2) % units + 1))
                else:
                    dve.wait_ge(out_ready[1], after(units * it))
                dve.tensor_copy(probT[u % 2][:, 0:n], turn[0][:, 0:n]).then_inc(probT_ready[0], 1)

            def norm(it, u):
                b, i, hd = all_units[u]
                dve.wait_ge(prob_ready, after(U * it + u + 1))
                dve.reciprocal(inv[:, u:u + 1], total[:, u:u + 1]).then_inc(inv_ready, 1)
                dve.wait_ge(inv_ready, after(U * it + u + 1))
                dve.wait_ge(out_ready[b], after(units * it + u % units + 1))
                dve.wait_ge(oT_ready, after(U // 2 * it + max(u // 2 - 1, 0)))
                at = P * (i % 2) + DH * hd
                dve.tensor_scalar(o[i % 2][:, DH * hd:DH * hd + DH], ops[:, at:at + DH], inv[:, u:u + 1], None,
                                  ALU.mult).then_inc(o_ready, 1)

            with dve.Fori(0, pairs // 2) as it:
                for s in range(U + 2):
                    if s < U:
                        logit(it, s)
                    if 0 <= s - 1 < U:
                        copy(it, s - 1)
                    if 0 <= s - 2 < U:
                        norm(it, s - 2)

        @block.scalar
        def _(act):
            def exp(it, u):
                b, i, hd = all_units[u]
                act.wait_ge(ntop_ready, after(U * it + u + 1))
                act.activation(prob[u % 2][:, 0:keys[i]], prob[u % 2][:, 0:keys[i]], ACT.Exp, bias=ntop[:, u:u + 1],
                               scale=DH ** -0.5, accum_out=total[:, u:u + 1]).then_inc(prob_ready, 1)

            def copy(it, u):
                b, i, hd = all_units[u]
                if second[u]:
                    act.wait_ge(turned[1], after(seconds * it + sum(second[:u + 1])))
                    if u >= 2:
                        bb = all_units[u - 2][0]
                        act.wait_ge(out_ready[bb], after(units * it + (u - 2) % units + 1))
                    else:
                        act.wait_ge(out_ready[1], after(units * it))
                    act.activation(probT[u % 2][:, 512:keys[i]], turn[1][:, 0:keys[i] - 512], ACT.Copy
                                   ).then_inc(probT_ready[1], 1)

            def out(it, u):
                b, i, hd = all_units[u]
                if hd == 0:
                    return
                act.wait_ge(oT_ready, after(U // 2 * it + u // 2 + 1))
                if i == 0:
                    act.wait_ge(stored[b], after(16 * it))
                act.activation(oT[b][:, P * i:P * i + P], oTps[:, 0:P], ACT.Copy).then_inc(oT_copied[b], 1)
                if i == TILES - 1:
                    act.wait_ge(oT_copied[b], after(TILES * it + TILES))
                    act.dma_start(mix[2 * it + b][:, 0:T], oT[b][:]).then_inc(stored[b], 16)

            with act.Fori(0, pairs // 2) as it:
                for s in range(U + 3):
                    if s < U:
                        exp(it, s)
                    if 0 <= s - 1 < U:
                        copy(it, s - 1)
                    if 0 <= s - 3 < U:
                        out(it, s - 3)
            for b in range(2):
                act.wait_ge(stored[b], after(16 * (pairs // 2)))


def sample_attention_phase(nc, name, io, z, q0, k0, vt, v0, k_past, v_past, past, skew, length, shift, heads, mask_dram,
                           ident, mix):
    groups = heads // 4
    keys = past + S
    blocks = past // P + 1
    pieces = [(lo, min(lo + 1024, keys)) for lo in range(0, keys, 1024)]
    quads = [(lo, min(lo + 4, blocks)) for lo in range(0, blocks, 4)]
    with Tools(nc) as m:
        q = [m.sb(f"{name}_q{b}", [P, 4, S]) for b in range(2)]
        k = [m.sb(f"{name}_k{b}", [P, 2, keys]) for b in range(2)]
        v = [m.sb(f"{name}_v{b}", [P, blocks, 256]) for b in range(2)]
        bias = [m.sb(f"{name}_bias{b}", [P, keys]) for b in range(2)]
        mask = m.sb(f"{name}_mask", [P, keys]) if mask_dram is not None else None
        prob = m.sb(f"{name}_prob", [P, keys])
        probT = m.sb(f"{name}_probT", [P, blocks, P])
        top = m.sb(f"{name}_max", [P, 8])
        total, inv = m.sb(f"{name}_sum", [P, 1]), m.sb(f"{name}_inv", [P, 1])
        o, oT = m.sb(f"{name}_o", [P, DH]), m.sb(f"{name}_oT", [DH, P])
        dots = [m.ps(f"{name}_dots{a}", [P, 1024]) for a in range(2)]
        turn = [m.ps(f"{name}_turn{a}", [P, 512]) for a in range(2)]
        ops, oTps = m.ps(f"{name}_out", [P, 512]), m.ps(f"{name}_outT", [P, 512])
        loaded = [m.sem(f"{name}_in{b}") for b in range(2)]
        halves_zero = m.sem(f"{name}_halves_zero")
        mask_in, bias_ready = m.sem(f"{name}_mask_in"), m.sem(f"{name}_bias")
        dots_ready, logits, top_ready, ntop_ready, prob_ready = (
            m.sem(f"{name}_{x}") for x in ("dots", "logits", "top", "ntop", "prob"))
        turned, probT_ready, out_ready, inv_ready, o_ready, oT_ready, oT_copied, stored = (
            m.sem(f"{name}_{x}") for x in ("turned", "probT", "out", "inv", "o", "oT", "oT_copied", "stored"))
        block = m.block()

        @block.sync
        def _(sp):
            if mask is not None:
                for j in range(4):
                    sp.dma_start(mask[S * j:S * j + S, :], mask_dram).then_inc(mask_in, 16)
            for g in range(groups):
                b = g % 2
                if g >= 2:
                    sp.wait_ge(out_ready, after(g - 1))
                for hd in range(2):
                    half = slice(DH * hd, DH * hd + DH)
                    sp.dma_start(q[b][half, hd::2, :], z[q0 + 2 * g:q0 + 2 * g + 2, half, T:N]
                                 .rearrange("c p n -> p c n")).then_inc(loaded[b], 16)
                sp.dma_start(k[b][:, :, 0:past], k_past[2 * g:2 * g + 2].rearrange("c p n -> p c n")
                             ).then_inc(loaded[b], 16)
                sp.dma_start(k[b][:, :, past:keys], z[k0 + 2 * g:k0 + 2 * g + 2, :, T:N].rearrange("c p n -> p c n")
                             ).then_inc(loaded[b], 16)
                for j in range(4):
                    sp.dma_start(bias[b][S * j:S * j + S, :], shifted(skew[4 * g + j:4 * g + j + 1], S, length, shift, keys)
                                 .rearrange("p h n -> p (h n)")).then_inc(loaded[b], 16)
                sp.dma_start(v[b][:, 0:blocks - 1, :], v_past[:, 256 * g:256 * g + 256]
                             .rearrange("(i p) n -> p i n", p=P)).then_inc(loaded[b], 16)
                sp.dma_start(v[b][0:S, blocks - 1, :], vt[T:N, v0 + 256 * g:v0 + 256 * g + 256]
                             ).then_inc(loaded[b], 16)

        IN = 16 * 10

        @block.gpsimd
        def _(pool):
            for b in range(2):
                for hd in range(2):
                    pool.memset(q[b][DH * (1 - hd):DH * (2 - hd), hd::2, :], 0.0).then_inc(halves_zero, 1)
            pool.wait_ge(halves_zero, after(4))
            if mask is not None:
                pool.wait_ge(mask_in, after(64))
                for g in range(groups):
                    b = g % 2
                    pool.wait_ge(loaded[b], after(IN * (g // 2 + 1)))
                    pool.tensor_tensor(bias[b][:], bias[b][:], mask[:], ALU.add).then_inc(bias_ready, 1)

        @block.tensor
        def _(pe):
            n_dots = n_turn = 0
            pe.wait_ge(halves_zero, after(4))
            for g in range(groups):
                b = g % 2
                pe.wait_ge(loaded[b], after(IN * (g // 2 + 1)))
                for lo, hi in pieces:
                    if n_dots >= 2:
                        pe.wait_ge(logits, after(n_dots - 1))
                    for j in range(4):
                        for c in range(lo, hi, 512):
                            e = min(c + 512, hi)
                            last = pe.matmul(dots[n_dots % 2][S * j:S * j + S, c - lo:e - lo], q[b][:, j, :],
                                             k[b][:, j // 2, c:e], start=True, stop=True)
                    last.then_inc(dots_ready, 1)
                    n_dots += 1
                pe.wait_ge(prob_ready, after(g + 1))
                for lo, hi in quads:
                    if n_turn >= 2:
                        pe.wait_ge(probT_ready, after(n_turn - 1))
                    for c in range(lo, hi):
                        n = P if c < blocks - 1 else S
                        last = pe.transpose(turn[n_turn % 2][0:n, P * (c - lo):P * (c - lo) + P],
                                            prob[:, P * c:P * c + n], ident[:])
                    last.then_inc(turned, 1)
                    n_turn += 1
                pe.wait_ge(probT_ready, after(n_turn))
                if g >= 1:
                    pe.wait_ge(o_ready, after(g))
                for j in range(4):
                    for c in range(blocks):
                        n = P if c < blocks - 1 else S
                        last = pe.matmul(ops[S * j:S * j + S, 0:DH], probT[0:n, c, S * j:S * j + S],
                                         v[b][0:n, c, DH * j:DH * j + DH], start=c == 0, stop=c == blocks - 1)
                last.then_inc(out_ready, 1)
                pe.wait_ge(o_ready, after(g + 1))
                if g >= 1:
                    pe.wait_ge(oT_copied, after(g))
                pe.transpose(oTps[0:DH, 0:P], o[:], ident[:]).then_inc(oT_ready, 1)

        @block.vector
        def _(dve):
            n_dots = n_turn = 0
            for g in range(groups):
                b = g % 2
                if mask is not None:
                    dve.wait_ge(bias_ready, after(g + 1))
                else:
                    dve.wait_ge(loaded[b], after(IN * (g // 2 + 1)))
                if g >= 1:
                    dve.wait_ge(turned, after(len(quads) * g))
                for c, (lo, hi) in enumerate(pieces):
                    n_dots += 1
                    dve.wait_ge(dots_ready, after(n_dots))
                    dve.tensor_tensor_reduce(prob[:, lo:hi], dots[(n_dots - 1) % 2][:, 0:hi - lo], bias[b][:, lo:hi],
                                             1.0, -3.0e38, ALU.add, ALU.max, top[:, c:c + 1]).then_inc(logits, 1)
                dve.wait_ge(logits, after(n_dots))
                dve.tensor_reduce(top[:, 4:5], top[:, 0:len(pieces)], AX_X, ALU.max).then_inc(top_ready, 1)
                dve.wait_ge(top_ready, after(g + 1))
                dve.tensor_scalar(top[:, 5:6], top[:, 4:5], -DH ** -0.5, None, ALU.mult).then_inc(ntop_ready, 1)
                if g >= 1:
                    dve.wait_ge(out_ready, after(g))
                for lo, hi in quads:
                    n_turn += 1
                    dve.wait_ge(turned, after(n_turn))
                    full = min(hi, blocks - 1)
                    bank = turn[(n_turn - 1) % 2]
                    if full > lo:
                        last = dve.tensor_copy(probT[:, lo:full, :], bank[:, 0:P * (full - lo)]
                                               .rearrange("p (c n) -> p c n", n=P))
                    if hi == blocks:
                        last = dve.tensor_copy(probT[0:S, blocks - 1, :], bank[0:S, P * (full - lo):P * (full - lo) + P])
                    last.then_inc(probT_ready, 1)
                dve.wait_ge(prob_ready, after(g + 1))
                dve.reciprocal(inv[:], total[:]).then_inc(inv_ready, 1)
                dve.wait_ge(inv_ready, after(g + 1))
                dve.wait_ge(out_ready, after(g + 1))
                if g >= 1:
                    dve.wait_ge(oT_ready, after(g))
                dve.tensor_scalar(o[:], ops[:, 0:DH], inv[:], None, ALU.mult).then_inc(o_ready, 1)

        @block.scalar
        def _(act):
            for g in range(groups):
                act.wait_ge(ntop_ready, after(g + 1))
                if g >= 1:
                    act.wait_ge(inv_ready, after(g))
                act.activation(prob[:], prob[:], ACT.Exp, bias=top[:, 5:6], scale=DH ** -0.5,
                               accum_out=total[:]).then_inc(prob_ready, 1)
                act.wait_ge(oT_ready, after(g + 1))
                if g >= 1:
                    act.wait_ge(stored, after(64 * g))
                act.activation(oT[:], oTps[0:DH, 0:P], ACT.Copy).then_inc(oT_copied, 1)
                act.wait_ge(oT_copied, after(g + 1))
                for j in range(4):
                    act.dma_start(mix[2 * g + j // 2, DH * (j % 2):DH * (j % 2) + DH, T:N], oT[:, S * j:S * j + S]
                                  ).then_inc(stored, 16)
            act.wait_ge(stored, after(64 * groups))
LEVELS = 7


def recurrence_phase(nc, io, ident, o, raw):
    TP = (TILES + 1) * P
    W = HB * P
    ALL = LEVELS + 2
    TO_END, FROM_START = LEVELS, LEVELS + 1
    with Tools(nc) as m:
        q = m.sb("hg_q", [P, HB, TP])
        k = m.sb("hg_k", [P, HB, TP])
        g = m.sb("hg_g", [P, HB, TP])
        v = m.sb("hg_v", [P, TILES + 1, W])
        lb2 = m.sb("hg_lb2", [P, 2, HB])
        lbt = m.sb("hg_lbt", [P, 4, HB])
        masks = m.sb("hg_masks", [P, LEVELS + 1, P])
        one = m.sb("hg_one", [P, P])
        kept = m.sb("hg_kept", [P, HB, P])
        dec = m.sb("hg_decayed", [P, ALL, W])
        last_decay = m.sb("hg_last_decay", [P, HB])
        att = m.sb("hg_att", [P, LEVELS + 1, P])
        attT = [m.sb(f"hg_attT{a}", [P, P]) for a in range(2)]
        kT = m.sb("hg_kT", [P, W])
        state = m.sb("hg_state", [P, HB, P])
        pairs = [m.ps(f"hg_pairs{a}", [P, 1024]) for a in range(2)]
        kTps, dS, ops = m.ps("hg_kTps", [P, 512]), m.ps("hg_dS", [P, 512]), [m.ps(f"hg_ops{a}", [P, 512]) for a in range(2)]
        small_in, f_in, q_in, v_in = m.sem("hg_small_in"), m.sem("hg_f_in"), m.sem("hg_q_in"), m.sem("hg_v_in")
        lb_steps, f_sig, f_done, g_done, q_done, k_done = (m.sem(f"hg_{x}") for x in ("lb", "sig", "f", "g", "q", "k"))
        setup_done = m.sem("hg_setup")
        summed, diffs, decays, decayed, kept_s = (m.sem(f"hg_{x}") for x in ("summed", "diffs", "decays", "decayed", "kept"))
        pairs_ready, masked, attT_ready, kT_turned, kT_ready = (
            m.sem(f"hg_{x}") for x in ("pairs", "masked", "attT", "kT_turned", "kT_copied"))
        out_ready, out_copied, dS_ready, state_ready, state_io = (
            m.sem(f"hg_{x}") for x in ("out", "out_copied", "dS", "state", "state_io"))
        decayed_v, last_ready = m.sem("hg_decayed_levels"), m.sem("hg_last_decay_ready")
        block = m.block()

        def tiles(eng, body):
            with eng.Fori(0, TILES) as c:
                body(c, False)
            body(TILES, True)

        @block.sync
        def _(sp):
            sp.dma_start(lb2[:], io["lb"]).then_inc(small_in, 16)
            sp.dma_start(masks[:], io["hg_masks"]).then_inc(small_in, 16)
            sp.dma_start(raw, io["z0"][FB:FB + HB].rearrange("c p n -> p c n")).then_inc(f_in, 16)
            sp.dma_start(q[:, :, 0:N], io["z0"][QB:QB + HB].rearrange("c p n -> p c n")).then_inc(q_in, 16)
            sp.dma_start(v[:, 0:TILES, :], io["zt0"][0:T, 512:1024].rearrange("(i p) n -> p i n", p=P)).then_inc(v_in, 16)
            sp.wait_ge(setup_done, after(1))
            sp.dma_start(v[0:S, TILES, :], io["zt0"][T:N, 512:1024]).then_inc(v_in, 16)
            sp.wait_ge(state_ready, after(HB * TILES))
            sp.dma_start(io["state_p"].rearrange("h k v -> k h v"), state[:]).then_inc(state_io, 16)
            sp.wait_ge(state_io, after(16))
            sp.wait_ge(out_ready, after(HB * TILES))
            sp.dma_start(state[:], io["state_in"].rearrange("h k v -> k h v")).then_inc(state_io, 16)
            sp.wait_ge(state_ready, after(HB * (TILES + 1)))
            sp.dma_start(io["state_s"].rearrange("h k v -> k h v"), state[:]).then_inc(state_io, 16)
            sp.wait_ge(state_io, after(48))

        @block.scalar
        def _(act):
            act.wait_ge(q_in, after(16))
            act.activation(q[:, :, 0:N], q[:, :, 0:N], ACT.Silu).then_inc(q_done, 1)
            act.wait_ge(f_in, after(16))
            act.activation(raw, raw, ACT.Sigmoid).then_inc(f_sig, 1)
            act.wait_ge(lb_steps, after(2))
            act.activation(lbt[:, 1:3, :], lb2[:], ACT.Exp).then_inc(lb_steps, 1)
            act.wait_ge(f_done, after(HB))
            act.activation(g[:, :, 0:N], raw, ACT.Ln).then_inc(g_done, 1)

            def body(c, sample):
                act.wait_ge(diffs, after(c + 1))
                act.activation(dec[:], dec[:], ACT.Exp).then_inc(decays, 1)
                act.wait_ge(kT_turned, after(c + 1))
                act.wait_ge(dS_ready, after(HB * c))
                act.activation(kT[:], kTps[:], ACT.Copy).then_inc(kT_ready, 1)
                for hd in range(HB):
                    act.wait_ge(out_ready, after(HB * c + hd + 1))
                    act.activation(o[:, bass.ds(c, 1), P * hd:P * hd + P], ops[hd % 2][:, 0:P].unsqueeze(1), ACT.Copy
                                   ).then_inc(out_copied, 1)
            tiles(act, body)

        @block.gpsimd
        def _(pool):
            pool.memset(one[:], 1.0)
            pool.memset(v[:, TILES, :], 0.0)
            pool.memset(q[:, :, N:TP], 0.0)
            pool.memset(k[:, :, N:TP], 0.0)
            pool.memset(g[:, :, N:TP], 0.0)
            pool.memset(state[:], 0.0).then_inc(setup_done, 1)

            def body(c, sample):
                qv, kv = q[:, :, bass.ds(c * P, P)], k[:, :, bass.ds(c * P, P)]
                pool.wait_ge(decays, after(c + 1))
                pool.wait_ge(out_ready, after(HB * c))
                pool.tensor_copy(kept[:], kv).then_inc(kept_s, 1)
                pool.tensor_tensor(dec[:, TO_END, :].rearrange("p (h n) -> p h n", h=HB),
                                   dec[:, TO_END, :].rearrange("p (h n) -> p h n", h=HB), kv, ALU.mult).then_inc(decayed, 1)
                pool.wait_ge(last_ready, after(c + 1))
                pool.tensor_tensor(dec[:, FROM_START, :].rearrange("p (h n) -> p h n", h=HB),
                                   dec[:, FROM_START, :].rearrange("p (h n) -> p h n", h=HB), qv, ALU.mult).then_inc(decayed, 1)
            pool.wait_ge(k_done, after(HB))
            pool.wait_ge(q_done, after(1))
            tiles(pool, body)

        def halves(view, level, side):
            return view.rearrange("p (b s m) -> p b s m", s=2, m=1 << level)[:, :, side, :]

        @block.vector
        def _(dve):
            dve.wait_ge(small_in, after(32))
            dve.tensor_tensor(lbt[:, 0, :], lb2[:, 0, :], lb2[:, 1, :], ALU.max).then_inc(lb_steps, 1)
            dve.wait_ge(lb_steps, after(1))
            dve.tensor_tensor(lb2[:], lb2[:], lbt[:, 0, :].unsqueeze(1).to_broadcast([P, 2, HB]), ALU.subtract
                              ).then_inc(lb_steps, 1)
            dve.wait_ge(lb_steps, after(3))
            dve.tensor_tensor(lbt[:, 3, :], lbt[:, 1, :], lbt[:, 2, :], ALU.add).then_inc(lb_steps, 1)
            dve.wait_ge(lb_steps, after(4))
            dve.reciprocal(lbt[:, 0, :], lbt[:, 3, :]).then_inc(lb_steps, 1)
            dve.wait_ge(lb_steps, after(5))
            dve.tensor_tensor(lbt[:, 1, :], lbt[:, 1, :], lbt[:, 0, :], ALU.mult).then_inc(lb_steps, 1)
            dve.wait_ge(lb_steps, after(6))
            dve.tensor_scalar(lbt[:, 2, :], lbt[:, 1, :], -1.0, 1.0, ALU.mult, ALU.add).then_inc(lb_steps, 1)
            dve.wait_ge(lb_steps, after(7))
            dve.wait_ge(f_sig, after(1))
            for hd in range(HB):
                dve.tensor_scalar(raw[:, hd, :], raw[:, hd, :], lbt[:, 2, hd:hd + 1], lbt[:, 1, hd:hd + 1],
                                  ALU.mult, ALU.add).then_inc(f_done, 1)
            dve.wait_ge(f_done, after(HB))
            for hd in range(HB):
                dve.tensor_scalar(k[:, hd, 0:N], raw[:, hd, :], -1.0, 1.0, ALU.mult, ALU.add).then_inc(k_done, 1)
            dve.wait_ge(setup_done, after(1))
            dve.wait_ge(g_done, after(1))
            dve.wait_ge(k_done, after(HB))
            dve.wait_ge(q_done, after(1))

            def body(c, sample):
                start = dec[:, FROM_START, :]
                dve.wait_ge(out_ready, after(HB * c))
                dve.wait_ge(state_ready, after(HB * c))
                for hd in range(HB):
                    dve.tensor_tensor_scan(dec[:, FROM_START, P * hd:P * hd + P], one[:],
                                           g[:, hd, bass.ds(c * P, P)], 0.0, ALU.mult, ALU.add).then_inc(summed, 1)
                dve.wait_ge(summed, after(HB * (c + 1)))
                for lv in range(LEVELS):
                    half = 1 << lv
                    first, second = halves(start, lv, 0), halves(start, lv, 1)
                    mid = first[:, :, half - 1:half].to_broadcast([P, W // (2 * half), half])
                    dve.tensor_tensor(halves(dec[:, lv, :], lv, 1), second, mid, ALU.subtract)
                    dve.tensor_tensor(halves(dec[:, lv, :], lv, 0), mid, first, ALU.subtract)
                byhead = start.rearrange("p (h n) -> p h n", h=HB)
                end = byhead[:, :, P - 1:P].to_broadcast([P, HB, P])
                dve.tensor_tensor(dec[:, TO_END, :].rearrange("p (h n) -> p h n", h=HB), end, byhead, ALU.subtract
                                  ).then_inc(diffs, 1)
                dve.wait_ge(decays, after(c + 1))
                dve.tensor_copy(last_decay[:].unsqueeze(2), byhead[:, :, P - 1:P]).then_inc(last_ready, 1)
                for lv in range(LEVELS):
                    for side, src in ((0, k), (1, q)):
                        sv = src[:, :, bass.ds(c * P, P)]
                        d4 = dec[:, lv, :].rearrange("p (h b s m) -> p h b s m", h=HB, s=2, m=1 << lv)[:, :, :, side, :]
                        s4 = sv.rearrange("p h (b s m) -> p h b s m", s=2, m=1 << lv)[:, :, :, side, :]
                        last = dve.tensor_tensor(d4, d4, s4, ALU.mult)
                last.then_inc(decayed_v, 1)
                for hd in range(HB):
                    n = HB * c + hd
                    dve.wait_ge(pairs_ready, after(n + 1))
                    dve.wait_ge(attT_ready, after(n))
                    dve.tensor_tensor(att[:], pairs[hd % 2][:].rearrange("p (l n) -> p l n", l=LEVELS + 1), masks[:],
                                      ALU.mult).then_inc(masked, 1)
                    dve.wait_ge(masked, after(n + 1))
                    if hd < 2:
                        dve.wait_ge(out_ready, after(HB * c))
                    else:
                        dve.wait_ge(out_ready, after(HB * c + hd - 1))
                    dve.tensor_reduce(attT[hd % 2][:], att[:].rearrange("p l n -> p n l"), AX_X, ALU.add
                                      ).then_inc(attT_ready, 1)
                    dve.wait_ge(dS_ready, after(n + 1))
                    dve.wait_ge(out_ready, after(n + 1))
                    dve.scalar_tensor_tensor(out=state[:, hd, :], in0=state[:, hd, :], scalar=last_decay[:, hd:hd + 1],
                                             in1=dS[:, P * hd:P * hd + P], op0=ALU.mult, op1=ALU.add).then_inc(state_ready, 1)
            tiles(dve, body)

        @block.tensor
        def _(pe):
            pe.wait_ge(v_in, after(32))
            pe.wait_ge(small_in, after(32))

            def body(c, sample):
                pe.wait_ge(decayed_v, after(c + 1))
                pe.wait_ge(decayed, after(2 * c + 2))
                pe.wait_ge(kept_s, after(c + 1))
                pe.wait_ge(kT_ready, after(c))
                for hd in range(HB):
                    h = slice(P * hd, P * hd + P)
                    last = pe.transpose(kTps[:, h], dec[:, TO_END, h], ident[:])
                last.then_inc(kT_turned, 1)

                def products(hd):
                    n = HB * c + hd
                    h = slice(P * hd, P * hd + P)
                    pe.wait_ge(masked, after(HB * c + max(hd - 1, 0)))
                    for lv in range(LEVELS):
                        pe.matmul(pairs[hd % 2][:, P * lv:P * lv + P], dec[:, lv, h], dec[:, lv, h], start=True, stop=True)
                    pe.matmul(pairs[hd % 2][:, P * LEVELS:], kept[:, hd, :], q[:, hd, bass.ds(c * P, P)],
                              start=True, stop=True).then_inc(pairs_ready, 1)

                products(0)
                for hd in range(HB):
                    if hd + 1 < HB:
                        products(hd + 1)
                    n = HB * c + hd
                    h = slice(P * hd, P * hd + P)
                    pe.wait_ge(kT_ready, after(c + 1))
                    pe.wait_ge(state_ready, after(n))
                    vv = v[:, bass.ds(c, 1), h].rearrange("p c n -> p (c n)")
                    pe.matmul(dS[:, h], kT[:, h], vv, start=True, stop=True).then_inc(dS_ready, 1)
                    pe.wait_ge(attT_ready, after(n + 1))
                    pe.wait_ge(out_copied, after(HB * c + max(hd - 1, 0)))
                    if sample and hd == 0:
                        pe.wait_ge(state_io, after(32))
                    pe.matmul(ops[hd % 2][:, 0:P], attT[hd % 2][:], vv, start=True, stop=False)
                    pe.matmul(ops[hd % 2][:, 0:P], dec[:, FROM_START, h], state[:, hd, :], start=False, stop=True
                              ).then_inc(out_ready, 1)
            tiles(pe, body)


def recurrence_out_phase(nc, io, consts, o, mix, x):
    ident = consts.ident
    TC = TILES + 1
    with Tools(nc) as m:
        gate = m.sb("ho_gate", [P, HB, N])
        gnorm = m.sb("ho_gnorm", [P, HB])
        squares = m.sb("ho_squares", [P, P])
        rstd = m.sb("ho_rstd", [P, TC * HB])
        eps = m.sb("ho_eps", [P, 1])
        out = m.sb("ho_out", [P, HB, N])
        turn = [m.ps(f"ho_turn{a}", [P, 512]) for a in range(2)]
        loaded, gated, eps_set = m.sem("ho_in"), m.sem("ho_gated"), m.sem("ho_eps_set")
        summed, root, inv, normed = (m.sem(f"ho_{x}") for x in ("summed", "root", "inv", "normed"))
        turned, done, stored, x_in, gain_step = (m.sem(f"ho_{x}") for x in ("turned", "done", "stored", "x_in", "gain"))
        units = [(hd, lo, min(lo + 4, TC)) for hd in range(HB) for lo in range(0, TC, 4)]
        block = m.block()

        @block.sync
        def _(sp):
            sp.dma_start(gate[:], io["z0"][GB:GB + HB].rearrange("c p n -> p c n")).then_inc(loaded, 16)
            sp.dma_start(gnorm[:], io["norm_b"]).then_inc(loaded, 16)
            sp.dma_start(x[:], io["xT"]).then_inc(x_in, 16)
            for hd in range(HB):
                sp.wait_ge(done, after(3 * (hd + 1)))
                sp.dma_start(mix[HB + hd], out[:, hd, :]).then_inc(stored, 16)
            sp.wait_ge(stored, after(16 * HB))
            sp.wait_ge(x_in, after(16))

        @block.scalar
        def _(act):
            act.wait_ge(loaded, after(32))
            act.activation(gate[:], gate[:], ACT.Silu).then_inc(gated, 1)
            for n in range(TC * HB):
                if n:
                    act.wait_ge(summed, after(n))
                act.activation(squares[:], o[:, n // HB, P * (n % HB):P * (n % HB) + P], ACT.Square,
                               accum_out=rstd[:, n:n + 1]).then_inc(summed, 1)
            act.wait_ge(summed, after(TC * HB))
            act.wait_ge(eps_set, after(1))
            act.activation(rstd[:], rstd[:], ACT.Sqrt, bias=eps[:, 0:1], scale=1.0 / P).then_inc(root, 1)

        @block.vector
        def _(dve):
            dve.memset(eps[:], EPS).then_inc(eps_set, 1)
            gain_columns(dve, (1, 2, 3), consts.mod, consts.norms, consts.gains, gain_step)
            dve.wait_ge(root, after(1))
            dve.reciprocal(rstd[:], rstd[:]).then_inc(inv, 1)
            dve.wait_ge(inv, after(1))
            ov = o[:].rearrange("p c (h n) -> p (c h) n", h=HB)
            dve.tensor_tensor(ov, ov, rstd[:].unsqueeze(2).to_broadcast([P, TC * HB, P]), ALU.mult).then_inc(normed, 1)
            dve.wait_ge(loaded, after(32))
            dve.wait_ge(gated, after(1))
            for u, (hd, lo, hi) in enumerate(units):
                cols = slice(P * lo, min(P * hi, N))
                n = cols.stop - cols.start
                dve.wait_ge(turned, after(u + 1))
                dve.scalar_tensor_tensor(out=out[:, hd, cols], in0=turn[u % 2][:, 0:n], scalar=gnorm[:, hd:hd + 1],
                                         in1=gate[:, hd, cols], op0=ALU.mult, op1=ALU.mult).then_inc(done, 1)

        @block.tensor
        def _(pe):
            pe.wait_ge(normed, after(1))
            for u, (hd, lo, hi) in enumerate(units):
                if u >= 2:
                    pe.wait_ge(done, after(u - 1))
                for c in range(lo, hi):
                    last = pe.transpose(turn[u % 2][:, P * (c - lo):P * (c - lo) + P], o[:, c, P * hd:P * hd + P], ident[:])
                last.then_inc(turned, 1)


class Constants:

    def __init__(self, m):
        self.mod = m.sb("mod", [P, 2, 6, KD, 2])
        self.gains = m.sb("gains", [P, 4, KD, 2])
        self.norms = m.sb("norms", [P, 5, KD])
        self.silu_c = m.sb("silu_c", [P, KD, 2])
        self.b_ada = m.sb("b_ada", [P, 2 * 6 * KD])
        self.ident = m.sb("ident", [P, P])
        self.ones = m.sb("ones", [P, P])


def projection_phase(nc, name, w_dram, count, src, z_dram):
    with Tools(nc) as m:
        loads, products, copies, _, _, halving = projection(m, name, w_dram, 0, count, src, z_dram,
                                                            halved=isinstance(src, Halves))
        block = m.block()
        if halving:
            block.gpsimd(halving)
        block.sync(loads)
        block.tensor(products)
        block.scalar(copies)


def token_major_phase(nc, name, w_dram, blocks, src, out_dram):
    with Tools(nc) as m:
        acc = [m.ps(f"{name}_acc{a}", [P, 512]) for a in range(4)]
        weights, stores, products, copies, halving = token_major(m, name, w_dram, blocks, src, out_dram, acc,
                                                                 halved=isinstance(src, Halves))
        block = m.block()
        if isinstance(src, Halves):
            block.gpsimd(halving)

        @block.sync
        def _(sp):
            weights(sp)
            stores(sp)

        block.tensor(products)
        block.scalar(copies)


def choice_phase(nc, io, h, score, c):
    with Tools(nc) as m:
        steps = modulation(m, "ada1", io["w_ada"], c.silu_c, c.b_ada, c.mod)
        rest = Z0_CHUNKS - Z0_FIRST
        loads, products, copies, acc, acc_read, _ = projection(
            m, "z0b", io["w0"], Z0_FIRST, rest, h, io["z0"], (steps, ADA_FIRST))
        weights, stores, tok_products, tok_copies, _ = token_major(
            m, "tok0b", io["wt0"], [(0, 512), (1, 512)], h, io["zt0"], acc[0] + acc[1],
            (steps, ADA_FIRST + rest, ADA_GROUPS - ADA_FIRST - rest, rest // 2))
        choose, store = choosing(m, score, io["mask_s"])
        block = m.block()

        @block.sync
        def _(sp):
            loads(sp)
            weights(sp)
            stores(sp)
            store(sp)

        @block.tensor
        def _(pe):
            products(pe)
            for b in range(2):
                pe.wait_ge(acc_read[b], after(3 * rest // 2))
            tok_products(pe)

        @block.scalar
        def _(act):
            copies(act)
            tok_copies(act)

        block.vector(choose)


def even_mixer(nc, io, h, c, mix, x):
    projection_phase(nc, "z0a", io["w0"], Z0_FIRST, h, io["z0"])
    token_major_phase(nc, "tok0", io["wt0"], [(2, HA)], h, io["zt0"])
    with Tools(nc) as s:
        score = s.sb("score", [P, SAMPLE_AT + SAMPLE_KEYS])
        index_phase(nc, io, score)
        choice_phase(nc, io, h, score, c)
        prompt_attention_phase(nc, "pa", io, io["z0"], QA, KA, io["zt0"], 0, io["skew_a"], T, HA, None, score, c.ident,
                               mix)
    sample_attention_phase(nc, "sa", io, io["z0"], QA, KA, io["zt0"], 0, io["ka_past"], io["va_past"], PAST,
                           io["skew_s"], SKEW_S, S - 1, HA, io["mask_s"], c.ident, mix)
    with Tools(nc) as s:
        o = s.sb("hg_o", [P, TILES + 1, HB * P])
        recurrence_phase(nc, io, c.ident, o, h[:, 0:HB, :])
        recurrence_out_phase(nc, io, c, o, mix, x)


def odd_mixer(nc, io, x, c, mix):
    with Tools(nc) as s:
        h = Halves(s, "h10", [P, KD, N])
        norm_phase(nc, "n10", x, None, c.gains[:, 2], c.mod[:, 1, 0], c.ones, halves=h)
        projection_phase(nc, "z1", io["w1"], Z1_CHUNKS, h, io["z1"])
        token_major_phase(nc, "tok1", io["wt1"], [(0, 512), (1, 512)], h, io["zt1"])
    prompt_attention_phase(nc, "pc", io, io["z1"], 0, 8, io["zt1"], 0, io["skew_c"], BAND_KEYS, HC, 4, None, c.ident, mix)
    sample_attention_phase(nc, "sc", io, io["z1"], 0, 8, io["zt1"], 0, io["kc_past"], io["vc_past"], BACK,
                           io["skew_c"], SKEW_C, P - 1, HC, None, c.ident, mix)


def build_program(nc, io):
    def dram(name, shape):
        io[name] = nc.dram_tensor(f"scratch_{name}", shape, F32, kind="Internal").ap()

    dram("skew_a", [HA, P * SKEW_A])
    dram("skew_s", [HA, S * SKEW_S])
    dram("skew_c", [HC, P * SKEW_C])
    dram("mask_s", [S, SAMPLE_KEYS])
    dram("mix0", [KD, P, N])
    dram("mix1", [KD, P, N])
    with Tools(nc) as m:
        c = Constants(m)
        x = m.sb("x", [P, KD, N])
        setup_phase(nc, io, x, c)
        bias_phase(nc, io)
        with Tools(nc) as s:
            h = s.sb("h00", [P, KD, N])
            norm_phase(nc, "n00", x, h, c.gains[:, 0], c.mod[:, 0, 0], c.ones)
            even_mixer(nc, io, h, c, io["mix0"], x)
        for l in range(2):
            if l == 1:
                odd_mixer(nc, io, x, c, io["mix1"])
            out_phase(nc, f"out{l}", io["w_out"][l], io[f"mix{l}"], x, c.mod[:, l, 2])
            with Tools(nc) as f:
                h = Halves(f, f"h{l}1", [P, KD, N])
                norm_phase(nc, f"n{l}1", x, None, c.gains[:, 2 * l + 1], c.mod[:, l, 3], c.ones, halves=h)
                ffn_phase(nc, f"ffn{l}", io["w_gate"][l], io["w_up"][l], io["w_down"][l], h, x, c.mod[:, l, 5])
        norm_phase(nc, "nf", x, None, c.norms[:, 4], None, c.ones, store=io["yT"])


def blocks_of(w, k):
    return np.ascontiguousarray(w.reshape(k, P, -1, P).transpose(2, 1, 0, 3))


def wide_blocks_of(w, n):
    return w.reshape(KD, P, n, 512).transpose(2, 1, 0, 3)


def features(a):
    return np.ascontiguousarray(a.T.reshape(KD, P, -1).transpose(1, 0, 2))


def arrays_of(i):
    i = {k: np.asarray(v) for k, v in i.items()}
    w = i["w_in_even"][0]
    qa, ka, va, qi, ki, wi, qb, fb, ib, gb = np.split(w, np.cumsum([512, 512, 512, 512, 64, 8, 512, 512, 512]), axis=1)
    wt0 = np.zeros((3, P, KD, 512), w.dtype)
    wt0[:2] = wide_blocks_of(np.concatenate([va, ib], 1), 2)
    wt0[2, :, :, :HA] = wi.reshape(KD, P, HA).transpose(1, 0, 2)
    w1 = i["w_in_odd"][0]
    return {
        "xT": features(np.concatenate([i["x_prompt"][0], i["x_sample"][0]])),
        "cT": features(np.concatenate([i["c_prompt"], i["c_sample"]])),
        "w_ada": np.ascontiguousarray(i["w_ada"].reshape(2, KD, P, 12, 4, P).transpose(0, 3, 2, 4, 1, 5)
                                      .reshape(24, P, 4, KD, P)),
        "b_ada": np.ascontiguousarray(i["b_ada"].reshape(96, P).T),
        "norms": np.ascontiguousarray(np.stack([i["norm_mix"][0], i["norm_ffn"][0], i["norm_mix"][1],
                                                i["norm_ffn"][1], i["norm_final"]])
                                      .reshape(5, KD, P).transpose(2, 0, 1)),
        "w0": blocks_of(np.concatenate([qa, ka, qi, ki, ki, qb, fb, gb], 1), KD),
        "wt0": wt0,
        "w1": blocks_of(w1[:, :2048], KD),
        "wt1": np.ascontiguousarray(wide_blocks_of(w1[:, 2048:], 2)),
        "w_out": np.stack([blocks_of(i["w_out_even"][0], KD), blocks_of(i["w_out_odd"][0], KD)]),
        "w_gate": np.stack([blocks_of(v, KD) for v in i["w_ffn_gate"]]),
        "w_up": np.stack([blocks_of(v, KD) for v in i["w_ffn_up"]]),
        "w_down": np.stack([blocks_of(v, KF) for v in i["w_ffn_down"]]),
            "t5": i["t5_table"],
        "t5_onehot": t5_onehot(),
        "rel_rev": np.ascontiguousarray(i["rel_table_c"][0].T[:, ::-1]),
        "lb": np.ascontiguousarray(i["lb_logits"].reshape(2, HB, P).transpose(2, 0, 1)),
        "norm_b": np.ascontiguousarray(i["norm_b_out"][0].reshape(HB, P).T),
        "hg_masks": halving_masks(),
        "state_in": i["state_b"][0, 0],
        "ki_past": np.ascontiguousarray(np.concatenate([i["cache_a_kidx"][0, 0].T] * 2)),
        "ka_past": np.ascontiguousarray(i["cache_a_k"][0, 0].reshape(PAST, 4, P).transpose(1, 2, 0)),
        "va_past": i["cache_a_v"][0, 0].reshape(PAST, HA * DH),
        "kc_past": np.ascontiguousarray(i["cache_c_k"][0, 0].reshape(BACK, 8, P).transpose(1, 2, 0)),
        "vc_past": i["cache_c_v"][0, 0].reshape(BACK, HC * DH),
    }


def t5_onehot():
    rel = np.arange(T5_LEN) - (PAST + S - 1)
    n = np.abs(rel)
    large = 8 + (np.log(np.maximum(n, 1).astype(np.float32) / 8) / np.log(1024 / 8) * 8).astype(np.int32)
    bucket = np.where(rel > 0, 16, 0) + np.where(n < 8, n, np.minimum(large, 15))
    return (np.arange(32)[:, None] == bucket[None, :]).astype(np.float32)


def halving_masks():
    s, t = np.arange(P)[:, None], np.arange(P)[None, :]
    out = [(s >> lv + 1 == t >> lv + 1) & (s >> lv & 1 == 0) & (t >> lv & 1 == 1) for lv in range(LEVELS)]
    return np.ascontiguousarray(np.stack(out + [s == t], 1).astype(np.float32))


_OUTS = [("z0", (Z0_CHUNKS, P, N)), ("zt0", (N, 1024 + HA)), ("z1", (Z1_CHUNKS, P, N)), ("zt1", (N, 1024)),
         ("state_p", (HB, P, P)), ("state_s", (HB, P, P)), ("yT", (P, KD, N))]


def kernel(**inputs):
    import concourse.bacc as _bacc
    from concourse.bass_utils import run_bass_kernel_spmd as _run

    nc = _bacc.Bacc("TRN2", target_bir_lowering=False, num_devices=1)
    arrays, io = {}, {}
    for name, a in arrays_of(inputs).items():
        arrays[f"in_{name}_dram"] = a = np.ascontiguousarray(a)
        io[name] = nc.dram_tensor(f"in_{name}_dram", a.shape, mybir.dt.from_np(a.dtype), kind="ExternalInput").ap()
    for name, shape in _OUTS:
        io[name] = nc.dram_tensor(f"out_{name}_dram", shape, F32, kind="ExternalOutput").ap()
    build_program(nc, io)
    r = _run(nc, [arrays], core_ids=[0]).results[0]
    r = {name: r[f"out_{name}_dram"] for name, _ in _OUTS}

    def rows(z):
        return z.reshape(-1, N).T

    y = r["yT"].transpose(2, 1, 0).reshape(N, D)
    ka, kidx, kc = rows(r["z0"][KA:KA + 4]), rows(r["z0"][KI])[:, :DH], rows(r["z1"][8:16])
    va, vc = r["zt0"][:, :512], r["zt1"]

    def out(a, lo, hi, *shape):
        return np.ascontiguousarray(a[lo:hi]).reshape(shape)

    return (out(y, 0, T, 1, T, D), out(y, T, N, 1, S, D),
            out(ka, 0, T, 1, 1, T, HA, DH), out(va, 0, T, 1, 1, T, HA, DH), out(kidx, 0, T, 1, 1, T, DH),
            r["state_p"].reshape(1, 1, HB, P, P),
            out(kc, T - BACK, T, 1, 1, BACK, HC, DH), out(vc, T - BACK, T, 1, 1, BACK, HC, DH),
            out(ka, T, N, 1, 1, S, HA, DH), out(va, T, N, 1, 1, S, HA, DH), out(kidx, T, N, 1, 1, S, DH),
            r["state_s"].reshape(1, 1, HB, P, P),
            out(kc, T, N, 1, 1, S, HC, DH), out(vc, T, N, 1, 1, S, HC, DH))
```
